# Optimizing a Trainium2 kernel written in Bass

```python
import jax
import jax.numpy as jnp
from jax import lax
import numpy as np

D_MODEL = 1024
BATCH = 1
SEQ = 512
DEPTH = 2

CTX_LEN = 256
GRID_W = 64
CHUNK = 64
CONV_W = 3
EPS = 1e-6
M_INIT = -1e30
N_MOD = 6
N_EVEN = (DEPTH + 1) // 2
N_ODD = DEPTH // 2

GLA_HEADS = 4
GLA_DK = D_MODEL // (2 * GLA_HEADS)
GLA_DV = D_MODEL // GLA_HEADS
GLA_QK = GLA_HEADS * GLA_DK
GLA_V = GLA_HEADS * GLA_DV
GLA_GATE_RANK = 16
GLA_GATE_TAU = 16.0

SSD_HEADDIM = 64
SSD_HEADS = D_MODEL // SSD_HEADDIM
SSD_STATE = 128
SSD_GROUPS = 2
SSD_INNER = SSD_HEADS * SSD_HEADDIM
SSD_BC = SSD_GROUPS * SSD_STATE
SSD_XBC = SSD_INNER + 2 * SSD_BC

A_SIZES = (GLA_QK, GLA_QK, GLA_V, GLA_V, 2 * GLA_GATE_RANK, SSD_INNER, SSD_XBC, 2 * SSD_HEADS)
A_SPLITS = [sum(A_SIZES[:i + 1]) for i in range(len(A_SIZES) - 1)]
A_IN = sum(A_SIZES)
A_MIX = GLA_V + SSD_INNER

MLSTM_INNER = 2 * D_MODEL
MLSTM_HEADS = 4
MLSTM_DH = MLSTM_INNER // MLSTM_HEADS
QKV_BLOCK = 4

D_FF = -(-(8 * D_MODEL) // (3 * 256)) * 256

kernel_name = 'hybrid_gla_ssd_mlstm_prefix_trunk'

def rmsnorm(x, w):
    xf = x.astype(jnp.float32)
    xf = xf * lax.rsqrt(jnp.mean(xf * xf, axis=-1, keepdims=True) + EPS)
    return (xf * w.astype(jnp.float32)).astype(x.dtype)

def layernorm_nobias(x, w):
    xf = x.astype(jnp.float32)
    mu = jnp.mean(xf, axis=-1, keepdims=True)
    var = jnp.mean(jnp.square(xf - mu), axis=-1, keepdims=True)
    return ((xf - mu) * lax.rsqrt(var + EPS) * w.astype(jnp.float32)).astype(x.dtype)

def modulate(h, shift, scale):
    return h * (1.0 + scale) + shift

def swiglu(h, w1, w3, w2):
    return (jax.nn.silu(h @ w1) * (h @ w3)) @ w2

def dwconv_centred(x, w, b):
    left = (CONV_W - 1) // 2
    y = lax.conv_general_dilated(x, w[:, None, :], window_strides=(1,),
                                 padding=[(left, CONV_W - 1 - left)],
                                 dimension_numbers=('NWC', 'WIO', 'NWC'),
                                 feature_group_count=x.shape[-1])
    return y + b

def to_heads(t, n):
    b, l, f = t.shape
    return t.reshape(b, l, n, f // n).transpose(0, 2, 1, 3)

def flip_seq(t):
    return jnp.flip(t, axis=2)

def to_colmajor(x):
    b, l, d = x.shape
    rows = l // GRID_W
    return x.reshape(b, rows, GRID_W, d).transpose(0, 2, 1, 3).reshape(b, l, d)

def from_colmajor(x):
    b, l, d = x.shape
    rows = l // GRID_W
    return x.reshape(b, GRID_W, rows, d).transpose(0, 2, 1, 3).reshape(b, l, d)

def _chunks(t):
    return jnp.moveaxis(t.reshape(t.shape[:2] + (t.shape[2] // CHUNK, CHUNK) + t.shape[3:]), 2, 0)

def _unchunk(t):
    t = jnp.moveaxis(t, 0, 2)
    return t.reshape(t.shape[:2] + (-1,) + t.shape[4:])

def gated_linear_scan(q, k, v, log_a, s0):
    f32 = jnp.float32
    causal = jnp.tril(jnp.ones((CHUNK, CHUNK), dtype=bool))
    vector_decay = log_a.shape[-1] != 1

    def step(s, inp):
        qc, kc, vc, gc = inp
        g_cum = jnp.cumsum(gc, axis=2)
        g_last = g_cum[:, :, -1:, :]
        rel = jnp.exp(jnp.where(causal[:, :, None],
                                g_cum[:, :, :, None, :] - g_cum[:, :, None, :, :], -jnp.inf))
        if vector_decay:
            scores = jnp.einsum('bhik,bhjk,bhijk->bhij', qc, kc, rel)
        else:
            scores = jnp.einsum('bhik,bhjk->bhij', qc, kc) * rel[..., 0]
        o = (jnp.einsum('bhij,bhjv->bhiv', scores, vc)
             + jnp.einsum('bhik,bhkv->bhiv', qc * jnp.exp(g_cum), s))
        s = (s * jnp.exp(g_last)[:, :, 0, :, None]
             + jnp.einsum('bhjk,bhjv->bhkv', kc * jnp.exp(g_last - g_cum), vc))
        return s, o

    xs = tuple(_chunks(t.astype(f32)) for t in (q, k, v, log_a))
    s_fin, o = lax.scan(step, s0.astype(f32), xs)
    return _unchunk(o).astype(v.dtype), s_fin

def bidir_scan(q, k_f, k_b, v, la_f, la_b, s0_f, s0_b):
    o_f, s_f = gated_linear_scan(q, k_f, v, la_f, s0_f)
    o_b, s_b = gated_linear_scan(flip_seq(q), flip_seq(k_b), flip_seq(v), flip_seq(la_b), s0_b)
    return o_f + flip_seq(o_b), s_f, s_b

def mlstm_scan(q, k, v, log_i, log_f, state):
    f32 = jnp.float32
    causal = jnp.tril(jnp.ones((CHUNK, CHUNK), dtype=bool))

    def step(carry, inp):
        c0, n0, m0 = carry
        qc, kc, vc, ic, fc = inp
        b = jnp.cumsum(fc, axis=-1)
        log_d = jnp.where(causal, b[..., :, None] - b[..., None, :] + ic[..., None, :], -jnp.inf)
        log_inter = b + m0[..., None]
        m_row = jnp.maximum(log_inter, jnp.max(log_d, axis=-1))
        s = jnp.einsum('bhid,bhjd->bhij', qc, kc) * jnp.exp(log_d - m_row[..., None])
        w_inter = jnp.exp(log_inter - m_row)
        num = (jnp.einsum('bhij,bhje->bhie', s, vc)
               + w_inter[..., None] * jnp.einsum('bhid,bhde->bhie', qc, c0))
        den = jnp.sum(s, axis=-1) + w_inter * jnp.einsum('bhid,bhd->bhi', qc, n0)
        h = num / jnp.maximum(jnp.abs(den), jnp.exp(-m_row))[..., None]
        log_w = b[..., -1:] - b + ic
        m_new = jnp.maximum(b[..., -1] + m0, jnp.max(log_w, axis=-1))
        w_k = jnp.exp(log_w - m_new[..., None])[..., None]
        decay0 = jnp.exp(b[..., -1] + m0 - m_new)
        c_new = decay0[..., None, None] * c0 + jnp.einsum('bhjd,bhje->bhde', kc * w_k, vc)
        n_new = decay0[..., None] * n0 + jnp.sum(kc * w_k, axis=2)
        return (c_new, n_new, m_new), h

    xs = tuple(_chunks(t.astype(f32)) for t in (q, k, v, log_i, log_f))
    final, h = lax.scan(step, state, xs)
    return _unchunk(h).astype(v.dtype), final

def zero_states_gla_ssd(b):
    f32 = jnp.float32
    gla = jnp.zeros((b, GLA_HEADS, GLA_DK, GLA_DV), f32)
    ssd = jnp.zeros((b, SSD_HEADS, SSD_STATE, SSD_HEADDIM), f32)
    return (gla, gla, ssd, ssd)

def zero_states_mlstm(b):
    f32 = jnp.float32
    st = (jnp.zeros((b, MLSTM_HEADS, MLSTM_DH, MLSTM_DH), f32),
          jnp.zeros((b, MLSTM_HEADS, MLSTM_DH), f32),
          jnp.full((b, MLSTM_HEADS), M_INIT, f32))
    return (st, st)

def gla_ssd_features(h, init, w_in, gla_w_gate, gla_b_gate, gla_norm, conv_w, conv_b,
                     a_log, dt_bias, d_skip, ssd_norm):
    b, l, _ = h.shape
    f32 = jnp.float32
    q, k, v, g, r, z, xbc, dt = jnp.split(h @ w_in, A_SPLITS, axis=-1)
    qh = to_heads(q, GLA_HEADS) * (GLA_DK ** -0.5)
    kh = to_heads(k, GLA_HEADS)
    vh = to_heads(v, GLA_HEADS)
    gate_logit = jnp.einsum('bldr,drk->bldk', r.reshape(b, l, 2, GLA_GATE_RANK), gla_w_gate) + gla_b_gate
    log_alpha = jax.nn.log_sigmoid(gate_logit.astype(f32)) / GLA_GATE_TAU
    o_gla, sg_f, sg_b = bidir_scan(qh, kh, kh, vh,
                                   to_heads(log_alpha[:, :, 0], GLA_HEADS),
                                   to_heads(log_alpha[:, :, 1], GLA_HEADS), init[0], init[1])
    o_gla = rmsnorm(o_gla.transpose(0, 2, 1, 3), gla_norm).reshape(b, l, GLA_V) * jax.nn.silu(g)
    xbc = jax.nn.silu(dwconv_centred(xbc, conv_w, conv_b))
    xs, bm, cm = jnp.split(xbc, [SSD_INNER, SSD_INNER + SSD_BC], axis=-1)
    dt = jax.nn.softplus(dt.reshape(b, l, 2, SSD_HEADS).astype(f32) + dt_bias.astype(f32))
    dt = dt.transpose(2, 0, 3, 1)[..., None]
    log_a = dt * (-jnp.exp(a_log.astype(f32)))[:, None, :, None, None]
    rep = SSD_HEADS // SSD_GROUPS
    xh = to_heads(xs, SSD_HEADS)
    bh = jnp.repeat(to_heads(bm, SSD_GROUPS), rep, axis=1)
    ch = jnp.repeat(to_heads(cm, SSD_GROUPS), rep, axis=1)
    y, ss_f, ss_b = bidir_scan(ch, bh * dt[0], bh * dt[1], xh, log_a[0], log_a[1], init[2], init[3])
    y = y + xh * d_skip[None, :, None, None]
    y = y.transpose(0, 2, 1, 3).reshape(b, l, SSD_INNER) * jax.nn.silu(z)
    y = rmsnorm(y.reshape(b, l, SSD_GROUPS, SSD_INNER // SSD_GROUPS),
                ssd_norm.reshape(SSD_GROUPS, SSD_INNER // SSD_GROUPS)).reshape(b, l, SSD_INNER)
    return jnp.concatenate([o_gla, y.astype(o_gla.dtype)], axis=-1), (sg_f, sg_b, ss_f, ss_b)

def mlstm_features(h, init, w_up, conv_w, conv_b, wq, wk, wv, w_if, b_if, mh_norm, skip):
    b, l, _ = h.shape
    f32 = jnp.float32
    xm, z = jnp.split(h @ w_up, 2, axis=-1)
    xc = jax.nn.silu(dwconv_centred(xm, conv_w, conv_b))

    def blockdiag(t, w):
        return jnp.einsum('blnd,nde->blne', t.reshape(b, l, -1, QKV_BLOCK), w).reshape(b, l, MLSTM_INNER)

    q, k, v = blockdiag(xc, wq), blockdiag(xc, wk), blockdiag(xm, wv)
    gates = sum(jnp.einsum('blc,dcg->dbgl', t, w_if[:, i * MLSTM_INNER:(i + 1) * MLSTM_INNER]).astype(f32)
                for i, t in enumerate((q, k, v)))
    gates = gates + b_if.astype(f32)[:, None, :, None]
    log_i = gates[:, :, :MLSTM_HEADS]
    log_f = jax.nn.log_sigmoid(gates[:, :, MLSTM_HEADS:])
    qh = to_heads(q, MLSTM_HEADS)
    kh = to_heads(k, MLSTM_HEADS) * (MLSTM_DH ** -0.5)
    vh = to_heads(v, MLSTM_HEADS)
    h_f, st_f = mlstm_scan(qh, kh, vh, log_i[0], log_f[0], init[0])
    h_b, st_b = mlstm_scan(flip_seq(qh), flip_seq(kh), flip_seq(vh),
                           flip_seq(log_i[1]), flip_seq(log_f[1]), init[1])
    hs = (h_f + flip_seq(h_b)).transpose(0, 2, 1, 3)
    hs = layernorm_nobias(hs, mh_norm.reshape(MLSTM_HEADS, MLSTM_DH)).reshape(b, l, MLSTM_INNER)
    return (hs + skip * xc) * jax.nn.silu(z), (st_f, st_b)

def setup_inputs(seed: int = 0) -> dict:
    key = jax.random.key(seed)
    keys = iter(jax.random.split(key, 48))

    def nrm(shape, scale):
        return jax.random.normal(next(keys), shape, jnp.float32) * scale

    def gain(shape):
        return 1.0 + nrm(shape, 0.05)

    def uni(shape, lo, hi):
        return jax.random.uniform(next(keys), shape, jnp.float32, lo, hi)

    dt0 = jnp.exp(uni((N_EVEN, 2, SSD_HEADS), float(np.log(1e-3)), float(np.log(1e-1))))
    qkv_shape = (N_ODD, MLSTM_INNER // QKV_BLOCK, QKV_BLOCK, QKV_BLOCK)
    return {
        'x': nrm((BATCH, SEQ, D_MODEL), 1.0),
        'c': nrm((BATCH, D_MODEL), 1.0),
        'ctx': nrm((BATCH, CTX_LEN, D_MODEL), 1.0),
        'c_ctx': nrm((D_MODEL,), 1.0),
        'w_mod': nrm((DEPTH, D_MODEL, N_MOD * D_MODEL), D_MODEL ** -0.5),
        'b_mod': nrm((DEPTH, N_MOD * D_MODEL), 0.02),
        'norm_mix': gain((DEPTH, D_MODEL)),
        'norm_ffn': gain((DEPTH, D_MODEL)),
        'ffn_w1': nrm((DEPTH, D_MODEL, D_FF), D_MODEL ** -0.5),
        'ffn_w3': nrm((DEPTH, D_MODEL, D_FF), D_MODEL ** -0.5),
        'ffn_w2': nrm((DEPTH, D_FF, D_MODEL), D_FF ** -0.5),
        'a_w_in': nrm((N_EVEN, D_MODEL, A_IN), D_MODEL ** -0.5),
        'a_gla_w_gate': nrm((N_EVEN, 2, GLA_GATE_RANK, GLA_QK), GLA_GATE_RANK ** -0.5),
        'a_gla_b_gate': nrm((N_EVEN, 2, GLA_QK), 0.5),
        'a_gla_norm': gain((N_EVEN, GLA_DV)),
        'a_ssd_conv_w': nrm((N_EVEN, CONV_W, SSD_XBC), CONV_W ** -0.5),
        'a_ssd_conv_b': nrm((N_EVEN, SSD_XBC), 0.02),
        'a_ssd_A_log': jnp.log(uni((N_EVEN, 2, SSD_HEADS), 1.0, 16.0)),
        'a_ssd_dt_bias': dt0 + jnp.log(-jnp.expm1(-dt0)),
        'a_ssd_D': gain((N_EVEN, SSD_HEADS)),
        'a_ssd_norm': gain((N_EVEN, SSD_INNER)),
        'a_w_out': nrm((N_EVEN, A_MIX, D_MODEL), A_MIX ** -0.5),
        'b_w_up': nrm((N_ODD, D_MODEL, 2 * MLSTM_INNER), D_MODEL ** -0.5),
        'b_conv_w': nrm((N_ODD, CONV_W, MLSTM_INNER), CONV_W ** -0.5),
        'b_conv_b': nrm((N_ODD, MLSTM_INNER), 0.02),
        'b_wq': nrm(qkv_shape, QKV_BLOCK ** -0.5),
        'b_wk': nrm(qkv_shape, QKV_BLOCK ** -0.5),
        'b_wv': nrm(qkv_shape, QKV_BLOCK ** -0.5),
        'b_w_if': nrm((N_ODD, 2, 3 * MLSTM_INNER, 2 * MLSTM_HEADS), (3 * MLSTM_INNER) ** -0.5),
        'b_b_if': jnp.concatenate([nrm((N_ODD, 2, MLSTM_HEADS), 0.1),
                                   jnp.linspace(3.0, 6.0, MLSTM_HEADS) + nrm((N_ODD, 2, MLSTM_HEADS), 0.1)],
                                  axis=-1),
        'b_mh_norm': gain((N_ODD, MLSTM_INNER)),
        'b_skip': gain((N_ODD, MLSTM_INNER)),
        'b_w_down': nrm((N_ODD, MLSTM_INNER, D_MODEL), MLSTM_INNER ** -0.5),
        'final_norm': gain((D_MODEL,)),
    }

def reference(x, c, ctx, c_ctx, w_mod, b_mod, norm_mix, norm_ffn, ffn_w1, ffn_w3, ffn_w2,
              a_w_in, a_gla_w_gate, a_gla_b_gate, a_gla_norm, a_ssd_conv_w, a_ssd_conv_b,
              a_ssd_A_log, a_ssd_dt_bias, a_ssd_D, a_ssd_norm, a_w_out,
              b_w_up, b_conv_w, b_conv_b, b_wq, b_wk, b_wv, b_w_if, b_b_if, b_mh_norm, b_skip,
              b_w_down, final_norm):
    bsz = x.shape[0]
    for layer in range(DEPTH):
        last = layer == DEPTH - 1
        j = layer // 2
        mx = jnp.split((jax.nn.silu(c) @ w_mod[layer] + b_mod[layer])[:, None, :], N_MOD, axis=-1)
        mc = jnp.split(jax.nn.silu(c_ctx) @ w_mod[layer] + b_mod[layer], N_MOD, axis=-1)
        hx = modulate(rmsnorm(x, norm_mix[layer]), mx[0], mx[1])
        hc = modulate(rmsnorm(ctx, norm_mix[layer]), mc[0], mc[1])
        if layer % 2 == 0:
            pa = (a_w_in[j], a_gla_w_gate[j], a_gla_b_gate[j], a_gla_norm[j], a_ssd_conv_w[j],
                  a_ssd_conv_b[j], a_ssd_A_log[j], a_ssd_dt_bias[j], a_ssd_D[j], a_ssd_norm[j])
            fc, st = gla_ssd_features(hc, zero_states_gla_ssd(bsz), *pa)
            fx, _ = gla_ssd_features(hx, st, *pa)
            w_o = a_w_out[j]
        else:
            pb = (b_w_up[j], b_conv_w[j], b_conv_b[j], b_wq[j], b_wk[j], b_wv[j],
                  b_w_if[j], b_b_if[j], b_mh_norm[j], b_skip[j])
            fc, st = mlstm_features(hc, zero_states_mlstm(bsz), *pb)
            fx, _ = mlstm_features(to_colmajor(hx), st, *pb)
            fx = from_colmajor(fx)
            w_o = b_w_down[j]
        x = x + mx[2] * (fx @ w_o)
        x = x + mx[5] * swiglu(modulate(rmsnorm(x, norm_ffn[layer]), mx[3], mx[4]),
                               ffn_w1[layer], ffn_w3[layer], ffn_w2[layer])
        if not last:
            ctx = ctx + mc[2] * (fc @ w_o)
            ctx = ctx + mc[5] * swiglu(modulate(rmsnorm(ctx, norm_ffn[layer]), mc[3], mc[4]),
                                       ffn_w1[layer], ffn_w3[layer], ffn_w2[layer])
    return rmsnorm(x, final_norm)


_drawn_inputs = setup_inputs


def setup_inputs(seed=0):
    import zlib

    import numpy as np

    out = dict(_drawn_inputs(seed))
    spreads = {}
    factors = {'a_ssd_conv_b': 4.858, 'a_ssd_D': 7.117, 'b_mh_norm': 3.147, 'b_skip': 3.392}
    for name, (base, spread) in spreads.items():
        noise = np.random.default_rng([zlib.crc32(name.encode()), seed]).standard_normal(out[name].shape)
        drawn = base * np.exp(spread * noise) if base else spread * noise
        out[name] = jnp.asarray(drawn.astype(out[name].dtype))
    for name, factor in factors.items():
        out[name] = (out[name] * factor).astype(out[name].dtype)
    return out
```

```python
from contextlib import ExitStack

import concourse.bass as bass
from concourse import mybir

F32 = mybir.dt.float32
F32R = mybir.dt.float32r
ALU = mybir.AluOpType
ACT = mybir.ActivationFunctionType

P = 128
D = 1024
KD = D // P
LAT = 512
CTX = 256
T = LAT + CTX
GRID_W = 64
GRID_H = LAT // GRID_W
EPS = 1e-6
N_MOD = 6
MODS = 2 * N_MOD * KD
D_FF = 2816
FF_TILES = D_FF // P
FF_GROUPS = (8, 8, 6)
RING = 4

GLA_HEADS = 4
GLA_DK = 128
GLA_TAU = 16.0
SUB = 64
SSD_HEADS = 16
ML_HEADS = 4
ML_DH = 512

Q0, K0, V0, G0, Z0, X0, B0, C0, PROJ0 = 0, 4, 8, 16, 24, 32, 40, 42, 44
COL_R = 3072
COL_Z = 3104
COL_DT = 5664
PT = {}


def table_rows():
    at = {}
    t1 = [("norm_mix", 16), ("norm_ffn", 16), ("final_norm", 8), ("gla_b", 8), ("gla_norm", 2), ("conv_w", 36),
          ("conv_b", 12), ("ssd_norm", 8), ("c", 8), ("c_ctx", 8)]
    t2 = [("m_conv_w", 48), ("m_conv_b", 16), ("mh_norm", 16), ("skip", 16)]
    for table, rows in ((1, t1), (2, t2)):
        n = 0
        for name, count in rows:
            at[name] = (table, n, count)
            n += count
    at["b_mod"] = (0, 0, MODS)
    return at


ROWS = table_rows()
TABLE_LEN = [max(n + c for t, n, c in ROWS.values() if t == k) for k in range(3)]


def table_loads(a):
    def rows(w):
        while len(w.shape) > 1:
            w = w.rearrange("a b -> (a b)") if len(w.shape) == 2 else w.rearrange("a b c -> (a b c)")
        return w.rearrange("(r p) -> r p", p=P)

    sources = {"b_mod": a["b_mod"], "norm_mix": a["norm_mix"], "norm_ffn": a["norm_ffn"], "final_norm": a["final_norm"],
               "gla_b": a["a_gla_b_gate"], "gla_norm": a["a_gla_norm"], "conv_w": a["a_ssd_conv_w"],
               "conv_b": a["a_ssd_conv_b"], "ssd_norm": a["a_ssd_norm"], "c": a["c"], "c_ctx": a["c_ctx"],
               "m_conv_w": a["b_conv_w"], "m_conv_b": a["b_conv_b"], "mh_norm": a["b_mh_norm"], "skip": a["b_skip"]}
    return [(*ROWS[name][:2], rows(w)) for name, w in sources.items()]


def each_ring(eng, n0, count, body):
    first, last = n0 // RING, (n0 + count) // RING
    while first < min(2, last):
        for s in range(RING):
            body(first, s)
        first += 1
    if first < last:
        with eng.Fori(first, last) as r:
            for s in range(RING):
                body(r, s)


class Chain:

    def __init__(self, eng, own):
        self.eng, self.own, self.n = eng, own, {}

    def __call__(self, ins, sem=None, wait=True):
        sem = sem or self.own
        self.n[sem] = self.n.get(sem, 0) + 1
        ins.then_inc(sem, 1)
        if wait:
            self.eng.wait_ge(sem, self.n[sem])


def weight_segments(a):
    def kview(w):
        return w.rearrange("(k p) m -> p k m", p=P)

    segs, n = {}, 0

    def seg(name, count, kt, w, col0=0, w_odd=None):
        nonlocal n
        assert n % RING == 0 and count % RING == 0
        n0 = n
        if w_odd is None:
            def src(r, s):
                return w[:, :, bass.ds(r * (RING * P) + (s * P + col0 - n0 * P), P)]
        else:
            def src(r, s):
                return (w_odd if s % 2 else w)[:, :, bass.ds(r * (2 * P) + (s // 2 * P + col0 - n0 // 2 * P), P)]
        segs[name] = (n0, count, kt, src)
        n += count

    win, wup, wdn = kview(a["a_w_in"][0]), kview(a["b_w_up"][0]), kview(a["b_w_down"][0])
    wout = kview(a["a_w_out"][0])

    def ffn(layer):
        w1, w3, w2 = (kview(a[x][layer]) for x in ("ffn_w1", "ffn_w3", "ffn_w2"))
        f0 = 0
        for g, tiles in enumerate(FF_GROUPS):
            seg(f"up{layer}{g}", 2 * tiles, KD, w1, f0 * P, w3)
            seg(f"down{layer}{g}", KD, tiles, w2[:, f0:f0 + tiles, :])
            f0 += tiles

    seg("qkv", 16, KD, win)
    seg("g", 8, KD, win, 16 * P)
    seg("z", 8, KD, win, COL_Z)
    seg("xbc", 12, KD, win, COL_Z + 8 * P)
    seg("out0", 8, KD, wout[:, 0:KD, :])
    seg("out1", 8, KD, wout[:, KD:2 * KD, :])
    ffn(0)
    seg("xm", 16, KD, wup)
    seg("zm", 16, KD, wup, 16 * P)
    seg("mout0", 8, KD, wdn[:, 0:KD, :])
    seg("mout1", 8, KD, wdn[:, KD:2 * KD, :])
    ffn(1)
    segs["end"] = (n, 0, 0, None)
    return segs


def trunk(nc, a, out):
    segs = weight_segments(a)
    base, end = -(-nc.sbuf_base // 32) * 32, nc.sbuf_usable_end
    with ExitStack() as stack:
        top = [base]

        def sem(name):
            return stack.enter_context(nc.semaphore(name))

        def sb(name, shape, dt=F32, offset=None):
            size = 4
            for d in shape[1:]:
                size *= d
            where = top[0] if offset is None else arena_at + offset
            if offset is None:
                top[0] += -(-size // 32) * 32
            assert where + size <= end, (name, where + size - end)
            return nc.alloc_sbuf_tensor_at(name, shape, dt, offset=where)

        def dram(name, shape):
            return nc.dram_tensor(name, shape, F32, kind="Internal").ap()

        xT = sb("xT", [P, KD, T])
        act_hi_at = top[0]
        act_hi = sb("act_hi", [P, KD, T], F32R)
        act_lo_at = top[0]
        act_lo = sb("act_lo", [P, KD, T], F32R)
        w_raw = sb("w_raw", [P, RING, KD, P])
        w_hi = sb("w_hi", [P, RING, KD, P], F32R)
        w_lo = sb("w_lo", [P, RING, KD, P], F32R)
        ident = sb("ident", [P, P])
        ones = sb("ones", [P, P])
        tri = sb("tri", [P, 2, P])
        ptab = sb("ptab", [P, 3, P])
        modv = sb("modv", [P, MODS, 2])
        mscale = sb("mscale", [P, 2, 2, KD, 2])
        cs = sb("cs", [P, KD, 2])
        rcol = sb("rcol", [P, T // P])
        rdiag = sb("rdiag", [P, T])
        eps_col = sb("eps_col", [P, 1])
        one_col = sb("one_col", [P, 1])
        arena_at = top[0]
        PS = stack.enter_context(nc.psum_tensor("PS", [P, 4096], F32))

        def slot(s):
            return PS[:, 1024 * s:1024 * s + T]

        def bank(b, n=512):
            return PS[:, 512 * b:512 * b + n]

        def par(name, k, n=1):
            t, row, _ = ROWS[name]
            return ptab[:, t, row + k:row + k + n]

        def par_at(name, j):
            t, row, _ = ROWS[name]
            return ptab[:, t, bass.ds(j + row, 1)]

        def mod_col(s):
            return 1024 * s + T

        def mod(layer, which, k):
            return layer * N_MOD * KD + which * KD + k

        proj0 = dram("proj0", (PROJ0, P, T))

        w_in = [sem(f"w_in{s}") for s in range(RING)]
        w_hi_done = sem("w_hi_done")
        w_split = sem("w_split")
        mm_done = sem("mm_done")
        evac = sem("evac")
        act_ready = sem("act_ready")
        act_own, dve_own, pool_own = sem("act_own"), sem("dve_own"), sem("pool_own")
        tab_in, x_in, consts = sem("tab_in"), sem("x_in"), sem("consts")
        tab_tr, x_tr, x_put, c_silu, mod_mm, mod_put = (sem(n) for n in ("tab_tr", "x_tr", "x_put", "c_silu", "mod_mm", "mod_put"))
        tab_put = sem("tab_put")
        mod_in = [sem(f"mod_in{s}") for s in range(3)]
        mrow_put, mrow_tr = sem("mrow_put"), sem("mrow_tr")
        m_in = [sem(f"m_in{s}") for s in range(RING)]
        m_step = sem("m_step")
        m_put = sem("m_put")
        prow = sb("prow", [P, 3, P], offset=0)
        xin = sb("xin", [P, 6, D], offset=1536)
        m_raw = sb("m_raw", [P, 3, KD, 512], offset=1536 + 24576)
        mrow = nc.alloc_sbuf_tensor_at("mrow", [2, 16 * P], F32, offset=act_lo_at)
        sq_done, sum_done, sum_mm, std_done, rstd_done, nt_done, nh_done, nhi_done = (
            sem(n) for n in ("sq_done", "sum_done", "sum_mm", "std_done", "rstd_done", "nt_done", "nh_done", "nhi_done"))
        nsum_step = sem("nsum_step")
        nsq = sb("nsq", [P, 2, T], offset=0)
        nacc = sb("nacc", [P, T], offset=6144)
        diag_done = sem("diag_done")
        nt = sb("nt", [P, 2, T], offset=12288)
        nh = sb("nh", [P, 2, T], offset=18432)
        stage = sb("stage", [P, RING, T], offset=24576)
        cpre = sb("cpre", [P, 2, T], offset=36864)
        cpost = sb("cpost", [P, 2, T], offset=43008)
        m_ring = sb("m_ring", [P, RING, KD, 2 * P], offset=49152)
        m_acc = sb("m_acc", [P, 2, 2, 2 * P], offset=18432)
        rd_raw = sb("rd_raw", [P, KD, P], offset=0)
        rd_hi = sb("rd_hi", [P, KD, P], F32R, offset=4096)
        rd_lo = sb("rd_lo", [P, KD, P], F32R, offset=8192)
        rT = sb("rT", [32, T], offset=12288)
        dtT = sb("dtT", [32, T], offset=15360)
        st_out = [sem(f"st_out{s}") for s in range(RING)]
        conv_step, silu_done, rd_in, rd_hi_done, rd_split, rd_mm, rd_put = (
            sem(n) for n in ("conv_step", "silu_done", "rd_in", "rd_hi_done", "rd_split", "rd_mm", "rd_put"))

        hq = sb("hq", [P, 4, T], offset=0)
        wg = sb("wg", [32, 2, P], offset=18432)
        gG = sb("gG", [P, 2, T], offset=19456)
        ga = sb("ga", [P, 2, T], offset=25600)
        gm = sb("gm", [P, 2, T], offset=31744)
        K2 = sb("K2", [P, 2, 6, 2, 2, SUB], offset=37888)
        qs = sb("qs", [P, 2, 6, SUB], offset=50176)
        qd = sb("qd", [P, 2, T], offset=53248)
        gS = sb("gS", [P, 2, 5, 2 * P], offset=59392)
        kdT = sb("kdT", [P, 10, P], offset=69632)
        vtok = sb("vtok", [P, 6, 2 * P], offset=74752)
        etot = sb("etot", [P, 2, 6], offset=80896)
        oT = gG
        hq_in, wg_zero, gate_mm, abs_done, min_done, ln_done, g_ready, x_ready, e0_done, qd_done, e1_done, e3_done = (
            sem("gla_" + n) for n in ("hq_in", "wg_zero", "gate_mm", "abs_done", "min_done", "ln_done", "g_ready", "x_ready",
                                      "e0_done", "qd_done", "e1_done", "e3_done"))
        y_ready, e4_done, kd_done, tr_done, tr_put, u_mm, s_done, sc_mm, a_done, o_mm, o_put, g_in, gsq_done, gfull = (
            sem("gla_" + n) for n in ("y_ready", "e4_done", "kd_done", "tr_done", "tr_put", "u_mm", "s_done", "sc_mm", "a_done",
                                      "o_mm", "o_put", "g_in", "gsq_done", "gfull"))
        CHUNKS = ((4, 5, 0, 1, 2, 3), (5, 4, 3, 2, 1, 0))
        KD_ORDER = [(d, CHUNKS[d][i]) for i in range(5) for d in range(2)]

        PAIRS = SSD_HEADS // 2
        DL, DC, DB = 0, 4 * LAT, 4 * LAT + 2 * CTX
        Dm = sb("Dm", [P, 2, DB + 6 * P], offset=0)
        cb = sb("cb", [P, DB], offset=26624)
        Grow = sb("Grow", [32, 2, T], offset=36864)
        xt = sb("xt", [P, 2, T], offset=43008)
        xtok = sb("xtok", [P, 2, 6, P], offset=49152)
        sz = sb("sz", [P, 2, T], offset=55296)
        bct = sb("bct", [P, 2, T], offset=61440)
        Btok = sb("Btok", [P, 2, P], offset=67584)
        nb = sb("nb", [P, 2, 6, 32], offset=68608)
        al = sb("al", [P, 2, 2, 32], offset=70144)
        ssS = sb("ssS", [P, 2, 2, P], offset=70656)
        xal = sb("xal", [P, 2, 2, 2, P], offset=72704)
        dcol = sb("dcol", [P, PAIRS], offset=76800)
        rowc = sb("rowc", [32, 4], offset=76832)
        Cb = nc.alloc_sbuf_tensor_at("Cb", [P, 2, 2, LAT], F32, offset=act_hi_at + 4 * T * 4)
        snacc = [sb("snacc0", [P, T], offset=76864), nc.alloc_sbuf_tensor_at("snacc1", [P, T], F32, offset=act_hi_at + 7 * T * 4)]
        ssq = nc.alloc_sbuf_tensor_at("ssq", [P, 2, T], F32, offset=act_hi_at + 2 * T * 4)
        yT = nc.alloc_sbuf_tensor_at("yT", [P, KD, T], F32, offset=act_lo_at)
        r_ab = sb("r_ab", [32, T], offset=0)
        r_e = sb("r_e", [32, T], offset=3072)
        r_s2 = sb("r_s2", [32, T], offset=6144)
        r_p = sb("r_p", [32, T], offset=9216)
        r_zz = sb("r_zz", [32, T], offset=12288)
        r_ln = sb("r_ln", [32, T], offset=18432)
        r_nb = sb("r_nb", [32, 2, T], offset=43008)
        r_al = sb("r_al", [32, 2, CTX], offset=49152)
        row_in, r_ez, r_dt, r_lnd, r_nbd, r_ald, ct_mm, ct_put, bc_in, cb_mm, cb_put, xt_in, xt_tr, xt_put, xal_done, s_mm = (
            sem("ssd_" + n) for n in ("row_in", "r_ez", "r_dt", "r_lnd", "r_nbd", "r_ald", "ct_mm", "ct_put", "bc_in", "cb_mm",
                                      "cb_put", "xt_in", "xt_tr", "xt_put", "xal_done", "s_mm"))
        ss_put, rows_mm, exp_done, mask_done, m_done, cbeta_done, y_mm, y_put, y_done, ysq_done, ysum = (
            sem("ssd_" + n) for n in ("ss_put", "rows_mm", "exp_done", "mask_done", "m_done", "cbeta_done", "y_mm", "y_put", "y_done",
                                      "ysq_done", "ysum"))
        yn_done, e_done, rows_read = sem("ssd_yn_done"), sem("ssd_e_done"), sem("ssd_rows_read")

        fsg = sb("fsg", [P, 2, T], offset=0)
        fhp = sb("fhp", [P, 2, T], offset=6144)
        hid_hi = sb("hid_hi", [P, 8, T], F32R, offset=12288)
        hid_lo = sb("hid_lo", [P, 8, T], F32R, offset=36864)
        fsg_done, fhh_done, hid_ready = sem("ffn_sg_done"), sem("ffn_hi_done"), sem("hid_ready")
        FF_BEFORE = {f"{layer}{g}": layer * FF_TILES + sum(FF_GROUPS[:g]) for layer in range(2) for g in range(3)}

        A_at = 61440
        wA = sb("wA", [P, 16, P], offset=A_at)
        w4 = sb("w4", [P, 3, 16, 4], offset=A_at + 8192)
        mask4 = sb("mask4", [P, P], offset=A_at + 8960)
        wG = sb("wG", [P, 2, 16, 40], offset=A_at + 9472)
        bif = sb("bif", [8, 2], offset=A_at + 14592)
        bd = sb("bd", [P, 2, 3, P], offset=24576)
        bdT = sb("bdT", [P, 2, 3, P], offset=27648)
        wif = rdiag[:].rearrange("p (x t d g) -> p x t d g", x=3, t=16, d=2)
        xms = sb("xms", [P, RING, T], offset=24576)
        xcr = sb("xcr", [P, RING, T], offset=36864)
        zst = sb("zst", [P, RING, LAT], offset=49152)
        gx = sb("gx", [P, RING, 2, T], offset=0)
        xm_d, xc_d = dram("xm_d", (16, P, T)), dram("xc_d", (16, P, T))
        z_d = dram("z_d", (16, P, LAT))
        wb_in, wif_in, m4_done, bd_done, bdt_mm, bdt_put, wa_mm, wa_put, wg0, mxc_done, gx_mm = (
            sem("ml_" + n) for n in ("wb_in", "wif_in", "m4_done", "bd_done", "bdt_mm", "bdt_put", "wa_mm", "wa_put", "wg0", 
                                     "mxc_done", "gx_mm"))

        mr_i = sb("mr_i", [8, T], offset=0)
        mr_f = sb("mr_f", [8, T], offset=3072)
        mr_ab = sb("mr_ab", [8, T], offset=6144)
        mr_b = sb("mr_b", [8, 2, T], offset=9216)
        mr_u = sb("mr_u", [8, 2, T], offset=15360)
        mr_M = sb("mr_M", [8, 2, T], offset=24576)
        mr_m = sb("mr_m", [8, 2, LAT], offset=30720)
        negM = sb("negM", [8, 2, LAT], offset=77056)
        ucol = sb("ucol", [P, 2, 6, 8], offset=81152)
        ecol = sb("ecol", [P, 2, 4, 8], offset=81536)
        dcl = sb("dcl", [P, 2, 4], offset=81792)
        xch = sb("xch", [P, 4, T], offset=0)
        xmr = sb("xmr", [P, 2, T], offset=12288)
        vt = sb("vt", [P, 6, 4 * P], offset=18432)
        qp = sb("qp", [P, 4, LAT], offset=30720)
        Wf = sb("Wf", [P, 6, LAT], offset=38912)
        hh = sb("hh", [P, 4, LAT], offset=51200)
        bdv = sb("bdv", [P, 4, P], offset=59392)
        mtmp = sb("mtmp", [P, 3, LAT], offset=70912)
        act1_hi = nc.alloc_sbuf_tensor_at("act1_hi", [P, KD, LAT], F32R, offset=act_hi_at)
        act1_lo = nc.alloc_sbuf_tensor_at("act1_lo", [P, KD, LAT], F32R, offset=act_hi_at + KD * LAT * 4)
        Wb = nc.alloc_sbuf_tensor_at("Wb", [P, 6, LAT], F32, offset=act_hi_at + 2 * KD * LAT * 4)
        zs = nc.alloc_sbuf_tensor_at("zs", [P, 2, LAT], F32, offset=act_hi_at + 2 * KD * LAT * 4 + 6 * LAT * 4)

        def xs(i):
            return xT[:, 2 * i:2 * i + 2, LAT:T]

        def halves(ap):
            return ap.rearrange("p (a t) -> p a t", a=2)

        A8 = 2 * GLA_HEADS
        A24, A40 = 6 * GLA_HEADS, 10 * GLA_HEADS
        mrows_mm, MROWS_MM0 = gate_mm, A8
        de_done, DE_DONE0 = min_done, A8
        wr_done, WR_DONE0 = abs_done, A8
        we_done, WE_DONE0 = ln_done, A8
        den_rdy, DEN_RDY0 = g_ready, A8
        rd_rdy, RD_RDY0 = x_ready, A8
        pn_done, PN_DONE0 = qd_done, A8
        hs_rdy, HS_RDY0 = y_ready, A8
        hc_done, HC_DONE0 = kd_done, A8
        h_put, H_PUT0 = e0_done, A8
        hsq_done, HSQ_DONE0 = e1_done, A8
        fin_done, FIN_DONE0 = gfull, A8
        h_mm, H_MM0 = tr_done, A24
        qv_mm, QV_MM0 = sc_mm, A24
        qv_put, QV_PUT0 = tr_put, A24
        s6_mm, S6_MM0 = u_mm, A40
        s6_put, S6_PUT0 = s_done, A40
        rfb_mm, RFB_MM0 = o_mm, A24
        xch_in, XCH_IN0 = hq_in, 96 * GLA_HEADS
        hsum, HSUM0 = a_done, A24
        xm_out, XM_OUT0 = st_out, 176
        z_out, Z_OUT0 = st_out, 240
        xc_out, XC_OUT0 = m_in, 160
        gx_in, GX_IN0 = m_in, 224
        xs_in, XS_IN0 = m_in, 352
        xmr_in, XMR_IN0 = st_out[0:2], 304
        z_in, Z_IN0 = st_out[2:4], 304
        gr_put, gab_done, gln_done, gm_done, ge_done, gc_mm, gc_put = (
            sem("mg_" + n) for n in ("gr_put", "gab_done", "gln_done", "gm_done", "ge_done", "gc_mm", "gc_put"))
        mk_done, bdv_done, den_mm, mean_mm = (sem("mh_" + n) for n in ("mk_done", "bdv_done", "den_mm", "mean_mm"))
        KEYS = (4, 5, 0, 1, 2, 3)
        fin = sb("fin", [P, KD, LAT], offset=24576)
        obuf = sb("obuf", [P, 2, D], offset=43008)
        fin_ready, out_tr, out_put = (sem(n) for n in ("fin_ready", "out_tr", "out_put"))
        out_st = [sem(f"out_st{s}") for s in range(2)]

        def diagonals(t, off, n, step):
            ap = t[:, off:off + P]
            return bass.AP(tensor=ap.tensor, offset=ap.offset, ap=[list(ap.ap[0]), [step, n], [1, P]])

        WITH_MOD = ("qkv", "g", "z", "xbc")
        MOD_UNITS = 44
        NORMS = ["mix0", "ffn0", "mix1", "ffn1", "final"]
        READY = {name: KD * i for i, name in enumerate(("mix0", "gla", "ssd", "ffn0", "mix1", "ml0", "ml1", "ffn1"))}

        def nh_count(name, tiles):
            return 2 * KD * NORMS.index(name) + tiles * (1 if name == "ffn1" else 2)

        block = stack.enter_context(nc.Block())

        @block.sync
        def _(sp):
            for t, row, src in table_loads(a):
                sp.dma_start(prow[row:row + src.shape[0], t, :], src).then_inc(tab_in, 16)
            sp.dma_start(xin[:, 0:4, :], a["x"][0].rearrange("(a p) d -> p a d", p=P)).then_inc(x_in, 16)
            sp.dma_start(xin[:, 4:6, :], a["ctx"][0].rearrange("(a p) d -> p a d", p=P)).then_inc(x_in, 16)
            for u in range(4):
                if u >= 3:
                    sp.wait_ge(mod_mm, u - 2)
                wm = a["w_mod"][0].rearrange("(k p) m -> p k m", p=P)
                sp.dma_start(m_raw[:, u % 3], wm[:, :, 512 * u:512 * u + 512]).then_inc(mod_in[u % 3], 16)
            n0, _, kt, src = segs["qkv"]
            for s in range(RING):
                sp.dma_start(w_raw[:, s, 0:kt], src(0, s)).then_inc(w_in[s], 16)
            sp.wait_ge(mod_put, 1)

            for name, (n0, count, kt, src) in segs.items():
                def load(r, s, kt=kt, src=src):
                    sp.wait_ge(w_split, r * RING + (s - RING + 1))
                    sp.dma_start(w_raw[:, s, 0:kt], src(r, s)).then_inc(w_in[s], 16)

                if n0 >= MOD_UNITS:
                    each_ring(sp, n0, count, load)
                    continue

                for r0, r1 in ((max(n0 // RING, 1), min((n0 + count) // RING, 5)), (max(n0 // RING, 5), (n0 + count) // RING)):
                    if r0 >= r1:
                        continue
                    layer = r0 // 5 if r0 < 5 else 1
                    wm = a["w_mod"][layer].rearrange("(k p) m -> p k m", p=P)

                    def load_both(r, s):
                        load(r, s)
                        if not (isinstance(r, int) and r == 1):
                            sp.wait_ge(m_step, (r * RING + (s - 2 * RING + 1)) * (2 * KD))
                        col = r * (2 * RING * P) + ((2 * s + 8 - 48 * layer) * P)
                        sp.dma_start(m_ring[:, s], wm[:, :, bass.ds(col, 2 * P)]).then_inc(m_in[s], 16)

                    if r0 == 1:
                        for s in range(RING):
                            load_both(1, s)
                        r0 = 2
                    each_ring(sp, r0 * RING, (r1 - r0) * RING, load_both)

        @block.gpsimd
        def _(pool):
            chain = Chain(pool, pool_own)
            chain(pool.memset(ones[:], 1.0))
            chain(pool.memset(eps_col[:], EPS))
            chain(pool.memset(one_col[:], 1.0))
            chain(pool.memset(ident[:], 0.0))
            chain(pool.memset(tri[:], 1.0))
            chain(pool.affine_select(out=ident[:], in_=ident[:], compare_op=ALU.not_equal, fill=1.0, base=0,
                                     pattern=[[-1, P]], channel_multiplier=1))
            chain(pool.affine_select(out=tri[:, 0], in_=tri[:, 0], compare_op=ALU.is_ge, fill=0.0, base=0,
                                     pattern=[[1, P]], channel_multiplier=-1))
            chain(pool.affine_select(out=tri[:, 1], in_=tri[:, 1], compare_op=ALU.is_ge, fill=0.0, base=0,
                                     pattern=[[-1, P]], channel_multiplier=1), consts)

            def split(r, s, kt, n0=None):
                pool.wait_ge(w_in[s], r * 16 + 16)
                if not (isinstance(r, int) and r == 0):
                    pool.wait_ge(mm_done, r * RING + (s - RING + 1))
                pool.tensor_tensor(w_hi[:, s, 0], w_raw[:, s, 0], ones[:], ALU.mult)
                pool.tensor_scalar(w_hi[:, s, 1:kt], w_raw[:, s, 1:kt], 1.0, 1.0, ALU.mult, ALU.mult).then_inc(w_hi_done, 1)
                pool.wait_ge(w_hi_done, r * RING + (s + 1))
                pool.tensor_tensor(w_lo[:, s, 0:kt], w_raw[:, s, 0:kt], w_hi[:, s, 0:kt].bitcast(F32),
                                   ALU.subtract).then_inc(w_split, 1)

            for name, (n0, count, kt, src) in segs.items():
                if name == "out0":
                    pool.wait_ge(act_ready, READY["mix0"] + KD)
                    pool.wait_ge(rd_in, 32)
                    pool.tensor_scalar(rd_hi[:], rd_raw[:], 1.0, 1.0, ALU.mult, ALU.mult).then_inc(rd_hi_done, 1)
                    pool.wait_ge(rd_hi_done, 1)
                    pool.tensor_tensor(rd_lo[:], rd_raw[:], rd_hi[:].bitcast(F32), ALU.subtract).then_inc(rd_split, 1)
                if name == "out1":
                    each_ring(pool, n0, RING, lambda r, s: split(r, s, kt))
                    for h in range(SSD_HEADS):
                        d = Dm[:, h % 2]
                        pool.wait_ge(e_done, 2 * h + 1)
                        for off, n, step in ((DL, 4, LAT + P), (DC, 2, CTX + P)):
                            blocks = diagonals(d, off, n, step)
                            pool.affine_select(out=blocks, in_=blocks, compare_op=ALU.is_ge, fill=-1e30, base=0,
                                               pattern=[[0, n], [1, P]], channel_multiplier=-1).then_inc(mask_done, 1)
                        pool.wait_ge(e_done, 2 * h + 2)
                        blocks = diagonals(d, DB, 6, P)
                        pool.affine_select(out=blocks, in_=blocks, compare_op=ALU.is_ge, fill=-1e30, base=0,
                                           pattern=[[0, 6], [-1, P]], channel_multiplier=1).then_inc(mask_done, 1)
                    each_ring(pool, n0 + RING, count - RING, lambda r, s: split(r, s, kt))
                    continue
                if name in ("mout0", "mout1"):
                    each_ring(pool, n0, RING, lambda r, s: split(r, s, kt))
                    for h in range(3) if name == "mout0" else (3,):
                        for d in range(2):
                            pool.wait_ge(de_done, DE_DONE0 + 2 * h + d + 1)
                            blocks = diagonals((Wf, Wb)[d][:].rearrange("p c t -> p (c t)"), 0, 4, LAT + P)
                            pool.affine_select(out=blocks, in_=blocks, compare_op=ALU.is_ge, fill=-1e30, base=0,
                                               pattern=[[0, 4], [1 - 2 * d, P]], channel_multiplier=2 * d - 1).then_inc(mk_done, 1)
                    each_ring(pool, n0 + RING, count - RING, lambda r, s: split(r, s, kt))
                    continue
                each_ring(pool, n0, count, lambda r, s: split(r, s, kt))
                if name == "up00":
                    pool.wait_ge(yn_done, 8)
                    m3 = mask4[:].rearrange("p (b e) -> p b e", e=4)
                    chain(pool.memset(mask4[:], 1.0))
                    chain(pool.memset(wG[:], 0.0), wg0)
                    chain(pool.affine_select(out=m3, in_=m3, compare_op=ALU.is_ge, fill=0.0, base=0,
                                             pattern=[[-4, 32], [0, 4]], channel_multiplier=1))
                    chain(pool.affine_select(out=m3, in_=m3, compare_op=ALU.is_ge, fill=0.0, base=3,
                                             pattern=[[4, 32], [0, 4]], channel_multiplier=-1), m4_done)

        @block.tensor
        def _(pe):
            pe.wait_ge(consts, 1)
            pe.wait_ge(tab_in, 16 * len(table_loads(a)))
            for t in range(3):
                n = TABLE_LEN[t]
                pe.transpose(bank(0)[:, t * P:t * P + n], prow[0:n, t, :], ident[0:n, 0:n]).then_inc(tab_tr, 1)
            pe.wait_ge(x_in, 32)
            for i in range(12):
                tt, half = i // 2, i % 2
                if i >= 2:
                    pe.wait_ge(x_put, i - 1)
                for q in range(4):
                    k = 4 * half + q
                    last = pe.transpose(bank(1 + i % 2)[:, q * P:q * P + P], xin[:, tt, k * P:k * P + P], ident[:])
                last.then_inc(x_tr, 1)
            pe.wait_ge(c_silu, 2)
            for u in range(4):
                pe.wait_ge(mod_in[u % 3], 16 * (u // 3 + 1))
                for k in range(KD):
                    last = pe.matmul(bank(3 + u)[0:2, :], cs[:, k, :], m_raw[:, u % 3, k, :], start=k == 0, stop=k == KD - 1)
                last.then_inc(mod_mm, 1)
            pe.wait_ge(mrow_put, 4)
            for m in range(16):
                last = pe.transpose(bank(7)[:, 2 * m:2 * m + 2], mrow[:, m * P:m * P + P], ident[0:2, 0:2])
            last.then_inc(mrow_tr, 1)

            rstds = [0]

            def rstd_products(sq, n, where):
                pe.wait_ge(sum_done, rstds[0] + 1)
                for t in range(n // P):
                    last = pe.matmul(slot(where)[:, t:t + 1], sq[:, t * P:t * P + P], ones[:, 0:1], start=True, stop=True)
                last.then_inc(sum_mm, 1)
                pe.wait_ge(diag_done, rstds[0] + 1)
                for c0, c1 in ((0, 512), (512, 768))[:1 if n == LAT else 2]:
                    last = pe.matmul(slot(where)[:, c0:c1], ones[:], rdiag[:, c0:c1], start=True, stop=True)
                last.then_inc(rstd_done, 1)
                rstds[0] += 1

            def unit(s, kt, hi, lo, n, wh, wl):
                for k in range(kt):
                    for w, x in ((wh, hi), (wh, lo), (wl, hi)):
                        for c0, c1 in ((0, 512), (512, 768))[:1 if n == LAT else 2]:
                            last = pe.matmul(slot(s)[:, c0:c1], w[:, k, :], x[:, k, c0:c1],
                                             start=k == 0 and w is wh and x is hi, stop=k == kt - 1 and w is wl)
                return last

            def project(name, hi, lo, n, ready, ready0):
                n0, count, kt, _ = segs[name]
                each_ring(pe, n0, count, lambda r, s: project_unit(name, r, s, kt, hi, lo, n, ready, ready0))

            def project_unit(name, r, s, kt, hi, lo, n, ready, ready0):
                pe.wait_ge(w_split, r * RING + (s + 1))
                if not (isinstance(r, int) and r == 0):
                    pe.wait_ge(evac, r * RING + (s - RING + 1))
                    if name in WITH_MOD and not (isinstance(r, int) and r <= 1):
                        pe.wait_ge(m_put, r * RING + (s - 2 * RING + 1))
                for k in range(kt):
                    if s == 0:
                        pe.wait_ge(ready, ready0 + k + 1)
                    for w, x in ((w_hi, hi), (w_hi, lo), (w_lo, hi)):
                        for c0, c1 in ((0, 512), (512, 768))[:1 if n == LAT else 2]:
                            last = pe.matmul(slot(s)[:, c0:c1], w[:, s, k, :], x[:, k, c0:c1],
                                             start=k == 0 and w is w_hi and x is hi, stop=k == kt - 1 and w is w_lo)
                    if name in WITH_MOD and not (isinstance(r, int) and r == 0) and k % 2 == 0:
                        if k == 0:
                            pe.wait_ge(m_step, (r * RING + (s - RING + 1)) * (2 * KD))
                        m, v = k // 4, k // 2 % 2
                        pe.matmul(PS[:, mod_col(s) + k // 2:mod_col(s) + k // 2 + 1], m_acc[:, s % 2, v, m * P:m * P + P],
                                  ones[:, 0:1], start=False, stop=False, skip_group_check=True)
                last.then_inc(mm_done, 1)

            rstd_products(nacc, T, 0)
            pe.wait_ge(nt_done, KD)
            for name in ("qkv", "g", "z", "xbc"):
                project(name, act_hi, act_lo, T, act_ready, 0)
            pe.wait_ge(rd_split, 1)
            pe.wait_ge(evac, MOD_UNITS)
            pe.wait_ge(m_put, MOD_UNITS - RING)
            unit(0, KD, act_hi, act_lo, T, rd_hi, rd_lo).then_inc(rd_mm, 1)
            pe.wait_ge(rd_put, 2)
            pe.wait_ge(wg_zero, 2)
            for h in range(GLA_HEADS):
                pe.wait_ge(hq_in, 96 * (h + 1))
                if h:
                    pe.wait_ge(gfull, 2 * h)
                    pe.wait_ge(a_done, 6 * h)
                for d in range(2):
                    for c0, c1 in ((0, 512), (512, 768)):
                        last = pe.matmul(slot(d)[:, c0:c1], wg[:, d, :], rT[:, c0:c1], start=True, stop=True)
                    last.then_inc(gate_mm, 1)
                pe.wait_ge(min_done, 2 * h + 2)
                pe.wait_ge(abs_done, 2 * h + 2)
                for i in range(3):
                    if i == 2:
                        pe.wait_ge(tr_put, 6 * h + 1)
                    for c in (2 * i, 2 * i + 1):
                        for t in range(2):
                            at = (c % 2 * 2 + t) * P
                            last = pe.transpose(bank(i % 2)[:, at:at + P], hq[:, 2 + t, c * P:c * P + P], ident[:])
                    last.then_inc(tr_done, 1)
                pe.wait_ge(kd_done, 2 * h + 2)
                for i in range(3):
                    pe.wait_ge(tr_put, 6 * h + i + 2)
                    for e in range(4 * i, min(4 * i + 4, 10)):
                        d, c = KD_ORDER[e]
                        last = pe.transpose(bank((3 + i) % 2)[:, e % 4 * P:e % 4 * P + P], ga[:, d, c * P:c * P + P], ident[:])
                    last.then_inc(tr_done, 1)

                def scores(i):
                    c = CHUNKS[0][i]
                    if i >= 2:
                        pe.wait_ge(a_done, 6 * h + i - 1)
                    for d in range(2):
                        for b in range(2):
                            q = qd[:, d, c * P + b * SUB:c * P + b * SUB + SUB] if b == d else qs[:, d, c, :]
                            last = pe.matmul(bank(2 + i % 2)[:, d * P + b * SUB:d * P + b * SUB + SUB],
                                             K2[:, d, c, b].rearrange("p a t -> p (a t)"), q, start=True, stop=True)
                    last.then_inc(sc_mm, 1)

                scores(0)
                for e, (d, c) in enumerate(KD_ORDER):
                    pe.wait_ge(tr_put, 6 * h + 4 + e // 4)
                    if 10 * h + e - 1 >= 1:
                        pe.wait_ge(s_done, 10 * h + e - 1)
                    pe.matmul(bank(4 + d)[:, 0:2 * P], kdT[:, e, :], vtok[:, c, :], start=True, stop=True).then_inc(u_mm, 1)
                    if d:
                        scores(e // 2 + 1)
                pe.wait_ge(s_done, 10 * h + 10)
                for i, c in enumerate(CHUNKS[0]):
                    pe.wait_ge(a_done, 6 * h + i + 1)
                    if 6 * h + i >= 2:
                        pe.wait_ge(o_put, 6 * h + i - 1)
                    for t in range(2):
                        terms = [(vtok[:, c, t * P:t * P + P], gm[:, 0, i * P:i * P + P])]
                        for d in range(2):
                            k = CHUNKS[d].index(c)
                            if k:
                                terms.append((gS[:, d, k - 1, t * P:t * P + P], qd[:, d, c * P:c * P + P]))
                        for n, (w, x) in enumerate(terms):
                            last = pe.matmul(bank(6 + i % 2)[:, t * P:t * P + P], w, x, start=n == 0, stop=n == len(terms) - 1)
                    last.then_inc(o_mm, 1)
                rstd_products(gm[:, 0], T, 0)
            pe.wait_ge(gfull, 8)
            pe.wait_ge(o_put, 24)
            project("out0", act_hi, act_lo, T, act_ready, READY["gla"])
            pe.wait_ge(evac, segs["out1"][0])
            pe.wait_ge(r_nbd, 2)
            pe.wait_ge(r_ald, 2)
            for d in range(2):
                for c in range(6):
                    pe.transpose(bank(6)[:, (6 * d + c) * 32:(6 * d + c) * 32 + 32], r_nb[:, d, c * P:c * P + P], ident[0:32, 0:32])
            for d in range(2):
                for c in range(2):
                    last = pe.transpose(bank(7)[:, (2 * d + c) * 32:(2 * d + c) * 32 + 32], r_al[:, d, c * P:c * P + P], ident[0:32, 0:32])
            last.then_inc(ct_mm, 1)

            def group_products(g):
                pe.wait_ge(bc_in, 32 * (g + 1))
                pe.wait_ge(ct_put, 2)
                if g:
                    pe.wait_ge(xt_put, 4 * g)
                    pe.wait_ge(ss_put, 4 * g)
                for i in range(6):
                    if 6 * g + i >= 2:
                        pe.wait_ge(cb_put, 6 * g + i - 1)
                    B, C, out = bct[:, 0], bct[:, 1], bank(6 + i % 2)
                    if i < 4:
                        last = pe.matmul(out[:], B[:, i * P:i * P + P], C[:, 0:LAT], start=True, stop=True)
                    elif i == 4:
                        for c in range(2):
                            last = pe.matmul(out[:, c * CTX:c * CTX + CTX], B[:, LAT + c * P:LAT + c * P + P], C[:, LAT:T],
                                             start=True, stop=True)
                    else:
                        for c in range(2):
                            last = pe.transpose(out[:, c * P:c * P + P], B[:, LAT + c * P:LAT + c * P + P], ident[:])
                    last.then_inc(cb_mm, 1)

            def x_transposes(p):
                pe.wait_ge(xt_in, 32 * (p + 1))
                if p % 4 == 0:
                    pe.wait_ge(cb_put, 6 * (p // 4 + 1))
                if p:
                    pe.wait_ge(ss_put, p)
                for c in range(6):
                    last = pe.transpose(slot(3)[:, c * P:c * P + P], xt[:, p % 2, c * P:c * P + P], ident[:])
                last.then_inc(xt_tr, 1)

            def states(p):
                pe.wait_ge(xal_done, 2 * p + 2)
                pe.wait_ge(xt_put, p + 1)
                for c in range(2):
                    last = pe.matmul(bank(6)[:, 0:2 * P], Btok[:, c], xal[:, p % 2, c].rearrange("t d f -> t (d f)"),
                                     start=c == 0, stop=c == 1)
                last.then_inc(s_mm, 1)

            def rows(h):
                for d in range(2):
                    if h:
                        pe.wait_ge(rows_read, 2 * h - 1 + d)
                    for c0, c1 in ((0, 512), (512, 768)):
                        r = 16 * d + h
                        last = pe.matmul(slot(d)[:, c0:c1], ident[0:32, r:r + 1].broadcast_to([32, P]), Grow[:, d, c0:c1],
                                         start=True, stop=True)
                    last.then_inc(rows_mm, 1)

            def head_products(h):
                p, f = h // 2, h % 2 * 64
                pe.wait_ge(m_done, h + 1)
                pe.wait_ge(cbeta_done, h + 1)
                pe.wait_ge(xt_put, p + 1)
                pe.wait_ge(ss_put, p + 1)
                if p and h % 2 == 0:
                    pe.wait_ge(y_put, p)
                y, d = slot(2)[f:f + 64], Dm[:, h % 2]
                for c in range(4):
                    pe.matmul(y[:, 0:LAT], xtok[:, p % 2, c, f:f + 64], d[:, c * LAT:c * LAT + LAT], start=c == 0, stop=False)
                for k in range(2):
                    pe.matmul(y[:, 0:LAT], ssS[:, p % 2, k, f:f + 64], Cb[:, h % 2, k], start=False, stop=k == 1)
                for c in range(2):
                    last = pe.matmul(y[:, LAT:T], xtok[:, p % 2, 4 + c, f:f + 64], d[:, DC + c * CTX:DC + c * CTX + CTX],
                                     start=c == 0, stop=c == 1)
                last.then_inc(y_mm, 1)

            group_products(0)
            x_transposes(0)
            states(0)
            rows(0)
            for h in range(SSD_HEADS):
                if h + 1 < SSD_HEADS:
                    rows(h + 1)
                    if h % 2 and h + 1 != 8:
                        x_transposes(h // 2 + 1)
                head_products(h)
                if h + 1 == 8:
                    group_products(1)
                    x_transposes(4)
                if h % 2 and h + 1 < SSD_HEADS:
                    states(h // 2 + 1)
            for g in range(2):
                rstd_products(snacc[g], T, 2 + g)
            project("out1", act_hi, act_lo, T, act_ready, READY["ssd"])
            def norm_products(name, n):
                pe.wait_ge(evac, segs[{"ffn0": "up00", "mix1": "xm", "ffn1": "up10"}.get(name, "end")][0])
                rstd_products(nacc, n, 0)
                pe.wait_ge(nt_done, KD * (NORMS.index(name) + 1))

            def ffn(layer, n):
                for g in range(3):
                    project(f"up{layer}{g}", act_hi, act_lo, n, act_ready, READY[f"ffn{layer}"])
                    project(f"down{layer}{g}", hid_hi, hid_lo, n, hid_ready, FF_BEFORE[f"{layer}{g}"])

            norm_products("ffn0", T)
            ffn(0, T)
            pe.wait_ge(evac, segs["xm"][0])
            pe.wait_ge(wif_in, 96)

            def block_transposes(t):
                pe.wait_ge(bd_done, t + 1)
                for m in range(3):
                    last = pe.transpose(bank(t % 2)[:, m * P:m * P + P], bd[:, t % 2, m], ident[:])
                last.then_inc(bdt_mm, 1)

            block_transposes(0)
            for t in range(16):
                if t + 1 < 16:
                    if t >= 1:
                        pe.wait_ge(bdt_put, t)
                    block_transposes(t + 1)
                pe.wait_ge(bdt_put, t + 1)
                b = bdT[:, t % 2]
                pe.matmul(bank(4 + t // 4)[:, t % 4 * P:t % 4 * P + P], b[:, 0], b[:, 1], start=True, stop=True)
                gates = bank(2).rearrange("p (x t g) -> p x t g", x=2, t=16)
                for m, x in ((0, 0), (1, 0), (2, 1)):
                    last = pe.matmul(gates[:, x, t], b[:, m], wif[:, m, t].rearrange("p d g -> p (d g)"), start=m != 1, stop=m != 0)
                last.then_inc(wa_mm, 1)
            norm_products("mix1", T)
            project("xm", act_hi, act_lo, T, act_ready, READY["mix1"])
            pe.wait_ge(evac, segs["zm"][0])
            n0 = segs["zm"][0]
            for j in range(8):
                project_unit("zm", (n0 + j) // RING, j % RING, KD, act_hi, act_lo, LAT, act_ready, READY["mix1"])
                for t in (2 * j, 2 * j + 1):
                    pe.wait_ge(gx_in[t % RING], GX_IN0 + 32 * (t // RING + 1))
                    for x in range(2):
                        for b, c0, c1 in ((1, 0, 512), (3, 512, 768)):
                            last = pe.matmul(bank(b)[0:40, 0:c1 - c0], wG[:, x, t], gx[:, t % RING, x, c0:c1],
                                             start=t == 0 and x == 0, stop=t == 15 and x == 1)
                    last.then_inc(gx_mm, 1)
            each_ring(pe, n0 + 8, 8, lambda r, s: project_unit("zm", r, s, KD, act_hi, act_lo, LAT, act_ready, READY["mix1"]))
            pe.wait_ge(gm_done, 1)
            pe.wait_ge(ge_done, 2)
            pe.wait_ge(evac, segs["mout0"][0])
            for d in range(2):
                for c in range(6):
                    at = (6 * d + c) * 8
                    pe.transpose(bank(0)[:, at:at + 8], mr_u[:, d, c * P:c * P + P], ident[0:8, 0:8])
                for c in range(4):
                    at = 96 + (4 * d + c) * 8
                    last = pe.transpose(bank(0)[:, at:at + 8], mr_m[:, d, c * P:c * P + P], ident[0:8, 0:8])
            last.then_inc(gc_mm, 1)

            def query_value(h):
                f = 12 * h
                pe.wait_ge(xch_in, XCH_IN0 + 16 * (h + 1))
                for t in range(4):
                    if f >= 2:
                        pe.wait_ge(qv_put, QV_PUT0 + f - 1)
                    pe.matmul(bank(2 + f % 2), wA[:, 4 * h + t], xch[:, t, 0:LAT], start=True, stop=True).then_inc(qv_mm, 1)
                    f += 1
                for t in range(4):
                    g = 4 * h + t
                    pe.wait_ge(xmr_in[g % 2], XMR_IN0 + 16 * (g // 2 + 1))
                    pe.wait_ge(bdv_done, g + 1)
                    for c0, c1 in ((0, 4), (4, 6)):
                        pe.wait_ge(qv_put, QV_PUT0 + f - 1)
                        for c in range(c0, c1):
                            last = pe.matmul(bank(2 + f % 2)[:, (c - c0) * P:(c - c0) * P + P], xmr[:, g % 2, c * P:c * P + P], bdv[:, t],
                                             start=True, stop=True)
                        last.then_inc(qv_mm, 1)
                        f += 1

            def stabiliser_rows(h):
                if h == 0:
                    pe.wait_ge(gc_put, 2)
                for d in range(2):
                    r = 4 * d + h
                    if h:
                        pe.wait_ge(pn_done, PN_DONE0 + 2 * h)
                    pe.matmul(bank(d), ident[0:8, r:r + 1].broadcast_to([8, P]), negM[:, d], start=True, stop=True).then_inc(mrows_mm, 1)

            pe.wait_ge(wa_put, 12)
            query_value(0)
            stabiliser_rows(0)
            for h in range(ML_HEADS):
                pe.wait_ge(qv_put, QV_PUT0 + 12 * h + 4)
                for i, c in enumerate(KEYS):
                    if 6 * h + i >= 2:
                        pe.wait_ge(s6_put, S6_PUT0 + 6 * h + i - 1)
                    for t in range(4):
                        last = pe.matmul(bank(4 + i % 2), xch[:, t, c * P:c * P + P], qp[:, t], start=t == 0, stop=t == 3)
                    last.then_inc(s6_mm, 1)
                pe.wait_ge(den_rdy, DEN_RDY0 + h + 1)
                for d in range(2):
                    for c in range(4):
                        last = pe.matmul(bank(0)[:, 4 * d + c:4 * d + c + 1], mtmp[:, 1 + d, c * P:c * P + P], ones[:, 0:1], start=True, stop=True)
                last.then_inc(den_mm, 1)
                pe.wait_ge(rd_rdy, RD_RDY0 + h + 1)
                if h == 2:
                    project("mout0", act1_hi, act1_lo, LAT, act_ready, READY["ml0"])
                    pe.wait_ge(evac, segs["mout1"][0])
                pe.matmul(bank(0), ones[:], rdiag[:, 0:LAT], start=True, stop=True)
                pe.matmul(bank(1), ones[:], mtmp[:, 0], start=True, stop=True).then_inc(rfb_mm, 1)
                pe.wait_ge(qv_put, QV_PUT0 + 12 * h + 12)
                if h:
                    pe.wait_ge(fin_done, FIN_DONE0 + 4 * h)
                for t in range(4):
                    f = 4 * h + t
                    if t >= 2:
                        pe.wait_ge(h_put, H_PUT0 + f - 1)
                    for i, c in enumerate(KEYS):
                        if t == 0 and i in (0, 2):
                            pe.wait_ge(pn_done, PN_DONE0 + 2 * h + (1 if i == 0 else 2))
                        last = pe.matmul(bank(6 + t % 2), vt[:, c, t * P:t * P + P], Wf[:, c], start=i == 0, stop=i == 5)
                    last.then_inc(h_mm, 1)
                if h + 1 < ML_HEADS:
                    stabiliser_rows(h + 1)
                    query_value(h + 1)
                pe.wait_ge(hs_rdy, HS_RDY0 + h + 1)
                pe.matmul(bank(7), ones[:], mtmp[:, 1], start=True, stop=True).then_inc(mean_mm, 1)
                rstd_products(mtmp[:, 1], LAT, 3)
            project("mout1", act1_hi, act1_lo, LAT, act_ready, READY["ml1"])
            norm_products("ffn1", LAT)
            ffn(1, LAT)
            pe.wait_ge(evac, segs["end"][0])
            rstd_products(nacc, LAT, 0)
            for t in range(4):
                for half in range(2):
                    i = 2 * t + half
                    pe.wait_ge(fin_ready, 4 * half + 4)
                    if i >= 2:
                        pe.wait_ge(out_put, i - 1)
                    for q in range(4):
                        last = pe.transpose(bank(2 + i % 2)[:, q * P:q * P + P], fin[:, 4 * half + q, t * P:t * P + P], ident[:])
                    last.then_inc(out_tr, 1)

        @block.scalar
        def _(act):
            chain = Chain(act, act_own)
            act.wait_ge(tab_put, 1)
            act.activation(cs[:, :, 0], par("c", 0, KD), ACT.Silu).then_inc(c_silu, 1)
            act.activation(cs[:, :, 1], par("c_ctx", 0, KD), ACT.Silu).then_inc(c_silu, 1)

            rstds = [0]

            def root(n, features, where):
                act.wait_ge(sum_mm, rstds[0] + 1)
                act.activation(rcol[:, 0:n // P], slot(where)[:, 0:n // P], ACT.Sqrt, scale=1.0 / features,
                               bias=eps_col[:]).then_inc(std_done, 1)
                rstds[0] += 1

            def squares(name, n):
                g = NORMS.index(name)
                for k in range(KD):
                    if k >= 3:
                        act.wait_ge(nsum_step, (KD - 1) * g + k - 2)
                    dst = nacc[:, 0:n] if k == 0 else nsq[:, k % 2, 0:n]
                    act.activation(dst, xT[:, k, 0:n], ACT.Square).then_inc(sq_done, 1)

            def norm(name, n, layer, which, permute=False):
                g = NORMS.index(name)
                squares(name, n)
                root(n, D, 0)
                for k in range(KD):
                    act.wait_ge(nt_done, g * KD + k + 1)
                    if k >= 2:
                        act.wait_ge(act_ready, READY[name] + k - 1)
                    parts = [(0, LAT, 0)] + [(LAT, n, 1)] * (n > LAT)
                    for c0, c1, col in parts:
                        src, dst = nt[:, k % 2, c0:c1], nh[:, k % 2, c0:c1]
                        if permute and col == 0:
                            src = src.rearrange("p (r c) -> p r c", c=GRID_W)
                            dst = dst.rearrange("p (c r) -> p r c", r=GRID_H)
                        chain(act.activation(dst, src, ACT.Identity, scale=mscale[:, layer, which, k, col:col + 1],
                                             bias=modv[:, mod(layer, 3 * which, k), col:col + 1]), nh_done)
                    act.activation(act_hi[:, k, 0:n], nh[:, k % 2, 0:n], ACT.Copy).then_inc(nhi_done, 1)

            for u in range(4):
                act.wait_ge(mod_mm, u + 1)
                act.activation(mrow[:, 512 * u:512 * u + 512], bank(3 + u)[0:2], ACT.Copy).then_inc(mrow_put, 1)
            act.wait_ge(mod_put, 1)
            act.wait_ge(x_put, 12)
            norm("mix0", T, 0, 0)

            win = a["a_w_in"][0].rearrange("(k p) m -> p k m", p=P)
            act.wait_ge(act_ready, READY["mix0"] + KD)
            act.dma_start(rd_raw[:, :, 0:64], win[:, :, COL_R:COL_R + 64]).then_inc(rd_in, 16)
            act.dma_start(rd_raw[:, :, 64:128], win[:, :, COL_DT - 32:COL_DT + 32]).then_inc(rd_in, 16)

            def to_stage(r, s, func, tile0):
                act.wait_ge(mm_done, r * RING + (s + 1))
                if not (isinstance(r, int) and r == 0):
                    act.wait_ge(st_out[s], r * 16)
                act.activation(stage[:, s], slot(s), func).then_inc(evac, 1)
                act.wait_ge(evac, r * RING + (s + 1))
                act.dma_start(proj0[bass.ds(r * RING + (s + tile0), 1)].rearrange("a p t -> p (a t)"), stage[:, s]).then_inc(st_out[s], 16)

            each_ring(act, segs["qkv"][0], 16, lambda r, s: to_stage(r, s, ACT.Copy, 0))
            each_ring(act, segs["g"][0], 16, lambda r, s: to_stage(r, s, ACT.Silu, 0))

            def conv_unit(r, s):
                j = r * RING + (s - 32)
                act.wait_ge(mm_done, r * RING + (s + 1))
                if s >= 2:
                    act.wait_ge(conv_step, (j - 1) * 5)
                else:
                    act.wait_ge(silu_done, j)
                act.activation(cpre[:, s % 2], slot(s), ACT.Copy).then_inc(evac, 1)
                act.wait_ge(st_out[s], r * 16)
                act.wait_ge(conv_step, (j + 1) * 5)
                act.activation(stage[:, s], cpost[:, s % 2], ACT.Silu).then_inc(silu_done, 1)
                act.wait_ge(silu_done, j + 1)
                act.dma_start(proj0[bass.ds(r * RING + s, 1)].rearrange("a p t -> p (a t)"), stage[:, s]).then_inc(st_out[s], 16)

            each_ring(act, segs["xbc"][0], 12, conv_unit)
            act.wait_ge(rd_mm, 1)
            act.activation(rT[:], slot(0)[0:32], ACT.Copy).then_inc(rd_put, 1)
            act.activation(dtT[:], slot(0)[96:128], ACT.Copy).then_inc(rd_put, 1)
            for s in range(RING):
                act.wait_ge(st_out[s], 16 * 11)
            act.wait_ge(m_put, MOD_UNITS - RING)
            act.wait_ge(conv_step, 60)

            def load_head(h):
                for t, tile in enumerate((Q0 + h, K0 + h, V0 + 2 * h, V0 + 2 * h + 1)):
                    act.dma_start(hq[:, t], proj0[tile]).then_inc(hq_in, 16)
                for d in range(2):
                    act.dma_start(wg[16 * d:16 * d + 16, d, :], a["a_gla_w_gate"][0, d, :, h * P:h * P + P]).then_inc(hq_in, 16)

            act.wait_ge(wg_zero, 2)
            load_head(0)
            for h in range(GLA_HEADS):
                for d in range(2):
                    act.wait_ge(gate_mm, 2 * h + d + 1)
                    chain(act.activation(ga[:, d], slot(d), ACT.Abs, bias=par("gla_b", 4 * d + h)), abs_done)
                for d in range(2):
                    chain(act.activation(ga[:, d], ga[:, d], ACT.Exp, scale=-1.0))
                for d in range(2):
                    chain(act.activation(ga[:, d], ga[:, d], ACT.Ln, bias=one_col[:]), ln_done)
                for i in range(3):
                    act.wait_ge(tr_done, 6 * h + i + 1)
                    act.activation(vtok[:, 2 * i:2 * i + 2, :].rearrange("p c v -> p (c v)"), bank(i % 2), ACT.Copy).then_inc(tr_put, 1)
                for d in range(2):
                    act.wait_ge(g_ready, 2 * h + d + 1)
                    chain(act.activation(ga[:, d], gG[:, d], ACT.Exp, scale=1.0 / GLA_TAU), e0_done)
                for d in range(2):
                    act.wait_ge(qd_done, 2 * h + d + 1)
                    act.wait_ge(x_ready, 2 * h + d + 1)
                    near, far = (1 - d) * SUB, d * SUB
                    chain(act.activation(ga[:, d], gm[:, d], ACT.Exp, scale=1.0 / GLA_TAU), e1_done)
                    x, G = (y[:, d].rearrange("p (c t) -> p c t", t=P) for y in (gm, gG))
                    chain(act.activation(x[:, :, near:near + SUB], x[:, :, near:near + SUB], ACT.Exp, scale=-1.0 / GLA_TAU))
                    chain(act.activation(x[:, :, far:far + SUB], G[:, :, far:far + SUB], ACT.Exp, scale=-1.0 / GLA_TAU), e3_done)
                for d in range(2):
                    act.wait_ge(y_ready, 2 * h + d + 1)
                    chain(act.activation(ga[:, d], ga[:, d], ACT.Exp, scale=1.0 / GLA_TAU), e4_done)
                for i in range(3):
                    act.wait_ge(tr_done, 6 * h + i + 4)
                    n = min(4, 10 - 4 * i)
                    act.activation(kdT[:, 4 * i:4 * i + n, :].rearrange("p e t -> p (e t)"), bank((3 + i) % 2, n * P),
                                   ACT.Copy).then_inc(tr_put, 1)
                for t in range(2):
                    act.dma_start(ga[:, t], proj0[G0 + 2 * h + t]).then_inc(g_in, 16)
                if h + 1 < GLA_HEADS:
                    load_head(h + 1)
                for i, c in enumerate(CHUNKS[0]):
                    act.wait_ge(o_mm, 6 * h + i + 1)
                    act.activation(oT[:, :, c * P:c * P + P], bank(6 + i % 2, 2 * P).rearrange("p (v t) -> p v t", v=2),
                                   ACT.Copy).then_inc(o_put, 1)
                act.wait_ge(o_put, 6 * h + 6)
                for t in range(2):
                    act.activation(gm[:, t], oT[:, t], ACT.Square).then_inc(gsq_done, 1)
                root(T, 2 * P, 0)
                for t in range(2):
                    act.wait_ge(gfull, 2 * h + t + 1)
                    act.activation(act_hi[:, 2 * h + t], oT[:, t], ACT.Copy).then_inc(nhi_done, 1)
            act.wait_ge(act_ready, READY["gla"] + KD)
            act.wait_ge(o_mm, 24)
            act.dma_start(rowc[:, 0:1], a["a_ssd_dt_bias"][0].rearrange("d (h o) -> (d h) o", o=1)).then_inc(row_in, 16)
            act.dma_start(rowc[:, 1:2], a["a_ssd_A_log"][0].rearrange("d (h o) -> (d h) o", o=1)).then_inc(row_in, 16)
            for f in range(2):
                src = a["a_ssd_D"][0]
                act.dma_start(dcol[64 * f:64 * f + 64, :], bass.AP(tensor=src.tensor, offset=src.offset + f, ap=[[0, 64], [2, PAIRS]]),
                              allow_slow_non_contiguous=True).then_inc(row_in, 16)
            act.wait_ge(row_in, 64)
            chain(act.activation(r_ab[:], dtT[:], ACT.Abs, bias=rowc[:, 0:1]))
            chain(act.activation(r_e[:], r_ab[:], ACT.Exp, scale=-1.0), r_ez)
            chain(act.activation(rowc[:, 2:3], rowc[:, 1:2], ACT.Exp), r_ez)

            def load_group(g):
                for k, tile in enumerate((B0 + g, C0 + g)):
                    act.dma_start(bct[:, k], proj0[tile]).then_inc(bc_in, 16)

            def load_pair(p):
                act.dma_start(xt[:, p % 2], proj0[X0 + p]).then_inc(xt_in, 16)
                act.dma_start(sz[:, p % 2], proj0[Z0 + p]).then_inc(xt_in, 16)

            load_group(0)
            act.wait_ge(r_dt, 1)
            chain(act.activation(r_ln[:], r_ab[:], ACT.Ln), r_lnd)
            for d in range(2):
                act.wait_ge(r_nbd, d + 1)
                end = T - 1 if d == 0 else LAT
                chain(act.activation(r_al[:, d], r_nb[:, d, LAT:T], ACT.Exp, bias=Grow[:, d, end:end + 1]), r_ald)
            act.wait_ge(ct_mm, 1)
            chain(act.activation(nb[:].rearrange("p d c r -> p (d c r)"), bank(6, 384), ACT.Copy), ct_put)
            chain(act.activation(al[:].rearrange("p d c r -> p (d c r)"), bank(7, 128), ACT.Copy), ct_put)
            load_pair(0)

            def group_copies(g):
                if g:
                    act.wait_ge(m_done, 8 * g)
                    act.wait_ge(s_mm, 4 * g)
                for i in range(6):
                    act.wait_ge(cb_mm, 6 * g + i + 1)
                    src = bank(6 + i % 2, 512 if i < 5 else 256)
                    dst = cb[:, i * LAT:i * LAT + LAT] if i < 5 else Btok[:].rearrange("p c n -> p (c n)")
                    act.activation(dst, src, ACT.Copy).then_inc(cb_put, 1)

            def x_copies(p):
                act.wait_ge(xt_tr, p + 1)
                act.activation(xtok[:, p % 2].rearrange("p c f -> p (c f)"), slot(3), ACT.Copy).then_inc(xt_put, 1)

            def decays(h):
                D = Dm[:, h % 2]
                if h >= 2:
                    act.wait_ge(y_mm, h - 1)
                for d in range(2):
                    act.wait_ge(e_done, 2 * h + d + 1)
                    row, r = slot(d), 16 * d + h
                    todo = []
                    for c in range(6):
                        lo, hi, off = (0, 4, DL + c * LAT) if c < 4 else (4, 6, DC + (c - 4) * CTX)
                        if d == 0 and c + 1 < hi:
                            todo.append((off + (c + 1 - lo) * P, c + 1, hi, c))
                        elif d == 1 and c > lo:
                            todo.append((off, lo, c, c))
                    for off, i0, i1, c in todo:
                        act.activation(D[:, off:off + (i1 - i0) * P], row[:, i0 * P:i1 * P], ACT.Exp, bias=nb[:, d, c, r:r + 1])
                    act.activation(Cb[:, h % 2, d], row[:, 0:LAT], ACT.Exp).then_inc(rows_read, 1)
                act.wait_ge(mask_done, 3 * h + 3)
                for k, (off, n, step) in enumerate(((DL, 4, LAT + P), (DC, 2, CTX + P), (DB, 6, P))):
                    blocks = diagonals(D, off, n, step)
                    act.activation(blocks, blocks, ACT.Exp).then_inc(exp_done, 1)

            def square(p):
                act.wait_ge(y_done, p + 1)
                dst = snacc[p // 4][:] if p % 4 == 0 else ssq[:, p % 2]
                if p >= 3:
                    act.wait_ge(ysum, (p - 2) - (p - 2) // 4)
                act.activation(dst, yT[:, p], ACT.Square).then_inc(ysq_done, 1)

            act.wait_ge(mm_done, segs["out1"][0])
            group_copies(0)
            x_copies(0)
            for h in range(SSD_HEADS):
                decays(h)
                if h % 2 == 0 and h // 2 + 1 < PAIRS:
                    if h >= 2:
                        act.wait_ge(y_done, h // 2)
                        act.wait_ge(xt_tr, h // 2)
                    load_pair(h // 2 + 1)
                if h + 1 == 8:
                    act.wait_ge(cbeta_done, 8)
                    load_group(1)
                    group_copies(1)
                if h % 2 and h + 1 < SSD_HEADS:
                    x_copies(h // 2 + 1)
                if h % 2 and h >= 3:
                    square((h - 3) // 2)
            square(7)
            for g in range(2):
                root(T, 4 * P, 2 + g)
                for t in range(4 * g, 4 * g + 4):
                    act.wait_ge(yn_done, t + 1)
                    act.activation(act_hi[:, t], yT[:, t], ACT.Copy).then_inc(nhi_done, 1)
            def hidden(layer, n):
                for g in range(3):
                    n0, count = segs[f"up{layer}{g}"][:2]

                    def body(r, s):
                        if s % 2:
                            return
                        t, u = r * 2 + (s // 2 - n0 // 2), r * RING + s
                        act.wait_ge(mm_done, u + 1)
                        act.wait_ge(evac, u - 2)
                        act.activation(fsg[:, s // 2, 0:n], slot(s)[:, 0:n], ACT.Silu).then_inc(fsg_done, 1)
                        act.wait_ge(evac, u + 2)
                        dst = hid_hi[:, bass.ds(t, 1), 0:n].rearrange("p a t -> p (a t)")
                        act.activation(dst, fhp[:, s // 2, 0:n], ACT.Copy).then_inc(fhh_done, 1)

                    each_ring(act, n0, count, body)

            act.wait_ge(evac, segs["up00"][0])
            norm("ffn0", T, 0, 1)
            act.wait_ge(act_ready, READY["ffn0"] + KD)
            hidden(0, T)
            for m, w in enumerate(("b_wq", "b_wk", "b_wv")):
                act.dma_start(w4[:, m], a[w][0].rearrange("n d e -> (n d) e").rearrange("(t p) e -> p t e", p=P)).then_inc(wb_in, 16)
            for d in range(2):
                for m in range(3):
                    act.dma_start(wif[:, m, :, d, :], a["b_w_if"][0, d, 16 * P * m:16 * P * (m + 1), :].rearrange("(t p) g -> p t g", p=P)).then_inc(wif_in, 16)
            for d in range(2):
                for k in range(2):
                    act.dma_start(bif[4 * d:4 * d + 4, k:k + 1], a["b_b_if"][0, d, 4 * k:4 * k + 4].unsqueeze(1)).then_inc(wb_in, 16)
            for t in range(16):
                act.wait_ge(bdt_mm, t + 1)
                if t >= 2:
                    act.wait_ge(wa_mm, t - 1)
                act.activation(bdT[:, t % 2].rearrange("p m e -> p (m e)"), bank(t % 2, 384), ACT.Copy).then_inc(bdt_put, 1)
            norm("mix1", T, 1, 0, permute=True)

            def xm_unit(first):
                def body(r, s):
                    j = r * RING + (s - segs["xm"][0])
                    act.wait_ge(mm_done, r * RING + (s + 1))
                    if not first:
                        act.wait_ge(xm_out[s], XM_OUT0 + (r - segs["xm"][0] // RING) * 16)
                        act.wait_ge(conv_step, (j - 3 + 12) * 5)
                    act.activation(xms[:, s], slot(s), ACT.Copy).then_inc(evac, 1)
                    act.wait_ge(evac, r * RING + (s + 1))
                    act.dma_start(xm_d[bass.ds(j, 1)].rearrange("a p t -> p (a t)"), xms[:, s]).then_inc(xm_out[s], 16)
                    act.wait_ge(conv_step, (j + 1 + 12) * 5)
                    act.activation(xcr[:, s], xcr[:, s], ACT.Silu).then_inc(mxc_done, 1)
                    act.wait_ge(mxc_done, j + 1)
                    act.dma_start(xc_d[bass.ds(j, 1)].rearrange("a p t -> p (a t)"), xcr[:, s]).then_inc(xc_out[s], 16)
                return body

            n0 = segs["xm"][0]
            each_ring(act, n0, RING, xm_unit(True))
            each_ring(act, n0 + RING, 16 - RING, xm_unit(False))

            def load_gates(t):
                if t >= RING:
                    act.wait_ge(gx_mm, t - RING + 1)
                act.dma_start(gx[:, t % RING, 0], xc_d[t]).then_inc(gx_in[t % RING], 16)
                act.dma_start(gx[:, t % RING, 1], xm_d[t]).then_inc(gx_in[t % RING], 16)

            def z_unit(j):
                r, s = segs["zm"][0] // RING + j // RING, j % RING
                act.wait_ge(mm_done, r * RING + s + 1)
                if j >= RING:
                    act.wait_ge(z_out[s], Z_OUT0 + 16 * (j // RING))
                act.activation(zst[:, s], slot(s)[:, 0:LAT], ACT.Silu).then_inc(evac, 1)
                act.wait_ge(evac, r * RING + s + 1)
                act.dma_start(z_d[j], zst[:, s]).then_inc(z_out[s], 16)

            for s in range(RING):
                act.wait_ge(xm_out[s], XM_OUT0 + 64)
                act.wait_ge(xc_out[s], XC_OUT0 + 64)
            for t in range(RING):
                load_gates(t)
            for j in range(8):
                z_unit(j)
                for t in (2 * j + 4, 2 * j + 5):
                    if t < 16:
                        load_gates(t)
            act.wait_ge(gx_mm, 16)
            for k, dst in ((0, mr_i), (1, mr_f)):
                for b, c0, c1 in ((1, 0, 512), (3, 512, 768)):
                    act.activation(dst[:, c0:c1], bank(b)[32 * k:32 * k + 8, 0:c1 - c0], ACT.Copy).then_inc(gr_put, 1)
            act.wait_ge(gr_put, 4)
            chain(act.activation(mr_ab[:], mr_f[:], ACT.Abs, bias=bif[:, 1:2]), gab_done)
            chain(act.activation(mr_ab[:], mr_ab[:], ACT.Exp, scale=-1.0))
            chain(act.activation(mr_ab[:], mr_ab[:], ACT.Ln, bias=one_col[0:8]), gln_done)
            for j in range(8, 16):
                z_unit(j)
            act.wait_ge(gm_done, 1)
            for d in range(2):
                chain(act.activation(mr_m[:, d], mr_m[:, d], ACT.Exp, scale=-1.0), ge_done)
            for s in range(RING):
                act.wait_ge(z_out[s], Z_OUT0 + 64)
            act.wait_ge(gc_mm, 1)
            chain(act.activation(ucol[:].rearrange("p d c r -> p (d c r)"), bank(0)[:, 0:96], ACT.Copy), gc_put)
            chain(act.activation(ecol[:].rearrange("p d c r -> p (d c r)"), bank(0)[:, 96:160], ACT.Copy), gc_put)

            def load_xc(h):
                act.dma_start(xch[:], xc_d[4 * h:4 * h + 4].rearrange("t p n -> p t n")).then_inc(xch_in, 16)

            def load_xm(g):
                act.dma_start(xmr[:, g % 2], xm_d[g]).then_inc(xmr_in[g % 2], 16)

            def qv_copies(h):
                f = 12 * h
                for t in range(4):
                    act.wait_ge(qv_mm, QV_MM0 + f + 1)
                    act.activation(qp[:, t], bank(2 + f % 2), ACT.Copy, scale=ML_DH ** -0.5).then_inc(qv_put, 1)
                    f += 1
                for t in range(4):
                    g = 4 * h + t
                    for c0, c1 in ((0, 4), (4, 6)):
                        act.wait_ge(qv_mm, QV_MM0 + f + 1)
                        act.activation(vt[:, c0:c1, t * P:t * P + P], bank(2 + f % 2, (c1 - c0) * P).rearrange("p (c e) -> p c e", e=P),
                                       ACT.Copy).then_inc(qv_put, 1)
                        f += 1
                    if g + 2 < 16 and not (t >= 2 and h + 1 < ML_HEADS and False):
                        load_xm(g + 2)

            def weights(h):
                for d in range(2):
                    act.wait_ge(de_done, DE_DONE0 + 2 * h + d + 1)
                    r, W = 4 * d + h, (Wf, Wb)[d]
                    for c in range(6):
                        i0, i1 = (0, 4) if c >= 4 else (c + 1, 4) if d == 0 else (0, c)
                        if i0 < i1:
                            last = act.activation(W[:, c, i0 * P:i1 * P], bank(d)[:, i0 * P:i1 * P], ACT.Exp, bias=ucol[:, d, c, r:r + 1])
                    last.then_inc(wr_done, 1)
                for d in range(2):
                    act.wait_ge(mk_done, 2 * h + d + 1)
                    blocks = diagonals((Wf, Wb)[d][:].rearrange("p c t -> p (c t)"), 0, 4, LAT + P)
                    act.activation(blocks, blocks, ACT.Exp).then_inc(we_done, 1)

            load_xc(0)
            load_xm(0)
            load_xm(1)
            qv_copies(0)
            weights(0)

            def load_output(h, t):
                g = 4 * h + t
                act.dma_start(zs[:, t % 2], z_d[g]).then_inc(z_in[t % 2], 16)

            for h in range(ML_HEADS):
                for t in range(4):
                    act.dma_start(xs(t), halves(xc_d[4 * h + t][:, 0:LAT])).then_inc(xs_in[t], 16)
                for t in range(2):
                    load_output(h, t)
                if h + 1 < ML_HEADS:
                    act.wait_ge(s6_mm, S6_MM0 + 6 * h + 6)
                    load_xc(h + 1)
                for t in range(4):
                    act.wait_ge(h_mm, H_MM0 + 4 * h + t + 1)
                    act.activation(hh[:, t], bank(6 + t % 2), ACT.Copy).then_inc(h_put, 1)
                if h + 1 < ML_HEADS:
                    weights(h + 1)
                    qv_copies(h + 1)
                for t in range(4):
                    act.wait_ge(hc_done, HC_DONE0 + 4 * h + t + 1)
                    if t == 3:
                        act.wait_ge(hsum, HSUM0 + 3 * h + 1)
                    dst = mtmp[:, (1, 0, 2, 0)[t]]
                    act.activation(dst, hh[:, t], ACT.Square).then_inc(hsq_done, 1)
                root(LAT, 4 * P, 3)
                for t in range(4):
                    act.wait_ge(fin_done, FIN_DONE0 + 4 * h + t + 1)
                    if h == 2 and t == 0:
                        act.wait_ge(mm_done, segs["mout1"][0])
                    act.activation(act1_hi[:, 4 * (h % 2) + t], hh[:, t], ACT.Copy).then_inc(nhi_done, 1)
                    if t < 2:
                        load_output(h, t + 2)
            act.wait_ge(evac, segs["up10"][0])
            norm("ffn1", LAT, 1, 1)
            act.wait_ge(act_ready, READY["ffn1"] + KD)
            hidden(1, LAT)
            act.wait_ge(evac, segs["end"][0])
            squares("final", LAT)
            root(LAT, D, 0)
            for i in range(8):
                t, half = i // 2, i % 2
                act.wait_ge(out_tr, i + 1)
                if t >= 2:
                    act.wait_ge(out_st[t % 2], 16)
                act.activation(obuf[:, t % 2, 512 * half:512 * half + 512], bank(2 + i % 2), ACT.Copy).then_inc(out_put, 1)
                if half:
                    act.wait_ge(out_put, i + 1)
                    act.dma_start(out[0, t * P:t * P + P, :], obuf[:, t % 2]).then_inc(out_st[t % 2], 16)
            act.wait_ge(out_st[0], 32)
            act.wait_ge(out_st[1], 32)
        @block.vector
        def _(dve):
            chain = Chain(dve, dve_own)
            dve.wait_ge(tab_tr, 3)
            for t in range(3):
                dve.tensor_copy(ptab[:, t, 0:TABLE_LEN[t]], bank(0)[:, t * P:t * P + TABLE_LEN[t]]).then_inc(dve_own, 1)
            dve.wait_ge(dve_own, 3)
            chain.n[dve_own] = 3
            dve.drain().then_inc(tab_put, 1)
            for i in range(12):
                tt, half = i // 2, i % 2
                dve.wait_ge(x_tr, i + 1)
                dve.tensor_copy(xT[:, 4 * half:4 * half + 4, tt * P:tt * P + P],
                                bank(1 + i % 2).rearrange("p (q t) -> p q t", q=4)).then_inc(x_put, 1)
            def scales(layer, which):
                m = mod(layer, 3 * which + 1, 0)
                w = par("norm_ffn" if which else "norm_mix", layer * KD, KD)
                chain(dve.scalar_tensor_tensor(mscale[:, layer, which], modv[:, m:m + KD, :], 1.0,
                                               w.unsqueeze(2).broadcast_to([P, KD, 2]), ALU.add, ALU.mult))

            dve.wait_ge(mrow_tr, 1)
            chain(dve.tensor_tensor(modv[:, 0:16, :], bank(7)[:, 0:32].rearrange("p (m x) -> p m x", x=2),
                                    ptab[:, 0, 0:16].unsqueeze(2).broadcast_to([P, 16, 2]), ALU.add))
            scales(0, 0)
            dve.drain().then_inc(mod_put, 1)

            def mod_products(r, s):
                step0 = (r * RING + (s - RING)) * (2 * KD)
                if not (isinstance(r, int) and r == 1 and s < 2):
                    dve.wait_ge(mm_done, r * RING + (s - 1))
                dve.wait_ge(m_in[s], r * 16)
                for k in range(KD):
                    for v in range(2):
                        acc, c = m_acc[:, s % 2, v], cs[:, k, v:v + 1]
                        if k == 0:
                            ins = dve.tensor_scalar(acc, m_ring[:, s, k], c, None, ALU.mult)
                        else:
                            if k == 1 and v == 0:
                                dve.wait_ge(m_step, step0 + 2)
                            elif not (k == 1 and v == 1):
                                dve.wait_ge(m_step, step0 + 2 * k + v - 1)
                            ins = dve.scalar_tensor_tensor(acc, m_ring[:, s, k], c, acc, ALU.mult, ALU.add)
                        ins.then_inc(m_step, 1)

            def mod_unit(r, s):
                dve.wait_ge(mm_done, r * RING + (s + 1))
                m = r * (2 * RING) + (2 * s + 8)
                src = PS[:, mod_col(s):mod_col(s) + 4].rearrange("p (m x) -> p m x", x=2)
                dve.wait_ge(evac, r * RING + (s + 1))
                dve.tensor_tensor(modv[:, bass.ds(m, 2), :], src, ptab[:, 0, bass.ds(m, 2)].unsqueeze(2).broadcast_to([P, 2, 2]),
                                  ALU.add).then_inc(m_put, 1)

            rstds = [0]

            def rstd_diagonal(n):
                q = n // P
                rstds[0] += 1
                dve.wait_ge(std_done, rstds[0])
                chain(dve.reciprocal(rcol[:, 0:q], rcol[:, 0:q]))
                dve.tensor_tensor(rdiag[:, 0:n].rearrange("p (q t) -> p q t", t=P), ident[:].unsqueeze(1).broadcast_to([P, q, P]),
                                  rcol[:, 0:q].unsqueeze(2).broadcast_to([P, q, P]), ALU.mult).then_inc(diag_done, 1)

            def norm_sums(name, n):
                g = NORMS.index(name)
                for k in range(1, KD):
                    dve.wait_ge(sq_done, g * KD + k + 1)
                    chain(dve.tensor_tensor(nacc[:, 0:n], nacc[:, 0:n], nsq[:, k % 2, 0:n], ALU.add), nsum_step)
                dve.drain().then_inc(sum_done, 1)
                rstd_diagonal(n)
                dve.wait_ge(rstd_done, rstds[0])

            def norm(name, n):
                g = NORMS.index(name)
                norm_sums(name, n)

                def scaled(k):
                    if k >= 2:
                        dve.wait_ge(nh_done, nh_count(name, k - 1))
                    dve.tensor_tensor(nt[:, k % 2, 0:n], xT[:, k, 0:n], slot(0)[:, 0:n], ALU.mult).then_inc(nt_done, 1)

                scaled(0)
                for k in range(KD):
                    if k + 1 < KD:
                        scaled(k + 1)
                    dve.wait_ge(nhi_done, READY[name] + k + 1)
                    dve.tensor_tensor(act_lo[:, k, 0:n], nh[:, k % 2, 0:n], act_hi[:, k, 0:n].bitcast(F32),
                                      ALU.subtract).then_inc(act_ready, 1)
                dve.wait_ge(act_ready, READY[name] + KD)

            norm("mix0", T)

            def next_products(r, s):
                mod_products(*((r, s + 1) if s + 1 < RING else (r + 1, 0)))

            def mod_both(r, s):
                next_products(r, s)
                mod_unit(r, s)

            mod_products(1, 0)
            each_ring(dve, RING, 28, mod_both)

            def convolve(src, dst, w, bias, step0):
                def step(ins, k):
                    ins.then_inc(conv_step, 1)
                    dve.wait_ge(conv_step, step0 + k)

                step(dve.tensor_scalar(dst, src, w[1], bias, ALU.mult, ALU.add), 1)
                k = 2
                for c0, c1 in ((0, LAT), (LAT, T)):
                    for tap, d0, s0 in ((0, 1, 0), (2, 0, 1)):
                        m = c1 - c0 - 1
                        ins = dve.scalar_tensor_tensor(dst[:, c0 + d0:c0 + d0 + m], src[:, c0 + s0:c0 + s0 + m], w[tap],
                                                       dst[:, c0 + d0:c0 + d0 + m], ALU.mult, ALU.add)
                        step(ins, k)
                        k += 1

            def conv_unit(r, s):
                j = r * RING + (s - 32)
                dve.wait_ge(evac, r * RING + (s + 1))
                if s < 2:
                    dve.wait_ge(silu_done, j)
                else:
                    dve.wait_ge(silu_done, j - 1)
                convolve(cpre[:, s % 2], cpost[:, s % 2], [par_at("conv_w", j + 12 * t) for t in range(3)],
                         par_at("conv_b", j), j * 5)

            def conv_mod_unit(r, s):
                next_products(r, s)
                conv_unit(r, s)
                mod_unit(r, s)

            each_ring(dve, segs["xbc"][0], 8, conv_mod_unit)
            r = MOD_UNITS // RING - 1
            for s in range(RING):
                if s + 1 < RING:
                    next_products(r, s)
                conv_unit(r, s)
                mod_unit(r, s)
            for layer, which in ((0, 1), (1, 0), (1, 1)):
                dve.wait_ge(m_put, 40)
                scales(layer, which)
            dve.wait_ge(silu_done, 12)
            for s in range(RING):
                dve.wait_ge(st_out[s], 16 * 11)
            dve.memset(wg[:], 0.0).then_inc(wg_zero, 1)
            dve.memset(K2[:], 0.0).then_inc(wg_zero, 1)
            dve.wait_ge(wg_zero, 2)
            for h in range(GLA_HEADS):
                q, k = hq[:, 0], hq[:, 1]
                if h:
                    dve.wait_ge(o_put, 6 * h)
                    dve.wait_ge(act_ready, READY["gla"] + 2 * h)
                for d in range(2):
                    dve.wait_ge(gate_mm, 2 * h + d + 1)
                    dve.wait_ge(abs_done, 2 * h + d + 1)
                    chain(dve.tensor_scalar(gm[:, d], slot(d), par("gla_b", 4 * d + h), 0.0, ALU.add, ALU.min), min_done)
                for d in range(2):
                    dve.wait_ge(ln_done, 2 * h + d + 1)
                    chain(dve.tensor_tensor(gm[:, d], gm[:, d], ga[:, d], ALU.subtract))
                    for c in range(6):
                        src, dst = gm[:, d, c * P:c * P + P], gG[:, d, c * P:c * P + P]
                        if d:
                            src, dst = src[:, ::-1], dst[:, ::-1]
                        dve.tensor_tensor_scan(dst, ones[:], src, 0.0, ALU.mult, ALU.add).then_inc(dve_own, 1)
                    chain.n[dve_own] += 6
                    dve.wait_ge(dve_own, chain.n[dve_own])
                    dve.drain().then_inc(g_ready, 1)
                for d in range(2):
                    G = gG[:, d].rearrange("p (c t) -> p c t", t=P)
                    mid = SUB - 1 + d
                    chain(dve.tensor_tensor(gm[:, d].rearrange("p (c t) -> p c t", t=P), G[:, :, mid:mid + 1].broadcast_to([P, 6, P]), G,
                                            ALU.subtract), x_ready)
                dve.wait_ge(hq_in, 96 * (h + 1))
                for d in range(2):
                    dve.wait_ge(e0_done, 2 * h + d + 1)
                    chain(dve.scalar_tensor_tensor(qd[:, d], q, GLA_DK ** -0.5, ga[:, d], ALU.mult, ALU.mult))
                    end = 0 if d else P - 1
                    chain(dve.tensor_copy(etot[:, d, :].unsqueeze(2), ga[:, d].rearrange("p (c t) -> p c t", t=P)[:, :, end:end + 1]), qd_done)
                for d in range(2):
                    near, far = (1 - d) * SUB, d * SUB
                    e, x, G, k3, q3 = (y.rearrange("p (c t) -> p c t", t=P) for y in (ga[:, d], gm[:, d], gG[:, d], k, q))
                    dve.wait_ge(e1_done, 2 * h + d + 1)
                    chain(dve.tensor_tensor(K2[:, d, :, 1 - d].rearrange("p c a t -> p c (a t)"), k3, e, ALU.mult))
                    last = P - 1 if d == 0 else 0
                    chain(dve.tensor_tensor(e, G[:, :, last:last + 1].broadcast_to([P, 6, P]), G, ALU.subtract), y_ready)
                    dve.wait_ge(e3_done, 2 * h + d + 1)
                    chain(dve.scalar_tensor_tensor(qs[:, d], q3[:, :, near:near + SUB], GLA_DK ** -0.5, x[:, :, near:near + SUB],
                                                   ALU.mult, ALU.mult))
                    chain(dve.tensor_tensor(K2[:, d, :, d, d, :], k3[:, :, far:far + SUB], x[:, :, far:far + SUB], ALU.mult))
                for d in range(2):
                    dve.wait_ge(e4_done, 2 * h + d + 1)
                    chain(dve.tensor_tensor(ga[:, d], ga[:, d], k, ALU.mult), kd_done)

                def masked(i):
                    dve.wait_ge(sc_mm, 6 * h + i + 1)
                    both = gm[:, 1, i % 2 * 256:i % 2 * 256 + 256].rearrange("p (d t) -> p d t", d=2)
                    chain(dve.tensor_tensor(both, bank(2 + i % 2, 2 * P).rearrange("p (d t) -> p d t", d=2), tri[:], ALU.mult))
                    chain(dve.tensor_tensor(gm[:, 0, i * P:i * P + P], both[:, 0], both[:, 1], ALU.add), a_done)

                masked(0)
                for e, (d, c) in enumerate(KD_ORDER):
                    i = e // 2
                    dve.wait_ge(u_mm, 10 * h + e + 1)
                    U = bank(4 + d, 2 * P)
                    if i == 0:
                        chain(dve.tensor_copy(gS[:, d, 0], U), s_done)
                    else:
                        chain(dve.scalar_tensor_tensor(gS[:, d, i], gS[:, d, i - 1], etot[:, d, c:c + 1], U, ALU.mult, ALU.add), s_done)
                    if d:
                        masked(i + 1)
                dve.wait_ge(gsq_done, 2 * h + 2)
                chain(dve.tensor_tensor(gm[:, 0], gm[:, 0], gm[:, 1], ALU.add))
                dve.drain().then_inc(sum_done, 1)
                rstd_diagonal(T)
                dve.wait_ge(rstd_done, rstds[0])
                dve.wait_ge(g_in, 32 * (h + 1))
                for t in range(2):
                    chain(dve.scalar_tensor_tensor(oT[:, t], oT[:, t], par("gla_norm", t), slot(0), ALU.mult, ALU.mult))
                    chain(dve.tensor_tensor(oT[:, t], oT[:, t], ga[:, t], ALU.mult), gfull)
                for t in range(2):
                    dve.wait_ge(nhi_done, KD + 2 * h + t + 1)
                    dve.tensor_tensor(act_lo[:, 2 * h + t], oT[:, t], act_hi[:, 2 * h + t].bitcast(F32), ALU.subtract).then_inc(act_ready, 1)

            def residual(name, layer, which, n, permuted=False):
                def body(r, s):
                    m = r * RING + (s - segs[name][0])
                    dve.wait_ge(mm_done, r * RING + (s + 1))
                    parts = [(0, LAT, 0)] + [(LAT, T, 1)] * (n > LAT)
                    for c0, c1, v in parts:
                        x = xT[:, bass.ds(m, 1), c0:c1].rearrange("p a t -> p (a t)")
                        g = modv[:, bass.ds(m + mod(layer, which, 0), 1), v:v + 1].rearrange("p a t -> p (a t)")
                        y = slot(s)[:, c0:c1]
                        if permuted:
                            x = x.rearrange("p (r c) -> p r c", c=GRID_W)
                            y = y.rearrange("p (c r) -> p r c", r=GRID_H)
                        ins = dve.scalar_tensor_tensor(x, y, g, x, ALU.mult, ALU.add)
                    ins.then_inc(evac, 1)

                each_ring(dve, segs[name][0], 8, body)

            dve.wait_ge(row_in, 64)
            dve.wait_ge(o_put, 24)
            dve.wait_ge(nhi_done, READY["gla"] + KD)
            chain(dve.tensor_scalar(r_zz[:], dtT[:], rowc[:, 0:1], 0.0, ALU.add, ALU.max))
            dve.wait_ge(r_ez, 1)
            chain(dve.tensor_scalar(r_p[:], r_e[:], 2.0, None, ALU.add))
            chain(dve.reciprocal(r_p[:], r_p[:]))
            chain(dve.tensor_tensor(r_e[:], r_e[:], r_p[:], ALU.mult))
            chain(dve.tensor_tensor(r_s2[:], r_e[:], r_e[:], ALU.mult))
            chain(dve.tensor_scalar(r_p[:], r_s2[:], 1.0 / 17.0, None, ALU.mult))
            for k in range(15, 1, -2):
                chain(dve.scalar_tensor_tensor(r_p[:], r_p[:], 1.0 / k, r_s2[:], ALU.add, ALU.mult))
            chain(dve.scalar_tensor_tensor(r_p[:], r_p[:], 1.0, r_e[:], ALU.add, ALU.mult))
            chain(dve.scalar_tensor_tensor(r_zz[:], r_p[:], 2.0, r_zz[:], ALU.mult, ALU.add))
            chain(dve.tensor_scalar(r_ab[:], r_zz[:], 1e-19, None, ALU.max), r_dt)
            dve.wait_ge(r_ez, 2)
            chain(dve.tensor_scalar(r_zz[:], r_zz[:], rowc[:, 2:3], -1.0, ALU.mult, ALU.mult))
            for d in range(2):
                for c0, c1 in ((0, LAT), (LAT, T)):
                    src, dst = r_zz[:, c0:c1], Grow[:, d, c0:c1]
                    if d:
                        src, dst = src[:, ::-1], dst[:, ::-1]
                    one = ones[0:32, 0:1].broadcast_to([32, c1 - c0])
                    chain(dve.tensor_tensor_scan(dst, one, src, 0.0, ALU.mult, ALU.add))
            dve.wait_ge(r_lnd, 1)
            for d in range(2):
                chain(dve.tensor_tensor(r_nb[:, d], r_ln[:], Grow[:, d], ALU.subtract), r_nbd)
            residual("out0", 0, 2, T)

            def exponents(h):
                D = Dm[:, h % 2]
                if h >= 2:
                    dve.wait_ge(y_mm, h - 1)
                for d in range(2):
                    dve.wait_ge(rows_mm, 2 * h + d + 1)
                    r = 16 * d + h
                    parts = ((DL, 0, 4, LAT + P), (DC, 4, 6, CTX + P)) if d == 0 else ((DB, 0, 6, P),)
                    for off, c0, c1, step in parts:
                        ins = dve.tensor_tensor(diagonals(D, off, c1 - c0, step), slot(d)[:, c0 * P:c1 * P].rearrange("p (c t) -> p c t", t=P),
                                                nb[:, d, c0:c1, r:r + 1].broadcast_to([P, c1 - c0, P]), ALU.add)
                    ins.then_inc(e_done, 1)

            def head_weights(h):
                D = Dm[:, h % 2]
                dve.wait_ge(exp_done, 3 * h + 3)
                dve.wait_ge(cb_put, 6 * (h // 8) + 6)
                f, b = diagonals(D, DL, 4, LAT + P), diagonals(D, DB, 4, P)
                chain(dve.tensor_tensor(f, f, b, ALU.add))
                f, b = diagonals(D, DC, 2, CTX + P), diagonals(D, DB + 4 * P, 2, P)
                chain(dve.tensor_tensor(f, f, b, ALU.add))
                dve.tensor_tensor(D[:, 0:DB], D[:, 0:DB], cb[:], ALU.mult).then_inc(m_done, 1)
                c = Cb[:, h % 2]
                dve.tensor_tensor(c, c, bct[:, 1, 0:LAT].unsqueeze(1).broadcast_to([P, 2, LAT]), ALU.mult).then_inc(cbeta_done, 1)

            def weighted_x(p):
                dve.wait_ge(xt_put, p + 1)
                if p >= 2:
                    dve.wait_ge(s_mm, p - 1)
                for d in range(2):
                    w = al[:, d, :, 16 * d + 2 * p:16 * d + 2 * p + 2].unsqueeze(3).broadcast_to([P, 2, 2, 64])
                    dve.tensor_tensor(xal[:, p % 2, :, d].rearrange("p c (h f) -> p c h f", h=2),
                                      xtok[:, p % 2, 4:6].rearrange("p c (h f) -> p c h f", h=2), w, ALU.mult).then_inc(xal_done, 1)

            def state_copy(p):
                dve.wait_ge(s_mm, p + 1)
                if p >= 2:
                    dve.wait_ge(y_mm, 2 * p - 2)
                dve.tensor_copy(ssS[:, p % 2].rearrange("p d f -> p (d f)"), bank(6, 2 * P)).then_inc(ss_put, 1)

            def output(p):
                dve.wait_ge(y_mm, 2 * p + 2)
                chain(dve.scalar_tensor_tensor(yT[:, p], xt[:, p % 2], dcol[:, p:p + 1], slot(2), ALU.mult, ALU.add), y_put)
                chain(dve.tensor_tensor(yT[:, p], yT[:, p], sz[:, p % 2], ALU.mult), y_done)

            def add_square(p):
                dve.wait_ge(ysq_done, p + 1)
                if p % 4:
                    chain(dve.tensor_tensor(snacc[p // 4][:], snacc[p // 4][:], ssq[:, p % 2], ALU.add), ysum)

            dve.wait_ge(ct_put, 2)
            weighted_x(0)
            state_copy(0)
            exponents(0)
            for h in range(SSD_HEADS):
                if h + 1 < SSD_HEADS:
                    exponents(h + 1)
                head_weights(h)
                if h % 2 == 0:
                    if h:
                        output(h // 2 - 1)
                        state_copy(h // 2)
                    if h >= 4:
                        add_square(h // 2 - 2)
                elif h + 1 < SSD_HEADS:
                    weighted_x(h // 2 + 1)
            output(7)
            for p in (6, 7):
                add_square(p)
            for g in range(2):
                dve.drain().then_inc(sum_done, 1)
                rstd_diagonal(T)
                dve.wait_ge(rstd_done, rstds[0])
                for t in range(4 * g, 4 * g + 4):
                    chain(dve.scalar_tensor_tensor(yT[:, t], yT[:, t], par("ssd_norm", t), slot(2 + g), ALU.mult, ALU.mult), yn_done)
                for t in range(4 * g, 4 * g + 4):
                    dve.wait_ge(nhi_done, READY["ssd"] + t + 1)
                    dve.tensor_tensor(act_lo[:, t], yT[:, t], act_hi[:, t].bitcast(F32), ALU.subtract).then_inc(act_ready, 1)
            residual("out1", 0, 2, T)
            def ffn(layer, n):
                for g in range(3):
                    n0, count = segs[f"up{layer}{g}"][:2]
                    before = FF_BEFORE[f"{layer}{g}"]

                    def body(r, s):
                        if s % 2 == 0:
                            return
                        i, t = s // 2, r * 2 + (s // 2 - n0 // 2)
                        dve.wait_ge(fsg_done, t + (before + 1))
                        dve.wait_ge(mm_done, r * RING + (s + 1))
                        dve.tensor_tensor(fhp[:, i, 0:n], fsg[:, i, 0:n], slot(s)[:, 0:n], ALU.mult).then_inc(evac, 2)
                        dve.wait_ge(fhh_done, t + (before + 1))
                        hi, lo = (x[:, bass.ds(t, 1), 0:n].rearrange("p a t -> p (a t)") for x in (hid_hi, hid_lo))
                        dve.tensor_tensor(lo, fhp[:, i, 0:n], hi.bitcast(F32), ALU.subtract).then_inc(hid_ready, 1)
                        dve.wait_ge(hid_ready, t + (before + 1))

                    each_ring(dve, n0, count, body)
                    residual(f"down{layer}{g}", layer, 5, n)

            norm("ffn0", T)
            ffn(0, T)
            dve.wait_ge(m4_done, 1)
            dve.wait_ge(wb_in, 7 * 16)
            for t in range(16):
                if t >= 2:
                    dve.wait_ge(bdt_mm, t - 1)
                dve.tensor_tensor(bd[:, t % 2].rearrange("p m (b e) -> p m b e", e=4),
                                  mask4[:].rearrange("p (b e) -> p b e", e=4).unsqueeze(1).broadcast_to([P, 3, 32, 4]),
                                  w4[:, :, t].unsqueeze(2).broadcast_to([P, 3, 32, 4]), ALU.mult).then_inc(bd_done, 1)
            dve.wait_ge(wa_mm, 16)
            for b in range(4):
                dve.tensor_copy(wA[:, 4 * b:4 * b + 4].rearrange("p t e -> p (t e)"), bank(4 + b)).then_inc(wa_put, 1)
            dve.wait_ge(wg0, 1)
            gates = bank(2).rearrange("p (x t d g) -> p x t d g", x=2, t=16, d=2)
            for x in range(2):
                for d in range(2):
                    for k in range(2):
                        c = 32 * k + 4 * d
                        dve.tensor_copy(wG[:, x, :, c:c + 4], gates[:, x, :, d, 4 * k:4 * k + 4]).then_inc(wa_put, 1)
            dve.wait_ge(wa_put, 12)
            norm("mix1", T)

            def xm_unit(first):
                def body(r, s):
                    j = r * RING + (s - segs["xm"][0])
                    dve.wait_ge(evac, r * RING + (s + 1))
                    if not first:
                        dve.wait_ge(xc_out[s], XC_OUT0 + (r - segs["xm"][0] // RING) * 16)
                    convolve(xms[:, s], xcr[:, s], [par_at("m_conv_w", j + 16 * t) for t in range(3)], par_at("m_conv_b", j), j * 5 + 60)
                return body

            n0 = segs["xm"][0]
            each_ring(dve, n0, RING, xm_unit(True))
            each_ring(dve, n0 + RING, 16 - RING, xm_unit(False))
            dve.wait_ge(gr_put, 4)
            chain(dve.tensor_scalar(mr_i[:], mr_i[:], bif[:, 0:1], None, ALU.add))
            dve.wait_ge(gab_done, 1)
            chain(dve.tensor_scalar(mr_f[:], mr_f[:], bif[:, 1:2], 0.0, ALU.add, ALU.min))
            dve.wait_ge(gln_done, 1)
            chain(dve.tensor_tensor(mr_f[:], mr_f[:], mr_ab[:], ALU.subtract))

            def both_parts(dst, src, start, op):
                for d in range(2):
                    for c0, c1, init in ((LAT, T, start), (0, LAT, dst[:, d, T - 1:T] if d == 0 else dst[:, d, LAT:LAT + 1])):
                        x, y = src(d)[:, c0:c1], dst[:, d, c0:c1]
                        if d:
                            x, y = x[:, ::-1], y[:, ::-1]
                        chain(dve.tensor_tensor_scan(y, ones[0:8, 0:1].broadcast_to([8, c1 - c0]), x, init, ALU.mult, op))

            both_parts(mr_b, lambda d: mr_f[:], 0.0, ALU.add)
            for d in range(2):
                chain(dve.tensor_tensor(mr_u[:, d], mr_i[:], mr_b[:, d], ALU.subtract))
            both_parts(mr_M, lambda d: mr_u[:, d], -1e30, ALU.max)
            for d in range(2):
                chain(dve.tensor_scalar(negM[:, d], mr_M[:, d, 0:LAT], -1.0, None, ALU.mult))
                chain(dve.tensor_tensor(mr_m[:, d], mr_b[:, d, 0:LAT], mr_M[:, d, 0:LAT], ALU.add))
            dve.drain().then_inc(gm_done, 1)

            def value_blocks(h):
                if h:
                    dve.wait_ge(qv_mm, QV_MM0 + 12 * h)
                for t in range(4):
                    dve.tensor_tensor(bdv[:, t].rearrange("p (b e) -> p b e", e=4), mask4[:].rearrange("p (b e) -> p b e", e=4),
                                      w4[:, 2, 4 * h + t].unsqueeze(1).broadcast_to([P, 32, 4]), ALU.mult).then_inc(bdv_done, 1)

            def weight_exponents(h):
                for d in range(2):
                    dve.wait_ge(mrows_mm, MROWS_MM0 + 2 * h + d + 1)
                    r = 4 * d + h
                    blocks = diagonals((Wf, Wb)[d][:].rearrange("p c t -> p (c t)"), 0, 4, LAT + P)
                    dve.tensor_tensor(blocks, bank(d).rearrange("p (c t) -> p c t", t=P), ucol[:, d, 0:4, r:r + 1].broadcast_to([P, 4, P]),
                                      ALU.add).then_inc(de_done, 1)

            value_blocks(0)
            dve.wait_ge(gc_put, 2)
            dve.wait_ge(ge_done, 2)
            weight_exponents(0)
            for h in range(ML_HEADS):
                dve.wait_ge(we_done, WE_DONE0 + 2 * h + 2)
                for i, c in enumerate(KEYS):
                    dve.wait_ge(s6_mm, S6_MM0 + 6 * h + i + 1)
                    for d, W in enumerate((Wf, Wb)):
                        i0, i1 = (0, LAT) if c >= 4 else (c * P, LAT) if d == 0 else (0, c * P + P)
                        ins = dve.tensor_tensor(W[:, c, i0:i1], W[:, c, i0:i1], bank(4 + i % 2)[:, i0:i1], ALU.mult)
                        if d == 0:
                            chain(ins)
                        else:
                            chain(ins, s6_put)
                        acc = mtmp[:, 1 + d]
                        if i == 1:
                            chain(dve.tensor_tensor(acc, W[:, 4], W[:, 5], ALU.add))
                        elif i > 1:
                            chain(dve.tensor_tensor(acc[:, i0:i1], acc[:, i0:i1], W[:, c, i0:i1], ALU.add))
                dve.drain().then_inc(den_rdy, 1)
                dve.wait_ge(den_mm, h + 1)
                den = bank(0)[:, 0:8].rearrange("p (d c) -> p d c", d=2)
                chain(dve.tensor_scalar(dcl[:], den, -1.0, None, ALU.mult))
                chain(dve.tensor_tensor(dcl[:], dcl[:], den, ALU.max))
                for d in range(2):
                    chain(dve.tensor_tensor(dcl[:, d], dcl[:, d], ecol[:, d, :, 4 * d + h], ALU.max))
                chain(dve.reciprocal(dcl[:], dcl[:]))
                for d in range(2):
                    dst = rdiag[:, 0:LAT] if d == 0 else mtmp[:, 0]
                    chain(dve.tensor_tensor(dst.rearrange("p (q t) -> p q t", t=P), ident[:].unsqueeze(1).broadcast_to([P, 4, P]),
                                            dcl[:, d].unsqueeze(2).broadcast_to([P, 4, P]), ALU.mult))
                dve.drain().then_inc(rd_rdy, 1)
                if h == 2:
                    residual("mout0", 1, 2, LAT, permuted=True)
                dve.wait_ge(rfb_mm, RFB_MM0 + h + 1)
                rf, rb = bank(0), bank(1)
                for d, W in enumerate((Wf, Wb)):
                    chain(dve.tensor_tensor(W[:, 4:6], W[:, 4:6], bank(d).unsqueeze(1).broadcast_to([P, 2, LAT]), ALU.mult))
                chain(dve.tensor_tensor(Wf[:, 4:6], Wf[:, 4:6], Wb[:, 4:6], ALU.add), pn_done)
                for c in range(4):
                    chain(dve.tensor_tensor(Wf[:, c, c * P:LAT], Wf[:, c, c * P:LAT], rf[:, c * P:LAT], ALU.mult))
                    if c:
                        chain(dve.tensor_tensor(Wf[:, c, 0:c * P], Wb[:, c, 0:c * P], rb[:, 0:c * P], ALU.mult))
                df, db = (diagonals(W[:].rearrange("p c t -> p (c t)"), 0, 4, LAT + P) for W in (Wf, Wb))
                chain(dve.tensor_tensor(db, db, rb.rearrange("p (c t) -> p c t", t=P), ALU.mult))
                chain(dve.tensor_tensor(df, df, db, ALU.add), pn_done)
                if h + 1 < ML_HEADS:
                    value_blocks(h + 1)
                    weight_exponents(h + 1)
                acc = mtmp[:, 1]
                dve.wait_ge(h_put, H_PUT0 + 4 * h + 2)
                chain(dve.tensor_tensor(acc, hh[:, 0], hh[:, 1], ALU.add))
                for t in (2, 3):
                    dve.wait_ge(h_put, H_PUT0 + 4 * h + t + 1)
                    chain(dve.tensor_tensor(acc, acc, hh[:, t], ALU.add))
                dve.drain().then_inc(hs_rdy, 1)
                dve.wait_ge(mean_mm, h + 1)
                for t in range(4):
                    chain(dve.scalar_tensor_tensor(hh[:, t], bank(7), -1.0 / ML_DH, hh[:, t], ALU.mult, ALU.add), hc_done)
                for t in range(1, 4):
                    dve.wait_ge(hsq_done, HSQ_DONE0 + 4 * h + t + 1)
                    chain(dve.tensor_tensor(acc, acc, mtmp[:, (1, 0, 2, 0)[t]], ALU.add), hsum)
                dve.drain().then_inc(sum_done, 1)
                rstd_diagonal(LAT)
                dve.wait_ge(rstd_done, rstds[0])
                for t in range(4):
                    g = 4 * h + t
                    chain(dve.scalar_tensor_tensor(hh[:, t], hh[:, t], par("mh_norm", g), bank(6), ALU.mult, ALU.mult))
                    dve.wait_ge(xs_in[t], XS_IN0 + 16 * (h + 1))
                    chain(dve.scalar_tensor_tensor(halves(hh[:, t]), xs(t), par("skip", g), halves(hh[:, t]), ALU.mult, ALU.add))
                    dve.wait_ge(z_in[t % 2], Z_IN0 + 16 * (2 * h + t // 2 + 1))
                    chain(dve.tensor_tensor(hh[:, t], hh[:, t], zs[:, t % 2], ALU.mult), fin_done)
                for t in range(4):
                    k = 4 * (h % 2) + t
                    dve.wait_ge(nhi_done, READY["ml0"] + 4 * h + t + 1)
                    dve.tensor_tensor(act1_lo[:, k], hh[:, t], act1_hi[:, k].bitcast(F32), ALU.subtract).then_inc(act_ready, 1)
                dve.wait_ge(act_ready, READY["ml0"] + 4 * h + 4)
            residual("mout1", 1, 2, LAT, permuted=True)
            norm("ffn1", LAT)
            ffn(1, LAT)
            norm_sums("final", LAT)
            for k in range(KD):
                dve.scalar_tensor_tensor(fin[:, k], xT[:, k, 0:LAT], par("final_norm", k), slot(0)[:, 0:LAT], ALU.mult, ALU.mult).then_inc(fin_ready, 1)


_INS = ["x", "c", "ctx", "c_ctx", "w_mod", "b_mod", "norm_mix", "norm_ffn", "ffn_w1", "ffn_w3", "ffn_w2", "a_w_in",
        "a_gla_w_gate", "a_gla_b_gate", "a_gla_norm", "a_ssd_conv_w", "a_ssd_conv_b", "a_ssd_A_log", "a_ssd_dt_bias",
        "a_ssd_D", "a_ssd_norm", "a_w_out", "b_w_up", "b_conv_w", "b_conv_b", "b_wq", "b_wk", "b_wv", "b_w_if", "b_b_if",
        "b_mh_norm", "b_skip", "b_w_down", "final_norm"]


def kernel(**inputs):
    import numpy as _np
    import concourse.bacc as _bacc
    from concourse import mybir as _mybir
    from concourse.bass_utils import run_bass_kernel_spmd as _run

    nc = _bacc.Bacc("TRN2", target_bir_lowering=False, num_devices=1)
    arrays, args = {}, {}
    for name in _INS:
        x = _np.ascontiguousarray(inputs[name])
        arrays[f"in_{name}"] = x
        args[name] = nc.dram_tensor(f"in_{name}", x.shape, _mybir.dt.from_np(x.dtype), kind="ExternalInput").ap()
    out = nc.dram_tensor("out_y", (1, LAT, D), _mybir.dt.float32, kind="ExternalOutput").ap()
    trunk(nc, args, out)
    r = _run(nc, [arrays], core_ids=[0])
    return r.results[0]["out_y"]
```

```python
from contextlib import ExitStack

import concourse.bass as bass
from concourse import mybir

F32 = mybir.dt.float32
F32R = mybir.dt.float32r
ALU = mybir.AluOpType
ACT = mybir.ActivationFunctionType

P = 128
D = 1024
KD = D // P
LAT = 512
CTX = 256
T = LAT + CTX
GRID_W = 64
GRID_H = LAT // GRID_W
EPS = 1e-6
N_MOD = 6
MODS = 2 * N_MOD * KD
D_FF = 2816
FF_TILES = D_FF // P
FF_GROUPS = (8, 8, 6)
RING = 4

GLA_HEADS = 4
GLA_DK = 128
GLA_TAU = 16.0
SUB = 64
SSD_HEADS = 16
ML_HEADS = 4
ML_DH = 512

Q0, K0, V0, G0, Z0, X0, B0, C0, PROJ0 = 0, 4, 8, 16, 24, 32, 40, 42, 44
COL_R = 3072
COL_Z = 3104
COL_DT = 5664


def table_rows():
    at = {}
    t1 = [("norm_mix", 16), ("norm_ffn", 16), ("final_norm", 8), ("gla_b", 8), ("gla_norm", 2), ("conv_w", 36),
          ("conv_b", 12), ("ssd_norm", 8), ("c", 8), ("c_ctx", 8)]
    t2 = [("m_conv_w", 48), ("m_conv_b", 16), ("mh_norm", 16), ("skip", 16)]
    for table, rows in ((1, t1), (2, t2)):
        n = 0
        for name, count in rows:
            at[name] = (table, n, count)
            n += count
    at["b_mod"] = (0, 0, MODS)
    return at


ROWS = table_rows()
TABLE_LEN = [max(n + c for t, n, c in ROWS.values() if t == k) for k in range(3)]


def table_loads(a):
    def rows(w):
        while len(w.shape) > 1:
            w = w.rearrange("a b -> (a b)") if len(w.shape) == 2 else w.rearrange("a b c -> (a b c)")
        return w.rearrange("(r p) -> r p", p=P)

    sources = {"b_mod": a["b_mod"], "norm_mix": a["norm_mix"], "norm_ffn": a["norm_ffn"], "final_norm": a["final_norm"],
               "gla_b": a["a_gla_b_gate"], "gla_norm": a["a_gla_norm"], "conv_w": a["a_ssd_conv_w"],
               "conv_b": a["a_ssd_conv_b"], "ssd_norm": a["a_ssd_norm"], "c": a["c"], "c_ctx": a["c_ctx"],
               "m_conv_w": a["b_conv_w"], "m_conv_b": a["b_conv_b"], "mh_norm": a["b_mh_norm"], "skip": a["b_skip"]}
    return [(*ROWS[name][:2], rows(w)) for name, w in sources.items()]


def each_ring(eng, n0, count, body):
    first, last = n0 // RING, (n0 + count) // RING
    while first < min(2, last):
        for s in range(RING):
            body(first, s)
        first += 1
    if first < last:
        with eng.Fori(first, last) as r:
            for s in range(RING):
                body(r, s)


class Chain:

    def __init__(self, eng, own):
        self.eng, self.own, self.n = eng, own, {}

    def __call__(self, ins, sem=None, wait=True):
        sem = sem or self.own
        self.n[sem] = self.n.get(sem, 0) + 1
        ins.then_inc(sem, 1)
        if wait:
            self.eng.wait_ge(sem, self.n[sem])


def weight_segments(a):
    def kview(w):
        return w.rearrange("(k p) m -> p k m", p=P)

    segs, n = {}, 0

    def seg(name, count, kt, w, col0=0, w_odd=None):
        nonlocal n
        assert n % RING == 0 and count % RING == 0
        n0 = n
        if w_odd is None:
            def src(r, s):
                return w[:, :, bass.ds(r * (RING * P) + (s * P + col0 - n0 * P), P)]
        else:
            def src(r, s):
                return (w_odd if s % 2 else w)[:, :, bass.ds(r * (2 * P) + (s // 2 * P + col0 - n0 // 2 * P), P)]
        segs[name] = (n0, count, kt, src)
        n += count

    win, wup, wdn = kview(a["a_w_in"][0]), kview(a["b_w_up"][0]), kview(a["b_w_down"][0])
    wout = kview(a["a_w_out"][0])

    def ffn(layer):
        w1, w3, w2 = (kview(a[x][layer]) for x in ("ffn_w1", "ffn_w3", "ffn_w2"))
        f0 = 0
        for g, tiles in enumerate(FF_GROUPS):
            seg(f"up{layer}{g}", 2 * tiles, KD, w1, f0 * P, w3)
            seg(f"down{layer}{g}", KD, tiles, w2[:, f0:f0 + tiles, :])
            f0 += tiles

    seg("qkv", 16, KD, win)
    seg("g", 8, KD, win, 16 * P)
    seg("z", 8, KD, win, COL_Z)
    seg("xbc", 12, KD, win, COL_Z + 8 * P)
    seg("out0", 8, KD, wout[:, 0:KD, :])
    seg("out1", 8, KD, wout[:, KD:2 * KD, :])
    ffn(0)
    seg("xm", 16, KD, wup)
    seg("zm", 16, KD, wup, 16 * P)
    seg("mout0", 8, KD, wdn[:, 0:KD, :])
    seg("mout1", 8, KD, wdn[:, KD:2 * KD, :])
    ffn(1)
    segs["end"] = (n, 0, 0, None)
    return segs


def trunk(nc, a, out):
    segs = weight_segments(a)
    base, end = -(-nc.sbuf_base // 32) * 32, nc.sbuf_usable_end
    with ExitStack() as stack:
        top = [base]

        def sem(name):
            return stack.enter_context(nc.semaphore(name))

        def sb(name, shape, dt=F32, offset=None):
            size = 4
            for d in shape[1:]:
                size *= d
            where = top[0] if offset is None else arena_at + offset
            if offset is None:
                top[0] += -(-size // 32) * 32
            assert where + size <= end, (name, where + size - end)
            return nc.alloc_sbuf_tensor_at(name, shape, dt, offset=where)

        def dram(name, shape):
            return nc.dram_tensor(name, shape, F32, kind="Internal").ap()

        xT = sb("xT", [P, KD, T])
        act_hi_at = top[0]
        act_hi = sb("act_hi", [P, KD, T], F32R)
        act_lo_at = top[0]
        act_lo = sb("act_lo", [P, KD, T], F32R)
        w_raw = sb("w_raw", [P, RING, KD, P])
        w_hi = sb("w_hi", [P, RING, KD, P], F32R)
        w_lo = sb("w_lo", [P, RING, KD, P], F32R)
        ident = sb("ident", [P, P])
        ones = sb("ones", [P, P])
        tri = sb("tri", [P, 2, P])
        ptab = sb("ptab", [P, 3, P])
        modv = sb("modv", [P, MODS, 2])
        mscale = sb("mscale", [P, 2, 2, KD, 2])
        cs = sb("cs", [P, KD, 2])
        rcol = sb("rcol", [P, 2, T // P])
        rdiag = sb("rdiag", [P, T])
        eps_col = sb("eps_col", [P, 1])
        one_col = sb("one_col", [P, 1])
        arena_at = top[0]
        PS = stack.enter_context(nc.psum_tensor("PS", [P, 4096], F32))

        def slot(s):
            return PS[:, 1024 * s:1024 * s + T]

        def bank(b, n=512):
            return PS[:, 512 * b:512 * b + n]

        def par(name, k, n=1):
            t, row, _ = ROWS[name]
            return ptab[:, t, row + k:row + k + n]

        def par_at(name, j):
            t, row, _ = ROWS[name]
            return ptab[:, t, bass.ds(j + row, 1)]

        def mod_col(s):
            return 1024 * s + T

        def mod(layer, which, k):
            return layer * N_MOD * KD + which * KD + k

        proj0 = dram("proj0", (PROJ0, P, T))

        w_in = [sem(f"w_in{s}") for s in range(RING)]
        w_hi_done = sem("w_hi_done")
        w_split = sem("w_split")
        mm_done = sem("mm_done")
        evac = sem("evac")
        act_ready = sem("act_ready")
        act_own, dve_own, pool_own = sem("act_own"), sem("dve_own"), sem("pool_own")
        tab_in, x_in, consts = sem("tab_in"), sem("x_in"), sem("consts")
        tab_tr, x_tr, x_put, c_silu, mod_mm, mod_put = (sem(n) for n in ("tab_tr", "x_tr", "x_put", "c_silu", "mod_mm", "mod_put"))
        tab_put = sem("tab_put")
        mod_in = [sem(f"mod_in{s}") for s in range(3)]
        mrow_put, mrow_tr = sem("mrow_put"), sem("mrow_tr")
        m_in = [sem(f"m_in{s}") for s in range(RING)]
        m_step = sem("m_step")
        m_put = sem("m_put")
        prow = sb("prow", [P, 3, P], offset=0)
        xin = sb("xin", [P, 6, D], offset=1536)
        m_raw = sb("m_raw", [P, 3, KD, 512], offset=1536 + 24576)
        mrow = nc.alloc_sbuf_tensor_at("mrow", [2, 16 * P], F32, offset=act_lo_at)
        sq_done, sum_done, sum_mm, std_done, rstd_done, nt_done, nh_done, nhi_done = (
            sem(n) for n in ("sq_done", "sum_done", "sum_mm", "std_done", "rstd_done", "nt_done", "nh_done", "nhi_done"))
        nsum_step = sem("nsum_step")
        nsq = sb("nsq", [P, 2, T], offset=0)
        nacc = sb("nacc", [P, T], offset=6144)
        diag_done = sem("diag_done")
        nt = sb("nt", [P, 2, T], offset=12288)
        nh = sb("nh", [P, 2, T], offset=18432)
        stage = sb("stage", [P, RING, T], offset=24576)
        cpre = sb("cpre", [P, 2, T], offset=36864)
        cpost = sb("cpost", [P, 2, T], offset=43008)
        m_ring = sb("m_ring", [P, RING, KD, 2 * P], offset=49152)
        m_acc = sb("m_acc", [P, 2, 2, 2 * P], offset=18432)
        rd_raw = sb("rd_raw", [P, KD, P], offset=0)
        rd_hi = sb("rd_hi", [P, KD, P], F32R, offset=4096)
        rd_lo = sb("rd_lo", [P, KD, P], F32R, offset=8192)
        rT = sb("rT", [32, T], offset=12288)
        dtT = sb("dtT", [32, T], offset=15360)
        st_out = [sem(f"st_out{s}") for s in range(RING)]
        conv_step, silu_done, rd_in, rd_hi_done, rd_split, rd_mm, rd_put = (
            sem(n) for n in ("conv_step", "silu_done", "rd_in", "rd_hi_done", "rd_split", "rd_mm", "rd_put"))

        hq = sb("hq", [P, 4, T], offset=0)
        wg = sb("wg", [32, 2, P], offset=18432)
        gG = sb("gG", [P, 2, T], offset=19456)
        ga = sb("ga", [P, 2, T], offset=25600)
        gm = sb("gm", [P, 2, T], offset=31744)
        K2 = sb("K2", [P, 2, 6, 2, 2, SUB], offset=37888)
        qs = sb("qs", [P, 2, 6, SUB], offset=50176)
        qd = sb("qd", [P, 2, T], offset=53248)
        gS = sb("gS", [P, 2, 5, 2 * P], offset=59392)
        kdT = sb("kdT", [P, 10, P], offset=69632)
        vtok = sb("vtok", [P, 6, 2 * P], offset=74752)
        etot = sb("etot", [P, 2, 6], offset=80896)
        oT = gG
        Gn = nc.alloc_sbuf_tensor_at("Gn", [P, 2, T], F32, offset=act_hi_at + 6 * T * 4)
        gmn = nc.alloc_sbuf_tensor_at("gmn", [P, 2, T], F32, offset=act_lo_at + 6 * T * 4)
        hq_in, wg_zero, gate_mm, abs_done, min_done, ln_done, g_ready, x_ready, e0_done, qd_done, e1_done, e3_done = (
            sem("gla_" + n) for n in ("hq_in", "wg_zero", "gate_mm", "abs_done", "min_done", "ln_done", "g_ready", "x_ready",
                                      "e0_done", "qd_done", "e1_done", "e3_done"))
        y_ready, e4_done, kd_done, tr_done, tr_put, u_mm, s_done, sc_mm, a_done, o_mm, o_put, g_in, gsq_done, gfull = (
            sem("gla_" + n) for n in ("y_ready", "e4_done", "kd_done", "tr_done", "tr_put", "u_mm", "s_done", "sc_mm", "a_done",
                                      "o_mm", "o_put", "g_in", "gsq_done", "gfull"))
        wg_in, k2_done = sem("gla_wg_in"), sem("gla_k2_done")
        CHUNKS = ((4, 5, 0, 1, 2, 3), (5, 4, 3, 2, 1, 0))
        KD_ORDER = [(d, CHUNKS[d][i]) for i in range(5) for d in range(2)]

        PAIRS = SSD_HEADS // 2
        DL, DC, DB = 0, 4 * LAT, 4 * LAT + 2 * CTX
        Dm = sb("Dm", [P, 2, DB + 6 * P], offset=0)
        cb = sb("cb", [P, DB], offset=26624)
        Grow = sb("Grow", [32, 2, T], offset=36864)
        xt = sb("xt", [P, 2, T], offset=43008)
        xtok = sb("xtok", [P, 2, 6, P], offset=49152)
        sz = sb("sz", [P, 2, T], offset=55296)
        bct = sb("bct", [P, 2, T], offset=61440)
        Btok = sb("Btok", [P, 2, P], offset=67584)
        nb = sb("nb", [P, 2, 6, 32], offset=68608)
        al = sb("al", [P, 2, 2, 32], offset=70144)
        ssS = sb("ssS", [P, 2, 2, P], offset=70656)
        xal = sb("xal", [P, 2, 2, 2, P], offset=72704)
        dcol = sb("dcol", [P, PAIRS], offset=76800)
        rowc = sb("rowc", [32, 4], offset=76832)
        Cb = [nc.alloc_sbuf_tensor_at("Cb0", [P, 2, LAT], F32, offset=act_hi_at + 2 * DB * 4),
              sb("Cb1", [P, 2, LAT], offset=76864)]
        Mm = nc.alloc_sbuf_tensor_at("Mm", [P, 2, DB], F32, offset=act_hi_at)
        rdiag2 = sb("rdiag2", [P, T], offset=12288)
        snacc = [sb("snacc0", [P, T], offset=0), sb("snacc1", [P, T], offset=3072)]
        ssq = sb("ssq", [P, 2, T], offset=6144)
        yT = nc.alloc_sbuf_tensor_at("yT", [P, KD, T], F32, offset=act_lo_at)
        r_ab = sb("r_ab", [32, T], offset=0)
        r_e = sb("r_e", [32, T], offset=3072)
        r_s2 = sb("r_s2", [32, T], offset=6144)
        r_p = sb("r_p", [32, T], offset=9216)
        r_zz = sb("r_zz", [32, T], offset=12288)
        r_ln = sb("r_ln", [32, T], offset=18432)
        r_nb = sb("r_nb", [32, 2, T], offset=43008)
        r_al = sb("r_al", [32, 2, CTX], offset=49152)
        row_in, r_ez, r_dt, r_lnd, r_nbd, r_ald, ct_mm, ct_put, bc_in, cb_mm, cb_put, xt_in, xt_tr, xt_put, xal_done, s_mm = (
            sem("ssd_" + n) for n in ("row_in", "r_ez", "r_dt", "r_lnd", "r_nbd", "r_ald", "ct_mm", "ct_put", "bc_in", "cb_mm",
                                      "cb_put", "xt_in", "xt_tr", "xt_put", "xal_done", "s_mm"))
        ss_put, rows_mm, exp_done, mask_done, m_done, cbeta_done, y_mm, y_put, y_done, ysq_done, ysum = (
            sem("ssd_" + n) for n in ("ss_put", "rows_mm", "exp_done", "mask_done", "m_done", "cbeta_done", "y_mm", "y_put", "y_done",
                                      "ysq_done", "ysum"))
        yn_done, e_done, rows_read = sem("ssd_yn_done"), sem("ssd_e_done"), sem("ssd_rows_read")

        fsg = sb("fsg", [P, 2, T], offset=0)
        fhp = sb("fhp", [P, 2, T], offset=6144)
        hid_hi = sb("hid_hi", [P, 8, T], F32R, offset=12288)
        hid_lo = sb("hid_lo", [P, 8, T], F32R, offset=36864)
        fsg_done, fhh_done, hid_ready = sem("ffn_sg_done"), sem("ffn_hi_done"), sem("hid_ready")
        FF_BEFORE = {f"{layer}{g}": layer * FF_TILES + sum(FF_GROUPS[:g]) for layer in range(2) for g in range(3)}

        A_at = 61440
        wA = sb("wA", [P, 16, P], offset=A_at)
        w4 = sb("w4", [P, 3, 16, 4], offset=A_at + 8192)
        mask4 = sb("mask4", [P, P], offset=A_at + 8960)
        wG = sb("wG", [P, 2, 16, 40], offset=A_at + 9472)
        bif = sb("bif", [8, 2], offset=A_at + 14592)
        bd = sb("bd", [P, 2, 3, P], offset=57344)
        bdT = sb("bdT", [P, 2, 3, P], offset=A_at + 14624)
        wif = rdiag[:].rearrange("p (x t d g) -> p x t d g", x=3, t=16, d=2)
        xms = sb("xms", [P, RING, T], offset=24576)
        xcr = sb("xcr", [P, RING, T], offset=36864)
        zst = sb("zst", [P, RING, LAT], offset=49152)
        gx = sb("gx", [P, RING, 2, T], offset=0)
        xm_d, xc_d = dram("xm_d", (16, P, T)), dram("xc_d", (16, P, T))
        z_d = dram("z_d", (16, P, LAT))
        wb_in, wif_in, m4_done, bd_done, bdt_mm, bdt_put, wa_mm, wa_put, wg0, mxc_done, gx_mm = (
            sem("ml_" + n) for n in ("wb_in", "wif_in", "m4_done", "bd_done", "bdt_mm", "bdt_put", "wa_mm", "wa_put", "wg0", 
                                     "mxc_done", "gx_mm"))

        mr_i = sb("mr_i", [8, T], offset=0)
        mr_f = sb("mr_f", [8, T], offset=3072)
        mr_ab = sb("mr_ab", [8, T], offset=6144)
        mr_b = sb("mr_b", [8, 2, T], offset=9216)
        mr_u = sb("mr_u", [8, 2, T], offset=15360)
        mr_M = sb("mr_M", [8, 2, T], offset=24576)
        mr_m = sb("mr_m", [8, 2, LAT], offset=30720)
        negM = sb("negM", [8, 2, LAT], offset=77056)
        ucol = sb("ucol", [P, 2, 6, 8], offset=81152)
        ecol = sb("ecol", [P, 2, 4, 8], offset=81536)
        dcl = sb("dcl", [P, 2, 4], offset=81792)
        xch = sb("xch", [P, 4, T], offset=0)
        xmr = sb("xmr", [P, 2, T], offset=12288)
        vt = sb("vt", [P, 6, 4 * P], offset=18432)
        qp = sb("qp", [P, 4, LAT], offset=30720)
        Wf = sb("Wf", [P, 6, LAT], offset=38912)
        hh = sb("hh", [P, 4, LAT], offset=51200)
        bdv = sb("bdv", [P, 4, P], offset=59392)
        mtmp = sb("mtmp", [P, 3, LAT], offset=70912)
        act1_hi = nc.alloc_sbuf_tensor_at("act1_hi", [P, KD, LAT], F32R, offset=act_hi_at)
        act1_lo = nc.alloc_sbuf_tensor_at("act1_lo", [P, KD, LAT], F32R, offset=act_hi_at + KD * LAT * 4)
        Wb = nc.alloc_sbuf_tensor_at("Wb", [P, 6, LAT], F32, offset=act_hi_at + 2 * KD * LAT * 4)
        zs = nc.alloc_sbuf_tensor_at("zs", [P, 2, LAT], F32, offset=act_hi_at + 2 * KD * LAT * 4 + 6 * LAT * 4)

        def xs(i):
            return xT[:, 2 * i:2 * i + 2, LAT:T]

        def halves(ap):
            return ap.rearrange("p (a t) -> p a t", a=2)

        A8 = 2 * GLA_HEADS
        A24, A40 = 6 * GLA_HEADS, 10 * GLA_HEADS
        mrows_mm, MROWS_MM0 = gate_mm, A8
        de_done, DE_DONE0 = min_done, A8
        we_done, WE_DONE0 = ln_done, A8
        den_rdy, DEN_RDY0 = g_ready, A8
        rd_rdy, RD_RDY0 = x_ready, A8
        pn_done, PN_DONE0 = qd_done, A8
        hs_rdy, HS_RDY0 = y_ready, A8
        hc_done, HC_DONE0 = kd_done, A8
        h_put, H_PUT0 = e0_done, A8
        hsq_done, HSQ_DONE0 = e1_done, A8
        fin_done, FIN_DONE0 = gfull, A8
        h_mm, H_MM0 = tr_done, A24
        qv_mm, QV_MM0 = sc_mm, A24
        qv_put, QV_PUT0 = tr_put, A24
        s6_mm, S6_MM0 = u_mm, A40
        s6_put, S6_PUT0 = s_done, A40
        rfb_mm, RFB_MM0 = o_mm, A24
        xch_in, XCH_IN0 = hq_in, 64 * GLA_HEADS
        hsum, HSUM0 = a_done, A24
        xm_out, XM_OUT0 = st_out, 176
        z_out, Z_OUT0 = st_out, 240
        xc_out, XC_OUT0 = m_in, 160
        gx_in, GX_IN0 = m_in, 224
        xs_in, XS_IN0 = m_in, 352
        xmr_in, XMR_IN0 = st_out[0:2], 304
        z_in, Z_IN0 = st_out[2:4], 304
        gr_put, gab_done, gln_done, gm_done, ge_done, gc_mm, gc_put = (
            sem("mg_" + n) for n in ("gr_put", "gab_done", "gln_done", "gm_done", "ge_done", "gc_mm", "gc_put"))
        mk_done, bdv_done, den_mm, mean_mm = (sem("mh_" + n) for n in ("mk_done", "bdv_done", "den_mm", "mean_mm"))
        OUT_BANKS = (6, 7, 4, 5)
        SCORE_BANKS = (4, 5, 2, 3, 4, 5)
        KEYS = (4, 5, 0, 1, 2, 3)
        fin = sb("fin", [P, KD, LAT], offset=24576)
        obuf = sb("obuf", [P, 4, D], offset=43008)
        fin_ready, out_tr, out_put = (sem(n) for n in ("fin_ready", "out_tr", "out_put"))
        out_st = [sem(f"out_st{s}") for s in range(2)]

        def diagonals(t, off, n, step):
            ap = t[:, off:off + P]
            return bass.AP(tensor=ap.tensor, offset=ap.offset, ap=[list(ap.ap[0]), [step, n], [1, P]])

        WITH_MOD = ("qkv", "g", "z", "xbc")
        MOD_UNITS = 44
        MOD_BANKS = (0, 3, 4, 5)
        NORM_AFTER = {"ffn0": "out1", "mix1": "down02", "ffn1": "mout1", "final": "down12"}
        NORMS = ["mix0", "ffn0", "mix1", "ffn1", "final"]
        READY = {name: KD * i for i, name in enumerate(("mix0", "gla", "ssd", "ffn0", "mix1", "ml0", "ml1", "ffn1"))}

        def nh_count(name, tiles):
            return 2 * KD * NORMS.index(name) + tiles * (1 if name == "ffn1" else 2)

        block = stack.enter_context(nc.Block())

        @block.sync
        def _(sp):
            for t, row, src in table_loads(a):
                sp.dma_start(prow[row:row + src.shape[0], t, :], src).then_inc(tab_in, 16)
            sp.dma_start(xin[:, 0:4, :], a["x"][0].rearrange("(a p) d -> p a d", p=P)).then_inc(x_in, 16)
            sp.dma_start(xin[:, 4:6, :], a["ctx"][0].rearrange("(a p) d -> p a d", p=P)).then_inc(x_in, 16)
            for u in range(4):
                if u >= 3:
                    sp.wait_ge(mod_mm, u - 2)
                wm = a["w_mod"][0].rearrange("(k p) m -> p k m", p=P)
                sp.dma_start(m_raw[:, u % 3], wm[:, :, 512 * u:512 * u + 512]).then_inc(mod_in[u % 3], 16)
            n0, _, kt, src = segs["qkv"]
            for s in range(RING):
                sp.dma_start(w_raw[:, s, 0:kt], src(0, s)).then_inc(w_in[s], 16)
            sp.wait_ge(mod_put, 1)

            for name, (n0, count, kt, src) in segs.items():
                def load(r, s, kt=kt, src=src):
                    sp.wait_ge(w_split, r * RING + (s - RING + 1))
                    sp.dma_start(w_raw[:, s, 0:kt], src(r, s)).then_inc(w_in[s], 16)

                if n0 >= MOD_UNITS:
                    each_ring(sp, n0, count, load)
                    continue

                for r0, r1 in ((max(n0 // RING, 1), min((n0 + count) // RING, 5)), (max(n0 // RING, 5), (n0 + count) // RING)):
                    if r0 >= r1:
                        continue
                    layer = r0 // 5 if r0 < 5 else 1
                    wm = a["w_mod"][layer].rearrange("(k p) m -> p k m", p=P)

                    def load_both(r, s):
                        load(r, s)
                        if not (isinstance(r, int) and r == 1):
                            sp.wait_ge(m_step, (r * RING + (s - 2 * RING + 1)) * (2 * KD))
                        col = r * (2 * RING * P) + ((2 * s + 8 - 48 * layer) * P)
                        sp.dma_start(m_ring[:, s], wm[:, :, bass.ds(col, 2 * P)]).then_inc(m_in[s], 16)

                    if r0 == 1:
                        for s in range(RING):
                            load_both(1, s)
                        r0 = 2
                    each_ring(sp, r0 * RING, (r1 - r0) * RING, load_both)

        @block.gpsimd
        def _(pool):
            chain = Chain(pool, pool_own)
            chain(pool.memset(ones[:], 1.0))
            chain(pool.memset(eps_col[:], EPS))
            chain(pool.memset(one_col[:], 1.0))
            chain(pool.memset(ident[:], 0.0))
            chain(pool.memset(tri[:], 1.0))
            chain(pool.affine_select(out=ident[:], in_=ident[:], compare_op=ALU.not_equal, fill=1.0, base=0,
                                     pattern=[[-1, P]], channel_multiplier=1))
            chain(pool.affine_select(out=tri[:, 0], in_=tri[:, 0], compare_op=ALU.is_ge, fill=0.0, base=0,
                                     pattern=[[1, P]], channel_multiplier=-1))
            chain(pool.affine_select(out=tri[:, 1], in_=tri[:, 1], compare_op=ALU.is_ge, fill=0.0, base=0,
                                     pattern=[[-1, P]], channel_multiplier=1), consts)

            def split(r, s, kt, n0=None):
                pool.wait_ge(w_in[s], r * 16 + 16)
                if not (isinstance(r, int) and r == 0):
                    pool.wait_ge(mm_done, r * RING + (s - RING + 1))
                pool.tensor_tensor(w_hi[:, s, 0], w_raw[:, s, 0], ones[:], ALU.mult)
                pool.tensor_scalar(w_hi[:, s, 1:kt], w_raw[:, s, 1:kt], 1.0, 1.0, ALU.mult, ALU.mult).then_inc(w_hi_done, 1)
                pool.wait_ge(w_hi_done, r * RING + (s + 1))
                pool.tensor_tensor(w_lo[:, s, 0:kt], w_raw[:, s, 0:kt], w_hi[:, s, 0:kt].bitcast(F32),
                                   ALU.subtract).then_inc(w_split, 1)

            for name, (n0, count, kt, src) in segs.items():
                if name == "out0":
                    pool.wait_ge(act_ready, READY["mix0"] + KD)
                    pool.wait_ge(rd_in, 32)
                    pool.tensor_scalar(rd_hi[:], rd_raw[:], 1.0, 1.0, ALU.mult, ALU.mult).then_inc(rd_hi_done, 1)
                    pool.wait_ge(rd_hi_done, 1)
                    pool.tensor_tensor(rd_lo[:], rd_raw[:], rd_hi[:].bitcast(F32), ALU.subtract).then_inc(rd_split, 1)
                if name == "out1":
                    each_ring(pool, n0, RING, lambda r, s: split(r, s, kt))
                    for h in range(SSD_HEADS):
                        d = Dm[:, h % 2]
                        pool.wait_ge(e_done, 2 * h + 1)
                        for off, n, step in ((DL, 4, LAT + P), (DC, 2, CTX + P)):
                            blocks = diagonals(d, off, n, step)
                            pool.affine_select(out=blocks, in_=blocks, compare_op=ALU.is_ge, fill=-1e30, base=0,
                                               pattern=[[0, n], [1, P]], channel_multiplier=-1).then_inc(mask_done, 1)
                        pool.wait_ge(e_done, 2 * h + 2)
                        blocks = diagonals(d, DB, 6, P)
                        pool.affine_select(out=blocks, in_=blocks, compare_op=ALU.is_ge, fill=-1e30, base=0,
                                           pattern=[[0, 6], [-1, P]], channel_multiplier=1).then_inc(mask_done, 1)
                    each_ring(pool, n0 + RING, count - RING, lambda r, s: split(r, s, kt))
                    continue
                if name in ("mout0", "mout1"):
                    each_ring(pool, n0, RING, lambda r, s: split(r, s, kt))
                    for h in range(3) if name == "mout0" else (3,):
                        for d in range(2):
                            pool.wait_ge(de_done, DE_DONE0 + 2 * h + d + 1)
                            blocks = diagonals((Wf, Wb)[d][:].rearrange("p c t -> p (c t)"), 0, 4, LAT + P)
                            pool.affine_select(out=blocks, in_=blocks, compare_op=ALU.is_ge, fill=-1e30, base=0,
                                               pattern=[[0, 4], [1 - 2 * d, P]], channel_multiplier=2 * d - 1).then_inc(mk_done, 1)
                    each_ring(pool, n0 + RING, count - RING, lambda r, s: split(r, s, kt))
                    continue
                each_ring(pool, n0, count, lambda r, s: split(r, s, kt))
                if name == "up00":
                    pool.wait_ge(yn_done, 8)
                    m3 = mask4[:].rearrange("p (b e) -> p b e", e=4)
                    chain(pool.memset(mask4[:], 1.0))
                    chain(pool.memset(wG[:], 0.0), wg0)
                    chain(pool.affine_select(out=m3, in_=m3, compare_op=ALU.is_ge, fill=0.0, base=0,
                                             pattern=[[-4, 32], [0, 4]], channel_multiplier=1))
                    chain(pool.affine_select(out=m3, in_=m3, compare_op=ALU.is_ge, fill=0.0, base=3,
                                             pattern=[[4, 32], [0, 4]], channel_multiplier=-1), m4_done)

        @block.tensor
        def _(pe):
            pe.wait_ge(consts, 1)
            pe.wait_ge(tab_in, 16 * len(table_loads(a)))
            for t in range(3):
                n = TABLE_LEN[t]
                pe.transpose(bank(0)[:, t * P:t * P + n], prow[0:n, t, :], ident[0:n, 0:n]).then_inc(tab_tr, 1)
            pe.wait_ge(x_in, 32)
            for i in range(12):
                tt, half = i // 2, i % 2
                if i >= 2:
                    pe.wait_ge(x_put, i - 1)
                for q in range(4):
                    k = 4 * half + q
                    last = pe.transpose(bank(1 + i % 2)[:, q * P:q * P + P], xin[:, tt, k * P:k * P + P], ident[:])
                last.then_inc(x_tr, 1)
            pe.wait_ge(c_silu, 2)
            def first_modulation(u):
                pe.wait_ge(mod_in[u % 3], 16 * (u // 3 + 1))
                for k in range(KD):
                    last = pe.matmul(bank(MOD_BANKS[u])[0:2, :], cs[:, k, :], m_raw[:, u % 3, k, :], start=k == 0, stop=k == KD - 1)
                last.then_inc(mod_mm, 1)

            rstds = [0, 0]

            def rstd_products(sq, n, where):
                rstd_sums(sq, n, where)
                rstd_spread(n, where)

            def rstd_sums(sq, n, where):
                rstds[1] += 1
                pe.wait_ge(sum_done, rstds[1])
                for t in range(n // P):
                    last = pe.matmul(slot(where)[:, t:t + 1], sq[:, t * P:t * P + P], ones[:, 0:1], start=True, stop=True)
                last.then_inc(sum_mm, 1)

            def rstd_spread(n, where, rdiag=rdiag):
                pe.wait_ge(diag_done, rstds[0] + 1)
                for c0, c1 in ((0, 512), (512, 768))[:1 if n == LAT else 2]:
                    last = pe.matmul(slot(where)[:, c0:c1], ones[:], rdiag[:, c0:c1], start=True, stop=True)
                last.then_inc(rstd_done, 1)
                rstds[0] += 1

            def unit(s, kt, hi, lo, n, wh, wl):
                for k in range(kt):
                    for w, x in ((wh, hi), (wh, lo), (wl, hi)):
                        for c0, c1 in ((0, 512), (512, 768))[:1 if n == LAT else 2]:
                            last = pe.matmul(slot(s)[:, c0:c1], w[:, k, :], x[:, k, c0:c1],
                                             start=k == 0 and w is wh and x is hi, stop=k == kt - 1 and w is wl)
                return last

            def project(name, hi, lo, n, ready, ready0, together=0):
                n0, count, kt, _ = segs[name]
                if together:
                    for s in range(together):
                        pe.wait_ge(w_split, n0 + s + 1)
                        if n0:
                            pe.wait_ge(evac, n0 + s - RING + 1)
                    for k in range(kt):
                        pe.wait_ge(ready, ready0 + k + 1)
                        for s in range(together):
                            last = tile_products(s, k, kt, hi, lo, n)
                            if k == kt - 1:
                                last.then_inc(mm_done, 1)
                    for s in range(together, RING):
                        project_unit(name, n0 // RING, s, kt, hi, lo, n, ready, ready0)
                    each_ring(pe, n0 + RING, count - RING, lambda r, s: project_unit(name, r, s, kt, hi, lo, n, ready, ready0))
                    return
                each_ring(pe, n0, count, lambda r, s: project_unit(name, r, s, kt, hi, lo, n, ready, ready0))

            def tile_products(s, k, kt, hi, lo, n):
                for w, x in ((w_hi, hi), (w_hi, lo), (w_lo, hi)):
                    for c0, c1 in ((0, 512), (512, 768))[:1 if n == LAT else 2]:
                        last = pe.matmul(slot(s)[:, c0:c1], w[:, s, k, :], x[:, k, c0:c1],
                                         start=k == 0 and w is w_hi and x is hi, stop=k == kt - 1 and w is w_lo)
                return last

            def project_unit(name, r, s, kt, hi, lo, n, ready, ready0, between=None):
                pe.wait_ge(w_split, r * RING + (s + 1))
                if not (isinstance(r, int) and r == 0):
                    pe.wait_ge(evac, r * RING + (s - RING + 1))
                    if name in WITH_MOD and not (isinstance(r, int) and r <= 1):
                        pe.wait_ge(m_put, r * RING + (s - 2 * RING + 1))
                for k in range(kt):
                    if s == 0:
                        pe.wait_ge(ready, ready0 + k + 1)
                    last = tile_products(s, k, kt, hi, lo, n)
                    if between and k % 2 == 0:
                        between(k // 2)
                    if name in WITH_MOD and not (isinstance(r, int) and r == 0) and k % 2 == 0:
                        if k == 0:
                            pe.wait_ge(m_step, (r * RING + (s - RING + 1)) * (2 * KD))
                        m, v = k // 4, k // 2 % 2
                        pe.matmul(PS[:, mod_col(s) + k // 2:mod_col(s) + k // 2 + 1], m_acc[:, s % 2, v, m * P:m * P + P],
                                  ones[:, 0:1], start=False, stop=False, skip_group_check=True)
                last.then_inc(mm_done, 1)

            first_modulation(0)
            first_modulation(1)
            rstd_sums(nacc, T, 3)
            first_modulation(2)
            rstd_spread(T, 3)
            first_modulation(3)
            pe.wait_ge(mrow_put, 4)
            pe.wait_ge(x_put, 12)
            for m in range(16):
                last = pe.transpose(bank(2)[:, 2 * m:2 * m + 2], mrow[:, m * P:m * P + P], ident[0:2, 0:2])
            last.then_inc(mrow_tr, 1)
            for name in ("qkv", "g", "z", "xbc"):
                project(name, act_hi, act_lo, T, act_ready, 0, together=3 if name == "qkv" else 0)
            pe.wait_ge(rd_split, 1)
            pe.wait_ge(evac, MOD_UNITS)
            pe.wait_ge(m_put, MOD_UNITS - RING)
            unit(0, KD, act_hi, act_lo, T, rd_hi, rd_lo).then_inc(rd_mm, 1)
            pe.wait_ge(rd_put, 2)
            pe.wait_ge(wg_zero, 2)
            def gla_gates(h):
                pe.wait_ge(wg_in, 32 * (h + 1))
                if h:
                    pe.wait_ge(tr_put, 6 * h)
                    pe.wait_ge(a_done, 6 * h)
                for d in range(2):
                    for c0, c1 in ((0, 512), (512, 768)):
                        last = pe.matmul(slot(d)[:, c0:c1], wg[:, d, :], rT[:, c0:c1], start=True, stop=True)
                    last.then_inc(gate_mm, 1)

            gla_gates(0)
            for h in range(GLA_HEADS):
                pe.wait_ge(hq_in, 64 * (h + 1))
                pe.wait_ge(min_done, 2 * h + 2)
                pe.wait_ge(abs_done, 2 * h + 2)
                for i in range(3):
                    if i == 2:
                        pe.wait_ge(tr_put, 6 * h + 1)
                    for c in (2 * i, 2 * i + 1):
                        for t in range(2):
                            at = (c % 2 * 2 + t) * P
                            last = pe.transpose(bank(i % 2)[:, at:at + P], hq[:, 2 + t, c * P:c * P + P], ident[:])
                    last.then_inc(tr_done, 1)

                def scores(i):
                    c = CHUNKS[0][i]
                    if i >= 2:
                        pe.wait_ge(a_done, 6 * h + i - 1)
                    for d in range(2):
                        for b in range(2):
                            q = qd[:, d, c * P + b * SUB:c * P + b * SUB + SUB] if b == d else qs[:, d, c, :]
                            last = pe.matmul(bank(2 + i % 2)[:, d * P + b * SUB:d * P + b * SUB + SUB],
                                             K2[:, d, c, b].rearrange("p a t -> p (a t)"), q, start=True, stop=True)
                    last.then_inc(sc_mm, 1)

                pe.wait_ge(k2_done, 2 * h + 2)
                scores(0)
                pe.wait_ge(kd_done, 2 * h + 2)
                for i in range(3):
                    pe.wait_ge(tr_put, 6 * h + i + 2)
                    for e in range(4 * i, min(4 * i + 4, 10)):
                        d, c = KD_ORDER[e]
                        last = pe.transpose(bank((3 + i) % 2)[:, e % 4 * P:e % 4 * P + P], ga[:, d, c * P:c * P + P], ident[:])
                    last.then_inc(tr_done, 1)

                if h:
                    pe.wait_ge(gfull, 2 * h)
                for e, (d, c) in enumerate(KD_ORDER):
                    pe.wait_ge(tr_put, 6 * h + 4 + e // 4)
                    if 10 * h + e - 1 >= 1:
                        pe.wait_ge(s_done, 10 * h + e - 1)
                    pe.matmul(bank(4 + d)[:, 0:2 * P], kdT[:, e, :], vtok[:, c, :], start=True, stop=True).then_inc(u_mm, 1)
                    if d:
                        scores(e // 2 + 1)
                pe.wait_ge(s_done, 10 * h + 10)
                for i, c in enumerate(CHUNKS[0]):
                    pe.wait_ge(a_done, 6 * h + i + 1)
                    if 6 * h + i >= 2:
                        pe.wait_ge(o_put, 6 * h + i - 1)
                    for t in range(2):
                        terms = [(vtok[:, c, t * P:t * P + P], gm[:, 0, i * P:i * P + P])]
                        for d in range(2):
                            k = CHUNKS[d].index(c)
                            if k:
                                terms.append((gS[:, d, k - 1, t * P:t * P + P], qd[:, d, c * P:c * P + P]))
                        for n, (w, x) in enumerate(terms):
                            last = pe.matmul(bank(6 + i % 2)[:, t * P:t * P + P], w, x, start=n == 0, stop=n == len(terms) - 1)
                    last.then_inc(o_mm, 1)
                if h + 1 < GLA_HEADS:
                    gla_gates(h + 1)
                rstd_products(gm[:, 0], T, 2)
            pe.wait_ge(gfull, 8)
            pe.wait_ge(o_put, 24)
            project("out0", act_hi, act_lo, T, act_ready, READY["gla"], together=2)
            pe.wait_ge(evac, segs["out1"][0])
            pe.wait_ge(r_nbd, 2)
            pe.wait_ge(r_ald, 2)
            for d in range(2):
                for c in range(6):
                    pe.transpose(bank(6)[:, (6 * d + c) * 32:(6 * d + c) * 32 + 32], r_nb[:, d, c * P:c * P + P], ident[0:32, 0:32])
            for d in range(2):
                for c in range(2):
                    last = pe.transpose(bank(7)[:, (2 * d + c) * 32:(2 * d + c) * 32 + 32], r_al[:, d, c * P:c * P + P], ident[0:32, 0:32])
            last.then_inc(ct_mm, 1)

            def group_products(g):
                pe.wait_ge(bc_in, 32 * (g + 1))
                pe.wait_ge(ct_put, 2)
                if g:
                    pe.wait_ge(xt_put, 4 * g)
                    pe.wait_ge(ss_put, 4 * g)
                for i in range(6):
                    if 6 * g + i >= 2:
                        pe.wait_ge(cb_put, 6 * g + i - 1)
                    B, C, out = bct[:, 0], bct[:, 1], bank(6 + i % 2)
                    if i < 4:
                        last = pe.matmul(out[:], B[:, i * P:i * P + P], C[:, 0:LAT], start=True, stop=True)
                    elif i == 4:
                        for c in range(2):
                            last = pe.matmul(out[:, c * CTX:c * CTX + CTX], B[:, LAT + c * P:LAT + c * P + P], C[:, LAT:T],
                                             start=True, stop=True)
                    else:
                        for c in range(2):
                            last = pe.transpose(out[:, c * P:c * P + P], B[:, LAT + c * P:LAT + c * P + P], ident[:])
                    last.then_inc(cb_mm, 1)

            def x_transposes(p):
                pe.wait_ge(xt_in, 32 * (p + 1))
                if p % 4 == 0:
                    pe.wait_ge(cb_put, 6 * (p // 4 + 1))
                if p:
                    pe.wait_ge(ss_put, p)
                for c in range(6):
                    last = pe.transpose(slot(3)[:, c * P:c * P + P], xt[:, p % 2, c * P:c * P + P], ident[:])
                last.then_inc(xt_tr, 1)

            def states(p):
                pe.wait_ge(xal_done, 2 * p + 2)
                pe.wait_ge(xt_put, p + 1)
                for c in range(2):
                    last = pe.matmul(bank(6)[:, 0:2 * P], Btok[:, c], xal[:, p % 2, c].rearrange("t d f -> t (d f)"),
                                     start=c == 0, stop=c == 1)
                last.then_inc(s_mm, 1)

            def rows(h):
                for d in range(2):
                    if h:
                        pe.wait_ge(rows_read, 2 * h - 1 + d)
                    for c0, c1 in ((0, 512), (512, 768)):
                        r = 16 * d + h
                        last = pe.matmul(slot(d)[:, c0:c1], ident[0:32, r:r + 1].broadcast_to([32, P]), Grow[:, d, c0:c1],
                                         start=True, stop=True)
                    last.then_inc(rows_mm, 1)

            def head_products(h):
                p, f = h // 2, h % 2 * 64
                pe.wait_ge(m_done, h + 1)
                pe.wait_ge(cbeta_done, h + 1)
                pe.wait_ge(xt_put, p + 1)
                pe.wait_ge(ss_put, p + 1)
                if p and h % 2 == 0:
                    pe.wait_ge(y_put, p)
                y, d = slot(2)[f:f + 64], Mm[:, h % 2]
                for c in range(4):
                    pe.matmul(y[:, 0:LAT], xtok[:, p % 2, c, f:f + 64], d[:, c * LAT:c * LAT + LAT], start=c == 0, stop=False)
                for k in range(2):
                    pe.matmul(y[:, 0:LAT], ssS[:, p % 2, k, f:f + 64], Cb[h % 2][:, k], start=False, stop=k == 1)
                for c in range(2):
                    last = pe.matmul(y[:, LAT:T], xtok[:, p % 2, 4 + c, f:f + 64], d[:, DC + c * CTX:DC + c * CTX + CTX],
                                     start=c == 0, stop=c == 1)
                last.then_inc(y_mm, 1)

            group_products(0)
            x_transposes(0)
            rows(0)
            rows(1)
            for h in range(SSD_HEADS):
                if h + 2 < SSD_HEADS and h + 1 != 8:
                    rows(h + 2)
                if h % 2 == 0:
                    states(h // 2)
                head_products(h)
                if h + 1 == 8:
                    group_products(1)
                if h % 2 and h + 1 < SSD_HEADS:
                    x_transposes(h // 2 + 1)
                if h + 1 == 8:
                    rows(9)
            for g in range(2):
                rstd_sums(snacc[g], T, 2 + g)
            for g in range(2):
                rstd_spread(T, 2 + g, (rdiag, rdiag2)[g])
            project("out1", act_hi, act_lo, T, act_ready, READY["ssd"], together=2)
            def norm_products(name, n):
                pe.wait_ge(evac, segs[{"ffn0": "up00", "mix1": "xm", "ffn1": "up10"}.get(name, "end")][0])
                rstd_products(nacc, n, 3)

            def ffn(layer, n):
                for g in range(3):
                    project(f"up{layer}{g}", act_hi, act_lo, n, act_ready, READY[f"ffn{layer}"], together=0 if g else 3)
                    project(f"down{layer}{g}", hid_hi, hid_lo, n, hid_ready, FF_BEFORE[f"{layer}{g}"], together=2)

            norm_products("ffn0", T)
            ffn(0, T)
            norm_products("mix1", T)
            project("xm", act_hi, act_lo, T, act_ready, READY["mix1"], together=3)
            pe.wait_ge(evac, segs["zm"][0])
            pe.wait_ge(wif_in, 96)
            n0 = segs["zm"][0]

            def block_transposes(t):
                pe.wait_ge(bd_done, t + 1)
                if t >= 2:
                    pe.wait_ge(bdt_put, t - 1)
                for m in range(3):
                    last = pe.transpose(bank(5 + 2 * (t % 2))[:, m * P:m * P + P], bd[:, t % 2, m], ident[:])
                last.then_inc(bdt_mm, 1)

            def block_products(t):
                pe.wait_ge(bdt_put, t + 1)
                if t >= 2:
                    pe.wait_ge(wa_put, 3 * (t - 1))
                b, to = bdT[:, t % 2], bank(1 + 2 * (t % 2))
                pe.matmul(to[:, 0:P], b[:, 0], b[:, 1], start=True, stop=True)
                for m, x in ((0, 0), (1, 0), (2, 1)):
                    last = pe.matmul(to[:, P + 16 * x:P + 16 * x + 16], b[:, m], wif[:, m, t].rearrange("p d g -> p (d g)"),
                                     start=m != 1, stop=m != 0)
                last.then_inc(wa_mm, 1)

            block_transposes(0)
            for j in range(4):
                def step(i):
                    if 4 * j + i + 1 < 16:
                        block_transposes(4 * j + i + 1)
                    block_products(4 * j + i)

                project_unit("zm", (n0 + j) // RING, j, KD, act_hi, act_lo, LAT, act_ready, READY["mix1"], between=step)
            pe.wait_ge(wa_put, 48)
            for j in range(4, 12):
                project_unit("zm", (n0 + j) // RING, j % RING, KD, act_hi, act_lo, LAT, act_ready, READY["mix1"])
                for t in (2 * j - 8, 2 * j - 7):
                    pe.wait_ge(gx_in[t % RING], GX_IN0 + 32 * (t // RING + 1))
                    for x in range(2):
                        for b, c0, c1 in ((1, 0, 512), (3, 512, 768)):
                            last = pe.matmul(bank(b)[0:40, 0:c1 - c0], wG[:, x, t], gx[:, t % RING, x, c0:c1],
                                             start=t == 0 and x == 0, stop=t == 15 and x == 1)
                    last.then_inc(gx_mm, 1)
            each_ring(pe, n0 + 12, 4, lambda r, s: project_unit("zm", r, s, KD, act_hi, act_lo, LAT, act_ready, READY["mix1"]))
            pe.wait_ge(gm_done, 1)
            pe.wait_ge(ge_done, 2)
            pe.wait_ge(evac, segs["mout0"][0])
            for d in range(2):
                for c in range(6):
                    at = (6 * d + c) * 8
                    pe.transpose(bank(0)[:, at:at + 8], mr_u[:, d, c * P:c * P + P], ident[0:8, 0:8])
                for c in range(4):
                    at = 96 + (4 * d + c) * 8
                    last = pe.transpose(bank(0)[:, at:at + 8], mr_m[:, d, c * P:c * P + P], ident[0:8, 0:8])
            last.then_inc(gc_mm, 1)

            def query(h):
                f = 12 * h
                if h:
                    pe.wait_ge(s6_put, S6_PUT0 + 6 * h)
                pe.wait_ge(xch_in, XCH_IN0 + 16 * (h + 1))
                for t in range(4):
                    if f >= 2:
                        pe.wait_ge(qv_put, QV_PUT0 + f - 1)
                    pe.matmul(bank(2 + f % 2), wA[:, 4 * h + t], xch[:, t, 0:LAT], start=True, stop=True).then_inc(qv_mm, 1)
                    f += 1

            def value(h):
                f = 12 * h + 4
                for t in range(4):
                    g = 4 * h + t
                    pe.wait_ge(xmr_in[g % 2], XMR_IN0 + 16 * (g // 2 + 1))
                    pe.wait_ge(bdv_done, g + 1)
                    for c0, c1 in ((0, 4), (4, 6)):
                        pe.wait_ge(qv_put, QV_PUT0 + f - 1)
                        for c in range(c0, c1):
                            last = pe.matmul(bank(2 + f % 2)[:, (c - c0) * P:(c - c0) * P + P], xmr[:, g % 2, c * P:c * P + P], bdv[:, t],
                                             start=True, stop=True)
                        last.then_inc(qv_mm, 1)
                        f += 1

            def stabiliser_rows(h):
                if h == 0:
                    pe.wait_ge(gc_put, 2)
                for d in range(2):
                    r = 4 * d + h
                    if h:
                        pe.wait_ge(pn_done, PN_DONE0 + 6 * h)
                    pe.matmul(bank(d), ident[0:8, r:r + 1].broadcast_to([8, P]), negM[:, d], start=True, stop=True).then_inc(mrows_mm, 1)

            def scores_of(h, chunks):
                pe.wait_ge(qv_put, QV_PUT0 + 12 * h + 12)
                for i in chunks:
                    if i >= 4:
                        pe.wait_ge(s6_put, S6_PUT0 + 6 * h + i - 3)
                    elif h:
                        pe.wait_ge(s6_put, S6_PUT0 + 6 * h)
                    for t in range(4):
                        c = KEYS[i]
                        last = pe.matmul(bank(SCORE_BANKS[i]), xch[:, t, c * P:c * P + P], qp[:, t], start=t == 0, stop=t == 3)
                    last.then_inc(s6_mm, 1)

            query(0)
            value(0)
            stabiliser_rows(0)
            scores_of(0, range(6))
            for h in range(ML_HEADS):
                pe.wait_ge(den_rdy, DEN_RDY0 + h + 1)
                for d in range(2):
                    for c in range(4):
                        last = pe.matmul(bank(0)[:, 4 * d + c:4 * d + c + 1], mtmp[:, 1 + d, c * P:c * P + P], ones[:, 0:1], start=True, stop=True)
                last.then_inc(den_mm, 1)
                pe.wait_ge(rd_rdy, RD_RDY0 + h + 1)
                if h == 2:
                    project("mout0", act1_hi, act1_lo, LAT, act_ready, READY["ml0"])
                    pe.wait_ge(evac, segs["mout1"][0])
                pe.matmul(bank(0), ones[:], rdiag[:, 0:LAT], start=True, stop=True)
                pe.matmul(bank(1), ones[:], mtmp[:, 0], start=True, stop=True).then_inc(rfb_mm, 1)
                if h + 1 < ML_HEADS:
                    query(h + 1)
                pe.wait_ge(qv_put, QV_PUT0 + 12 * h + 12)
                if h:
                    pe.wait_ge(fin_done, FIN_DONE0 + 4 * h)
                for i, c in enumerate(KEYS):
                    pe.wait_ge(pn_done, PN_DONE0 + 6 * h + i + 1)
                    for t in range(4):
                        last = pe.matmul(bank(OUT_BANKS[t]), vt[:, c, t * P:t * P + P], Wf[:, c], start=i == 0, stop=i == 5)
                        if i == 5:
                            last.then_inc(h_mm, 1)
                if h + 1 < ML_HEADS:
                    stabiliser_rows(h + 1)
                    value(h + 1)
                pe.wait_ge(hs_rdy, HS_RDY0 + h + 1)
                pe.matmul(bank(7), ones[:], mtmp[:, 1], start=True, stop=True).then_inc(mean_mm, 1)
                if h + 1 < ML_HEADS:
                    scores_of(h + 1, (0, 1))
                rstd_sums(mtmp[:, 1], LAT, 3)
                if h + 1 < ML_HEADS:
                    scores_of(h + 1, (2,))
                rstd_spread(LAT, 3)
                if h + 1 < ML_HEADS:
                    scores_of(h + 1, (3, 4, 5))
            project("mout1", act1_hi, act1_lo, LAT, act_ready, READY["ml1"], together=3)
            norm_products("ffn1", LAT)
            ffn(1, LAT)
            pe.wait_ge(evac, segs["end"][0])
            rstd_products(nacc, LAT, 3)
            for half in range(2):
                for t in range(4):
                    i = 4 * half + t
                    pe.wait_ge(fin_ready, 4 * half + 4)
                    if i >= 2:
                        pe.wait_ge(out_put, i - 1)
                    for q in range(4):
                        last = pe.transpose(bank(2 + i % 2)[:, q * P:q * P + P], fin[:, 4 * half + q, t * P:t * P + P], ident[:])
                    last.then_inc(out_tr, 1)

        @block.scalar
        def _(act):
            chain = Chain(act, act_own)
            act.wait_ge(tab_put, 1)
            act.activation(cs[:, :, 0], par("c", 0, KD), ACT.Silu).then_inc(c_silu, 1)
            act.activation(cs[:, :, 1], par("c_ctx", 0, KD), ACT.Silu).then_inc(c_silu, 1)

            rstds = [0]

            def root(n, features, where, i=0):
                act.wait_ge(sum_mm, rstds[0] + 1)
                act.activation(rcol[:, i, 0:n // P], slot(where)[:, 0:n // P], ACT.Sqrt, scale=1.0 / features,
                               bias=eps_col[:]).then_inc(std_done, 1)
                rstds[0] += 1

            def squares(name, n):
                g = NORMS.index(name)
                for k in range(KD):
                    if g:
                        act.wait_ge(evac, segs[NORM_AFTER[name]][0] + k + 1)
                    if k >= 3:
                        act.wait_ge(nsum_step, (KD - 1) * g + k - 2)
                    dst = nacc[:, 0:n] if k == 0 else nsq[:, k % 2, 0:n]
                    act.activation(dst, xT[:, k, 0:n], ACT.Square).then_inc(sq_done, 1)

            def norm(name, n, layer, which, permute=False):
                g = NORMS.index(name)
                if name != "mix0":
                    squares(name, n)
                if name != "mix0":
                    root(n, D, 3)
                for k in range(KD):
                    act.wait_ge(nt_done, g * KD + k + 1)
                    if k >= 2:
                        act.wait_ge(act_ready, READY[name] + k - 1)
                    parts = [(0, LAT, 0)] + [(LAT, n, 1)] * (n > LAT)
                    for c0, c1, col in parts:
                        src, dst = nt[:, k % 2, c0:c1], nh[:, k % 2, c0:c1]
                        if permute and col == 0:
                            src = src.rearrange("p (r c) -> p r c", c=GRID_W)
                            dst = dst.rearrange("p (c r) -> p r c", r=GRID_H)
                        chain(act.activation(dst, src, ACT.Identity, scale=mscale[:, layer, which, k, col:col + 1],
                                             bias=modv[:, mod(layer, 3 * which, k), col:col + 1]), nh_done)
                    act.activation(act_hi[:, k, 0:n], nh[:, k % 2, 0:n], ACT.Copy).then_inc(nhi_done, 1)

            act.wait_ge(x_put, 12)
            squares("mix0", T)
            root(T, D, 3)
            for u in range(4):
                act.wait_ge(mod_mm, u + 1)
                act.activation(mrow[:, 512 * u:512 * u + 512], bank(MOD_BANKS[u])[0:2], ACT.Copy).then_inc(mrow_put, 1)
            act.wait_ge(mod_put, 1)
            norm("mix0", T, 0, 0)

            win = a["a_w_in"][0].rearrange("(k p) m -> p k m", p=P)
            act.wait_ge(act_ready, READY["mix0"] + KD)
            act.dma_start(rd_raw[:, :, 0:64], win[:, :, COL_R:COL_R + 64]).then_inc(rd_in, 16)
            act.dma_start(rd_raw[:, :, 64:128], win[:, :, COL_DT - 32:COL_DT + 32]).then_inc(rd_in, 16)

            def to_stage(r, s, func, tile0):
                act.wait_ge(mm_done, r * RING + (s + 1))
                if not (isinstance(r, int) and r == 0):
                    act.wait_ge(st_out[s], r * 16)
                act.activation(stage[:, s], slot(s), func).then_inc(evac, 1)
                act.wait_ge(evac, r * RING + (s + 1))
                act.dma_start(proj0[bass.ds(r * RING + (s + tile0), 1)].rearrange("a p t -> p (a t)"), stage[:, s]).then_inc(st_out[s], 16)

            each_ring(act, segs["qkv"][0], 16, lambda r, s: to_stage(r, s, ACT.Copy, 0))
            each_ring(act, segs["g"][0], 16, lambda r, s: to_stage(r, s, ACT.Silu, 0))

            def conv_unit(r, s):
                j = r * RING + (s - 32)
                act.wait_ge(mm_done, r * RING + (s + 1))
                if s >= 2:
                    act.wait_ge(conv_step, (j - 1) * 5)
                else:
                    act.wait_ge(silu_done, j)
                act.activation(cpre[:, s % 2], slot(s), ACT.Copy).then_inc(evac, 1)
                act.wait_ge(st_out[s], r * 16)
                act.wait_ge(conv_step, (j + 1) * 5)
                act.activation(stage[:, s], cpost[:, s % 2], ACT.Silu).then_inc(silu_done, 1)
                act.wait_ge(silu_done, j + 1)
                act.dma_start(proj0[bass.ds(r * RING + s, 1)].rearrange("a p t -> p (a t)"), stage[:, s]).then_inc(st_out[s], 16)

            each_ring(act, segs["xbc"][0], 12, conv_unit)

            def load_gate_weights(h):
                for d in range(2):
                    act.dma_start(wg[16 * d:16 * d + 16, d, :], a["a_gla_w_gate"][0, d, :, h * P:h * P + P]).then_inc(wg_in, 16)

            act.wait_ge(wg_zero, 2)
            load_gate_weights(0)
            act.wait_ge(rd_mm, 1)
            act.activation(rT[:], slot(0)[0:32], ACT.Copy).then_inc(rd_put, 1)
            act.activation(dtT[:], slot(0)[96:128], ACT.Copy).then_inc(rd_put, 1)
            for s in range(RING):
                act.wait_ge(st_out[s], 16 * 11)
            act.wait_ge(m_put, MOD_UNITS - RING)
            act.wait_ge(conv_step, 60)

            def load_head(h):
                for t, tile in enumerate((Q0 + h, K0 + h, V0 + 2 * h, V0 + 2 * h + 1)):
                    act.dma_start(hq[:, t], proj0[tile]).then_inc(hq_in, 16)

            load_head(0)
            def gate_sizes(h):
                for d in range(2):
                    act.wait_ge(gate_mm, 2 * h + d + 1)
                    chain(act.activation(Gn[:, d], slot(d), ACT.Abs, bias=par("gla_b", 4 * d + h)), abs_done)

            def gate_logs(h):
                for d in range(2):
                    chain(act.activation(Gn[:, d], Gn[:, d], ACT.Exp, scale=-1.0))
                for d in range(2):
                    chain(act.activation(Gn[:, d], Gn[:, d], ACT.Ln, bias=one_col[:]), ln_done)

            def value_copies(h):
                for i in range(3):
                    act.wait_ge(tr_done, 6 * h + i + 1)
                    act.activation(vtok[:, 2 * i:2 * i + 2, :].rearrange("p c v -> p (c v)"), bank(i % 2), ACT.Copy).then_inc(tr_put, 1)

            gate_sizes(0)
            gate_logs(0)
            value_copies(0)
            for h in range(GLA_HEADS):
                for d in range(2):
                    act.wait_ge(g_ready, 2 * h + d + 1)
                    chain(act.activation(ga[:, d], Gn[:, d], ACT.Exp, scale=1.0 / GLA_TAU), e0_done)
                for d in range(2):
                    act.wait_ge(qd_done, 2 * h + d + 1)
                    act.wait_ge(x_ready, 2 * h + d + 1)
                    near, far = (1 - d) * SUB, d * SUB
                    chain(act.activation(ga[:, d], gm[:, d], ACT.Exp, scale=1.0 / GLA_TAU), e1_done)
                    x, G = (y[:, d].rearrange("p (c t) -> p c t", t=P) for y in (gm, Gn))
                    chain(act.activation(x[:, :, near:near + SUB], x[:, :, near:near + SUB], ACT.Exp, scale=-1.0 / GLA_TAU))
                    chain(act.activation(x[:, :, far:far + SUB], G[:, :, far:far + SUB], ACT.Exp, scale=-1.0 / GLA_TAU), e3_done)
                for d in range(2):
                    act.wait_ge(y_ready, 2 * h + d + 1)
                    chain(act.activation(ga[:, d], ga[:, d], ACT.Exp, scale=1.0 / GLA_TAU), e4_done)
                for i in range(3):
                    act.wait_ge(tr_done, 6 * h + i + 4)
                    n = min(4, 10 - 4 * i)
                    act.activation(kdT[:, 4 * i:4 * i + n, :].rearrange("p e t -> p (e t)"), bank((3 + i) % 2, n * P),
                                   ACT.Copy).then_inc(tr_put, 1)
                for t in range(2):
                    act.dma_start(ga[:, t], proj0[G0 + 2 * h + t]).then_inc(g_in, 16)
                if h + 1 < GLA_HEADS:
                    load_head(h + 1)
                    load_gate_weights(h + 1)
                for i, c in enumerate(CHUNKS[0]):
                    act.wait_ge(o_mm, 6 * h + i + 1)
                    act.activation(oT[:, :, c * P:c * P + P], bank(6 + i % 2, 2 * P).rearrange("p (v t) -> p v t", v=2),
                                   ACT.Copy).then_inc(o_put, 1)
                act.wait_ge(o_put, 6 * h + 6)
                for t in range(2):
                    act.activation(gm[:, t], oT[:, t], ACT.Square).then_inc(gsq_done, 1)
                if h + 1 < GLA_HEADS:
                    gate_sizes(h + 1)
                root(T, 2 * P, 2)
                if h + 1 < GLA_HEADS:
                    gate_logs(h + 1)
                    value_copies(h + 1)
                for t in range(2):
                    act.wait_ge(gfull, 2 * h + t + 1)
                    act.activation(act_hi[:, 2 * h + t], oT[:, t], ACT.Copy).then_inc(nhi_done, 1)
            act.wait_ge(act_ready, READY["gla"] + KD)
            act.wait_ge(o_mm, 24)
            act.dma_start(rowc[:, 0:1], a["a_ssd_dt_bias"][0].rearrange("d (h o) -> (d h) o", o=1)).then_inc(row_in, 16)
            act.dma_start(rowc[:, 1:2], a["a_ssd_A_log"][0].rearrange("d (h o) -> (d h) o", o=1)).then_inc(row_in, 16)
            for f in range(2):
                src = a["a_ssd_D"][0]
                act.dma_start(dcol[64 * f:64 * f + 64, :], bass.AP(tensor=src.tensor, offset=src.offset + f, ap=[[0, 64], [2, PAIRS]]),
                              allow_slow_non_contiguous=True).then_inc(row_in, 16)
            act.wait_ge(row_in, 64)
            chain(act.activation(r_ab[:], dtT[:], ACT.Abs, bias=rowc[:, 0:1]))
            chain(act.activation(r_e[:], r_ab[:], ACT.Exp, scale=-1.0), r_ez)
            chain(act.activation(rowc[:, 2:3], rowc[:, 1:2], ACT.Exp), r_ez)

            def load_group(g):
                for k, tile in enumerate((B0 + g, C0 + g)):
                    act.dma_start(bct[:, k], proj0[tile]).then_inc(bc_in, 16)

            def load_pair(p):
                act.dma_start(xt[:, p % 2], proj0[X0 + p]).then_inc(xt_in, 16)
                act.dma_start(sz[:, p % 2], proj0[Z0 + p]).then_inc(xt_in, 16)

            load_group(0)
            act.wait_ge(r_dt, 1)
            chain(act.activation(r_ln[:], r_ab[:], ACT.Ln), r_lnd)
            for d in range(2):
                act.wait_ge(r_nbd, d + 1)
                end = T - 1 if d == 0 else LAT
                chain(act.activation(r_al[:, d], r_nb[:, d, LAT:T], ACT.Exp, bias=Grow[:, d, end:end + 1]), r_ald)
            act.wait_ge(ct_mm, 1)
            chain(act.activation(nb[:].rearrange("p d c r -> p (d c r)"), bank(6, 384), ACT.Copy), ct_put)
            chain(act.activation(al[:].rearrange("p d c r -> p (d c r)"), bank(7, 128), ACT.Copy), ct_put)
            load_pair(0)

            def group_copies(g):
                if g:
                    act.wait_ge(m_done, 8 * g)
                    act.wait_ge(s_mm, 4 * g)
                for i in range(6):
                    act.wait_ge(cb_mm, 6 * g + i + 1)
                    src = bank(6 + i % 2, 512 if i < 5 else 256)
                    dst = cb[:, i * LAT:i * LAT + LAT] if i < 5 else Btok[:].rearrange("p c n -> p (c n)")
                    act.activation(dst, src, ACT.Copy).then_inc(cb_put, 1)

            def x_copies(p):
                act.wait_ge(xt_tr, p + 1)
                act.activation(xtok[:, p % 2].rearrange("p c f -> p (c f)"), slot(3), ACT.Copy).then_inc(xt_put, 1)

            def decays(h):
                D = Dm[:, h % 2]
                if h >= 2:
                    act.wait_ge(m_done, h - 1)
                for d in range(2):
                    act.wait_ge(e_done, 2 * h + d + 1)
                    row, r = slot(d), 16 * d + h
                    todo = []
                    for c in range(6):
                        lo, hi, off = (0, 4, DL + c * LAT) if c < 4 else (4, 6, DC + (c - 4) * CTX)
                        if d == 0 and c + 1 < hi:
                            todo.append((off + (c + 1 - lo) * P, c + 1, hi, c))
                        elif d == 1 and c > lo:
                            todo.append((off, lo, c, c))
                    for off, i0, i1, c in todo:
                        act.activation(D[:, off:off + (i1 - i0) * P], row[:, i0 * P:i1 * P], ACT.Exp, bias=nb[:, d, c, r:r + 1])
                    if h >= 2 and d == 0:
                        act.wait_ge(y_mm, h - 1)
                    act.activation(Cb[h % 2][:, d], row[:, 0:LAT], ACT.Exp).then_inc(rows_read, 1)
                act.wait_ge(mask_done, 3 * h + 3)
                for k, (off, n, step) in enumerate(((DL, 4, LAT + P), (DC, 2, CTX + P), (DB, 6, P))):
                    blocks = diagonals(D, off, n, step)
                    act.activation(blocks, blocks, ACT.Exp).then_inc(exp_done, 1)

            def square(p):
                act.wait_ge(y_done, p + 1)
                dst = snacc[p // 4][:] if p % 4 == 0 else ssq[:, p % 2]
                if p >= 3:
                    act.wait_ge(ysum, (p - 2) - (p - 2) // 4)
                act.activation(dst, yT[:, p], ACT.Square).then_inc(ysq_done, 1)

            act.wait_ge(mm_done, segs["out1"][0])
            group_copies(0)
            x_copies(0)
            for h in range(SSD_HEADS):
                decays(h)
                if h % 2 == 0 and h:
                    x_copies(h // 2)
                if h + 1 == 8:
                    act.wait_ge(cbeta_done, 8)
                    load_group(1)
                if h % 2 and h + 1 < SSD_HEADS:
                    if h >= 2:
                        act.wait_ge(y_done, h // 2)
                        act.wait_ge(xt_tr, h // 2)
                    load_pair(h // 2 + 1)
                if h + 1 == 8:
                    group_copies(1)
            act.wait_ge(m_done, SSD_HEADS)
            for p in range(PAIRS):
                square(p)
            for g in range(2):
                root(T, 4 * P, 2 + g, g)
            for g in range(2):
                for t in range(4 * g, 4 * g + 4):
                    act.wait_ge(yn_done, t + 1)
                    act.activation(act_hi[:, t], yT[:, t], ACT.Copy).then_inc(nhi_done, 1)
            def hidden(layer, n):
                for g in range(3):
                    n0, count = segs[f"up{layer}{g}"][:2]

                    def body(r, s):
                        if s % 2:
                            return
                        t, u = r * 2 + (s // 2 - n0 // 2), r * RING + s
                        act.wait_ge(mm_done, u + 1)
                        act.wait_ge(evac, u - 2)
                        act.activation(fsg[:, s // 2, 0:n], slot(s)[:, 0:n], ACT.Silu).then_inc(fsg_done, 1)
                        act.wait_ge(evac, u + 2)
                        dst = hid_hi[:, bass.ds(t, 1), 0:n].rearrange("p a t -> p (a t)")
                        act.activation(dst, fhp[:, s // 2, 0:n], ACT.Copy).then_inc(fhh_done, 1)

                    each_ring(act, n0, count, body)

            norm("ffn0", T, 0, 1)
            act.wait_ge(act_ready, READY["ffn0"] + KD)
            hidden(0, T)
            for m, w in enumerate(("b_wq", "b_wk", "b_wv")):
                act.dma_start(w4[:, m], a[w][0].rearrange("n d e -> (n d) e").rearrange("(t p) e -> p t e", p=P)).then_inc(wb_in, 16)
            norm("mix1", T, 1, 0, permute=True)
            for d in range(2):
                for m in range(3):
                    act.dma_start(wif[:, m, :, d, :], a["b_w_if"][0, d, 16 * P * m:16 * P * (m + 1), :].rearrange("(t p) g -> p t g", p=P)).then_inc(wif_in, 16)
            for d in range(2):
                for k in range(2):
                    act.dma_start(bif[4 * d:4 * d + 4, k:k + 1], a["b_b_if"][0, d, 4 * k:4 * k + 4].unsqueeze(1)).then_inc(wb_in, 16)

            def block_copies(t):
                act.wait_ge(bdt_mm, t + 1)
                if t >= 2:
                    act.wait_ge(wa_mm, t - 1)
                act.activation(bdT[:, t % 2].rearrange("p m e -> p (m e)"), bank(5 + 2 * (t % 2), 384), ACT.Copy).then_inc(bdt_put, 1)

            def xm_unit(first):
                def body(r, s):
                    j = r * RING + (s - segs["xm"][0])
                    act.wait_ge(mm_done, r * RING + (s + 1))
                    if not first:
                        act.wait_ge(xm_out[s], XM_OUT0 + (r - segs["xm"][0] // RING) * 16)
                        act.wait_ge(conv_step, (j - 3 + 12) * 5)
                    act.activation(xms[:, s], slot(s), ACT.Copy).then_inc(evac, 1)
                    act.wait_ge(evac, r * RING + (s + 1))
                    act.dma_start(xm_d[bass.ds(j, 1)].rearrange("a p t -> p (a t)"), xms[:, s]).then_inc(xm_out[s], 16)
                    act.wait_ge(conv_step, (j + 1 + 12) * 5)
                    act.activation(xcr[:, s], xcr[:, s], ACT.Silu).then_inc(mxc_done, 1)
                    act.wait_ge(mxc_done, j + 1)
                    act.dma_start(xc_d[bass.ds(j, 1)].rearrange("a p t -> p (a t)"), xcr[:, s]).then_inc(xc_out[s], 16)
                return body

            n0 = segs["xm"][0]
            each_ring(act, n0, RING, xm_unit(True))
            each_ring(act, n0 + RING, 16 - RING, xm_unit(False))

            def load_gates(t):
                if t >= RING:
                    act.wait_ge(gx_mm, t - RING + 1)
                act.dma_start(gx[:, t % RING, 0], xc_d[t]).then_inc(gx_in[t % RING], 16)
                act.dma_start(gx[:, t % RING, 1], xm_d[t]).then_inc(gx_in[t % RING], 16)

            def z_unit(j):
                r, s = segs["zm"][0] // RING + j // RING, j % RING
                act.wait_ge(mm_done, r * RING + s + 1)
                if j >= RING:
                    act.wait_ge(z_out[s], Z_OUT0 + 16 * (j // RING))
                act.activation(zst[:, s], slot(s)[:, 0:LAT], ACT.Silu).then_inc(evac, 1)
                act.wait_ge(evac, r * RING + s + 1)
                act.dma_start(z_d[j], zst[:, s]).then_inc(z_out[s], 16)

            for s in range(RING):
                act.wait_ge(xm_out[s], XM_OUT0 + 64)
                act.wait_ge(xc_out[s], XC_OUT0 + 64)
            for t in range(RING):
                load_gates(t)
            for j in range(12):
                for t in range(4 * j, 4 * j + 4) if j < 4 else ():
                    block_copies(t)
                z_unit(j)
                for t in (2 * j - 4, 2 * j - 3) if j >= 4 else ():
                    if t < 16:
                        load_gates(t)
            act.wait_ge(gx_mm, 16)
            for k, dst in ((0, mr_i), (1, mr_f)):
                for b, c0, c1 in ((1, 0, 512), (3, 512, 768)):
                    act.activation(dst[:, c0:c1], bank(b)[32 * k:32 * k + 8, 0:c1 - c0], ACT.Copy).then_inc(gr_put, 1)
            act.wait_ge(gr_put, 4)
            chain(act.activation(mr_ab[:], mr_f[:], ACT.Abs, bias=bif[:, 1:2]), gab_done)
            chain(act.activation(mr_ab[:], mr_ab[:], ACT.Exp, scale=-1.0))
            chain(act.activation(mr_ab[:], mr_ab[:], ACT.Ln, bias=one_col[0:8]), gln_done)
            for j in range(12, 16):
                z_unit(j)
            def load_xc(h):
                act.dma_start(xch[:], xc_d[4 * h:4 * h + 4].rearrange("t p n -> p t n")).then_inc(xch_in, 16)

            def load_xm(g):
                act.dma_start(xmr[:, g % 2], xm_d[g]).then_inc(xmr_in[g % 2], 16)

            act.wait_ge(gm_done, 1)
            load_xc(0)
            for d in range(2):
                chain(act.activation(mr_m[:, d], mr_m[:, d], ACT.Exp, scale=-1.0), ge_done)
            for s in range(RING):
                act.wait_ge(z_out[s], Z_OUT0 + 64)
            act.wait_ge(gc_mm, 1)
            load_xm(0)
            load_xm(1)
            chain(act.activation(ucol[:].rearrange("p d c r -> p (d c r)"), bank(0)[:, 0:96], ACT.Copy), gc_put)
            chain(act.activation(ecol[:].rearrange("p d c r -> p (d c r)"), bank(0)[:, 96:160], ACT.Copy), gc_put)

            def query_copies(h):
                f = 12 * h
                for t in range(4):
                    act.wait_ge(qv_mm, QV_MM0 + f + 1)
                    act.activation(qp[:, t], bank(2 + f % 2), ACT.Copy, scale=ML_DH ** -0.5).then_inc(qv_put, 1)
                    f += 1

            def head_value_copies(h):
                f = 12 * h + 4
                for t in range(4):
                    g = 4 * h + t
                    for c0, c1 in ((0, 4), (4, 6)):
                        act.wait_ge(qv_mm, QV_MM0 + f + 1)
                        act.activation(vt[:, c0:c1, t * P:t * P + P], bank(2 + f % 2, (c1 - c0) * P).rearrange("p (c e) -> p c e", e=P),
                                       ACT.Copy).then_inc(qv_put, 1)
                        f += 1
                    if g + 2 < 16:
                        load_xm(g + 2)

            def weights(h):
                for d in range(2):
                    act.wait_ge(de_done, DE_DONE0 + 2 * h + d + 1)
                    r, W = 4 * d + h, (Wf, Wb)[d]
                    for c in range(6):
                        i0, i1 = (0, 4) if c >= 4 else (c + 1, 4) if d == 0 else (0, c)
                        if i0 < i1:
                            act.activation(W[:, c, i0 * P:i1 * P], bank(d)[:, i0 * P:i1 * P], ACT.Exp, bias=ucol[:, d, c, r:r + 1])
                for d in range(2):
                    act.wait_ge(mk_done, 2 * h + d + 1)
                    blocks = diagonals((Wf, Wb)[d][:].rearrange("p c t -> p (c t)"), 0, 4, LAT + P)
                    act.activation(blocks, blocks, ACT.Exp).then_inc(we_done, 1)

            query_copies(0)
            head_value_copies(0)
            weights(0)

            def load_output(h, t):
                g = 4 * h + t
                act.dma_start(zs[:, t % 2], z_d[g]).then_inc(z_in[t % 2], 16)

            for h in range(ML_HEADS):
                for t in range(4):
                    act.dma_start(xs(t), halves(xc_d[4 * h + t][:, 0:LAT])).then_inc(xs_in[t], 16)
                for t in range(2):
                    load_output(h, t)
                if h + 1 < ML_HEADS:
                    act.wait_ge(s6_mm, S6_MM0 + 6 * h + 6)
                    load_xc(h + 1)
                    query_copies(h + 1)
                for t in range(4):
                    act.wait_ge(h_mm, H_MM0 + 4 * h + t + 1)
                    act.activation(hh[:, t], bank(OUT_BANKS[t]), ACT.Copy).then_inc(h_put, 1)
                if h + 1 < ML_HEADS:
                    weights(h + 1)
                    head_value_copies(h + 1)
                for t in range(4):
                    act.wait_ge(hc_done, HC_DONE0 + 4 * h + t + 1)
                    if t == 3:
                        act.wait_ge(hsum, HSUM0 + 3 * h + 1)
                    dst = mtmp[:, (1, 0, 2, 0)[t]]
                    act.activation(dst, hh[:, t], ACT.Square).then_inc(hsq_done, 1)
                root(LAT, 4 * P, 3)
                for t in range(4):
                    act.wait_ge(fin_done, FIN_DONE0 + 4 * h + t + 1)
                    if h == 2 and t == 0:
                        act.wait_ge(mm_done, segs["mout1"][0])
                    act.activation(act1_hi[:, 4 * (h % 2) + t], hh[:, t], ACT.Copy).then_inc(nhi_done, 1)
                    if t < 2:
                        load_output(h, t + 2)
            norm("ffn1", LAT, 1, 1)
            act.wait_ge(act_ready, READY["ffn1"] + KD)
            hidden(1, LAT)
            squares("final", LAT)
            root(LAT, D, 3)
            for i in range(8):
                t, half = i % 4, i // 4
                act.wait_ge(out_tr, i + 1)
                act.activation(obuf[:, t, 512 * half:512 * half + 512], bank(2 + i % 2), ACT.Copy).then_inc(out_put, 1)
                if half:
                    act.wait_ge(out_put, i + 1)
                    act.dma_start(out[0, t * P:t * P + P, :], obuf[:, t]).then_inc(out_st[t % 2], 16)
            act.wait_ge(out_st[0], 32)
            act.wait_ge(out_st[1], 32)
        @block.vector
        def _(dve):
            chain = Chain(dve, dve_own)
            dve.wait_ge(tab_tr, 3)
            for t in range(3):
                dve.tensor_copy(ptab[:, t, 0:TABLE_LEN[t]], bank(0)[:, t * P:t * P + TABLE_LEN[t]]).then_inc(dve_own, 1)
            dve.wait_ge(dve_own, 3)
            chain.n[dve_own] = 3
            dve.drain().then_inc(tab_put, 1)
            for i in range(12):
                tt, half = i // 2, i % 2
                dve.wait_ge(x_tr, i + 1)
                dve.tensor_copy(xT[:, 4 * half:4 * half + 4, tt * P:tt * P + P],
                                bank(1 + i % 2).rearrange("p (q t) -> p q t", q=4)).then_inc(x_put, 1)
            def scales(layer, which):
                m = mod(layer, 3 * which + 1, 0)
                w = par("norm_ffn" if which else "norm_mix", layer * KD, KD)
                chain(dve.scalar_tensor_tensor(mscale[:, layer, which], modv[:, m:m + KD, :], 1.0,
                                               w.unsqueeze(2).broadcast_to([P, KD, 2]), ALU.add, ALU.mult))

            def mod_products(r, s):
                step0 = (r * RING + (s - RING)) * (2 * KD)
                if not (isinstance(r, int) and r == 1 and s < 2):
                    dve.wait_ge(mm_done, r * RING + (s - 1))
                dve.wait_ge(m_in[s], r * 16)
                for k in range(KD):
                    for v in range(2):
                        acc, c = m_acc[:, s % 2, v], cs[:, k, v:v + 1]
                        if k == 0:
                            ins = dve.tensor_scalar(acc, m_ring[:, s, k], c, None, ALU.mult)
                        else:
                            if k == 1 and v == 0:
                                dve.wait_ge(m_step, step0 + 2)
                            elif not (k == 1 and v == 1):
                                dve.wait_ge(m_step, step0 + 2 * k + v - 1)
                            ins = dve.scalar_tensor_tensor(acc, m_ring[:, s, k], c, acc, ALU.mult, ALU.add)
                        ins.then_inc(m_step, 1)

            def mod_unit(r, s):
                dve.wait_ge(mm_done, r * RING + (s + 1))
                m = r * (2 * RING) + (2 * s + 8)
                src = PS[:, mod_col(s):mod_col(s) + 4].rearrange("p (m x) -> p m x", x=2)
                dve.wait_ge(evac, r * RING + (s + 1))
                dve.tensor_tensor(modv[:, bass.ds(m, 2), :], src, ptab[:, 0, bass.ds(m, 2)].unsqueeze(2).broadcast_to([P, 2, 2]),
                                  ALU.add).then_inc(m_put, 1)

            rstds = [0]

            def rstd_diagonal(n, i=0, rdiag=rdiag):
                q = n // P
                rstds[0] += 1
                dve.wait_ge(std_done, rstds[0])
                chain(dve.reciprocal(rcol[:, i, 0:q], rcol[:, i, 0:q]))
                dve.tensor_tensor(rdiag[:, 0:n].rearrange("p (q t) -> p q t", t=P), ident[:].unsqueeze(1).broadcast_to([P, q, P]),
                                  rcol[:, i, 0:q].unsqueeze(2).broadcast_to([P, q, P]), ALU.mult).then_inc(diag_done, 1)

            def add_norm_square(g, k, n):
                dve.wait_ge(sq_done, g * KD + k + 1)
                chain(dve.tensor_tensor(nacc[:, 0:n], nacc[:, 0:n], nsq[:, k % 2, 0:n], ALU.add), nsum_step)

            def norm_sums(name, n):
                g = NORMS.index(name)
                for k in range(KD - 1 if g else 1, KD):
                    add_norm_square(g, k, n)
                dve.drain().then_inc(sum_done, 1)
                rstd_diagonal(n)
                dve.wait_ge(rstd_done, rstds[0])

            def norm(name, n):
                g = NORMS.index(name)
                if g:
                    norm_sums(name, n)

                def scaled(k):
                    if k >= 2:
                        dve.wait_ge(nh_done, nh_count(name, k - 1))
                    dve.tensor_tensor(nt[:, k % 2, 0:n], xT[:, k, 0:n], slot(3)[:, 0:n], ALU.mult).then_inc(nt_done, 1)

                scaled(0)
                for k in range(KD):
                    if k + 1 < KD:
                        scaled(k + 1)
                    dve.wait_ge(nhi_done, READY[name] + k + 1)
                    dve.tensor_tensor(act_lo[:, k, 0:n], nh[:, k % 2, 0:n], act_hi[:, k, 0:n].bitcast(F32),
                                      ALU.subtract).then_inc(act_ready, 1)
                dve.wait_ge(act_ready, READY[name] + KD)

            norm_sums("mix0", T)
            dve.wait_ge(mrow_tr, 1)
            chain(dve.tensor_tensor(modv[:, 0:16, :], bank(2)[:, 0:32].rearrange("p (m x) -> p m x", x=2),
                                    ptab[:, 0, 0:16].unsqueeze(2).broadcast_to([P, 16, 2]), ALU.add))
            scales(0, 0)
            dve.drain().then_inc(mod_put, 1)

            norm("mix0", T)

            def next_products(r, s):
                mod_products(*((r, s + 1) if s + 1 < RING else (r + 1, 0)))

            def mod_both(r, s):
                next_products(r, s)
                mod_unit(r, s)

            mod_products(1, 0)
            each_ring(dve, RING, 28, mod_both)

            def convolve(src, dst, w, bias, step0):
                def step(ins, k):
                    ins.then_inc(conv_step, 1)
                    dve.wait_ge(conv_step, step0 + k)

                step(dve.tensor_scalar(dst, src, w[1], bias, ALU.mult, ALU.add), 1)
                k = 2
                for c0, c1 in ((0, LAT), (LAT, T)):
                    for tap, d0, s0 in ((0, 1, 0), (2, 0, 1)):
                        m = c1 - c0 - 1
                        ins = dve.scalar_tensor_tensor(dst[:, c0 + d0:c0 + d0 + m], src[:, c0 + s0:c0 + s0 + m], w[tap],
                                                       dst[:, c0 + d0:c0 + d0 + m], ALU.mult, ALU.add)
                        step(ins, k)
                        k += 1

            def conv_unit(r, s):
                j = r * RING + (s - 32)
                dve.wait_ge(evac, r * RING + (s + 1))
                if s < 2:
                    dve.wait_ge(silu_done, j)
                else:
                    dve.wait_ge(silu_done, j - 1)
                convolve(cpre[:, s % 2], cpost[:, s % 2], [par_at("conv_w", j + 12 * t) for t in range(3)],
                         par_at("conv_b", j), j * 5)

            def conv_mod_unit(r, s):
                next_products(r, s)
                conv_unit(r, s)
                mod_unit(r, s)

            each_ring(dve, segs["xbc"][0], 8, conv_mod_unit)
            r = MOD_UNITS // RING - 1
            for s in range(RING):
                if s + 1 < RING:
                    next_products(r, s)
                conv_unit(r, s)
                mod_unit(r, s)
            for layer, which in ((0, 1), (1, 0), (1, 1)):
                dve.wait_ge(m_put, 40)
                scales(layer, which)
            dve.wait_ge(silu_done, 12)
            for s in range(RING):
                dve.wait_ge(st_out[s], 16 * 11)
            dve.memset(wg[:], 0.0).then_inc(wg_zero, 1)
            dve.memset(K2[:], 0.0).then_inc(wg_zero, 1)
            dve.wait_ge(wg_zero, 2)
            def gate_minima(h):
                for d in range(2):
                    dve.wait_ge(gate_mm, 2 * h + d + 1)
                    dve.wait_ge(abs_done, 2 * h + d + 1)
                    chain(dve.tensor_scalar(gmn[:, d], slot(d), par("gla_b", 4 * d + h), 0.0, ALU.add, ALU.min), min_done)

            def gate_sums(h):
                for d in range(2):
                    dve.wait_ge(ln_done, 2 * h + d + 1)
                    chain(dve.tensor_tensor(gmn[:, d], gmn[:, d], Gn[:, d], ALU.subtract))
                    for c in range(6):
                        src, dst = gmn[:, d, c * P:c * P + P], Gn[:, d, c * P:c * P + P]
                        if d:
                            src, dst = src[:, ::-1], dst[:, ::-1]
                        dve.tensor_tensor_scan(dst, ones[:], src, 0.0, ALU.mult, ALU.add).then_inc(dve_own, 1)
                    chain.n[dve_own] += 6
                    dve.wait_ge(dve_own, chain.n[dve_own])
                    dve.drain().then_inc(g_ready, 1)

            def low_parts(h):
                for t in range(2):
                    dve.wait_ge(nhi_done, KD + 2 * h + t + 1)
                    dve.tensor_tensor(act_lo[:, 2 * h + t], oT[:, t], act_hi[:, 2 * h + t].bitcast(F32), ALU.subtract).then_inc(act_ready, 1)

            gate_minima(0)
            gate_sums(0)
            for h in range(GLA_HEADS):
                q, k = hq[:, 0], hq[:, 1]
                if h:
                    dve.wait_ge(o_put, 6 * h)
                for d in range(2):
                    G = Gn[:, d].rearrange("p (c t) -> p c t", t=P)
                    mid = SUB - 1 + d
                    chain(dve.tensor_tensor(gm[:, d].rearrange("p (c t) -> p c t", t=P), G[:, :, mid:mid + 1].broadcast_to([P, 6, P]), G,
                                            ALU.subtract), x_ready)
                if h:
                    low_parts(h - 1)
                dve.wait_ge(hq_in, 64 * (h + 1))
                for d in range(2):
                    dve.wait_ge(e0_done, 2 * h + d + 1)
                    chain(dve.scalar_tensor_tensor(qd[:, d], q, GLA_DK ** -0.5, ga[:, d], ALU.mult, ALU.mult))
                    end = 0 if d else P - 1
                    chain(dve.tensor_copy(etot[:, d, :].unsqueeze(2), ga[:, d].rearrange("p (c t) -> p c t", t=P)[:, :, end:end + 1]), qd_done)
                for d in range(2):
                    near, far = (1 - d) * SUB, d * SUB
                    e, x, G, k3, q3 = (y.rearrange("p (c t) -> p c t", t=P) for y in (ga[:, d], gm[:, d], Gn[:, d], k, q))
                    dve.wait_ge(e1_done, 2 * h + d + 1)
                    chain(dve.tensor_tensor(K2[:, d, :, 1 - d].rearrange("p c a t -> p c (a t)"), k3, e, ALU.mult))
                    last = P - 1 if d == 0 else 0
                    chain(dve.tensor_tensor(e, G[:, :, last:last + 1].broadcast_to([P, 6, P]), G, ALU.subtract), y_ready)
                    dve.wait_ge(e3_done, 2 * h + d + 1)
                    chain(dve.scalar_tensor_tensor(qs[:, d], q3[:, :, near:near + SUB], GLA_DK ** -0.5, x[:, :, near:near + SUB],
                                                   ALU.mult, ALU.mult))
                    chain(dve.tensor_tensor(K2[:, d, :, d, d, :], k3[:, :, far:far + SUB], x[:, :, far:far + SUB], ALU.mult), k2_done)
                for d in range(2):
                    dve.wait_ge(e4_done, 2 * h + d + 1)
                    chain(dve.tensor_tensor(ga[:, d], ga[:, d], k, ALU.mult), kd_done)

                def masked(i):
                    dve.wait_ge(sc_mm, 6 * h + i + 1)
                    both = gm[:, 1, i % 2 * 256:i % 2 * 256 + 256].rearrange("p (d t) -> p d t", d=2)
                    chain(dve.tensor_tensor(both, bank(2 + i % 2, 2 * P).rearrange("p (d t) -> p d t", d=2), tri[:], ALU.mult))
                    chain(dve.tensor_tensor(gm[:, 0, i * P:i * P + P], both[:, 0], both[:, 1], ALU.add), a_done)

                masked(0)
                for e, (d, c) in enumerate(KD_ORDER):
                    i = e // 2
                    dve.wait_ge(u_mm, 10 * h + e + 1)
                    U = bank(4 + d, 2 * P)
                    if i == 0:
                        chain(dve.tensor_copy(gS[:, d, 0], U), s_done)
                    else:
                        chain(dve.scalar_tensor_tensor(gS[:, d, i], gS[:, d, i - 1], etot[:, d, c:c + 1], U, ALU.mult, ALU.add), s_done)
                    if d:
                        masked(i + 1)
                dve.wait_ge(gsq_done, 2 * h + 2)
                chain(dve.tensor_tensor(gm[:, 0], gm[:, 0], gm[:, 1], ALU.add))
                dve.drain().then_inc(sum_done, 1)
                if h + 1 < GLA_HEADS:
                    gate_minima(h + 1)
                rstd_diagonal(T)
                if h + 1 < GLA_HEADS:
                    gate_sums(h + 1)
                dve.wait_ge(rstd_done, rstds[0])
                dve.wait_ge(g_in, 32 * (h + 1))
                for t in range(2):
                    chain(dve.scalar_tensor_tensor(oT[:, t], oT[:, t], par("gla_norm", t), slot(2), ALU.mult, ALU.mult))
                    chain(dve.tensor_tensor(oT[:, t], oT[:, t], ga[:, t], ALU.mult), gfull)
                if h + 1 == GLA_HEADS:
                    low_parts(h)

            def residual(name, layer, which, n, permuted=False, then=None):
                def body(r, s):
                    m = r * RING + (s - segs[name][0])
                    dve.wait_ge(mm_done, r * RING + (s + 1))
                    parts = [(0, LAT, 0)] + [(LAT, T, 1)] * (n > LAT)
                    for c0, c1, v in parts:
                        if isinstance(m, int):
                            x, g = xT[:, m, c0:c1], modv[:, m + mod(layer, which, 0), v:v + 1]
                        else:
                            x = xT[:, bass.ds(m, 1), c0:c1].rearrange("p a t -> p (a t)")
                            g = modv[:, bass.ds(m + mod(layer, which, 0), 1), v:v + 1].rearrange("p a t -> p (a t)")
                        y = slot(s)[:, c0:c1]
                        if permuted:
                            x = x.rearrange("p (r c) -> p r c", c=GRID_W)
                            y = y.rearrange("p (c r) -> p r c", r=GRID_H)
                        ins = dve.scalar_tensor_tensor(x, y, g, x, ALU.mult, ALU.add)
                    ins.then_inc(evac, 1)

                if then is None:
                    each_ring(dve, segs[name][0], 8, body)
                    return
                for k in range(KD):
                    body(segs[name][0] // RING + k // RING, k % RING)
                    if k >= 2:
                        add_norm_square(NORMS.index(then), k - 1, n)

            dve.wait_ge(row_in, 64)
            dve.wait_ge(o_put, 24)
            dve.wait_ge(nhi_done, READY["gla"] + KD)
            chain(dve.tensor_scalar(r_zz[:], dtT[:], rowc[:, 0:1], 0.0, ALU.add, ALU.max))
            dve.wait_ge(r_ez, 1)
            chain(dve.tensor_scalar(r_p[:], r_e[:], 2.0, None, ALU.add))
            chain(dve.reciprocal(r_p[:], r_p[:]))
            chain(dve.tensor_tensor(r_e[:], r_e[:], r_p[:], ALU.mult))
            chain(dve.tensor_tensor(r_s2[:], r_e[:], r_e[:], ALU.mult))
            chain(dve.tensor_scalar(r_p[:], r_s2[:], 1.0 / 17.0, None, ALU.mult))
            for k in range(15, 1, -2):
                chain(dve.scalar_tensor_tensor(r_p[:], r_p[:], 1.0 / k, r_s2[:], ALU.add, ALU.mult))
            chain(dve.scalar_tensor_tensor(r_p[:], r_p[:], 1.0, r_e[:], ALU.add, ALU.mult))
            chain(dve.scalar_tensor_tensor(r_zz[:], r_p[:], 2.0, r_zz[:], ALU.mult, ALU.add))
            chain(dve.tensor_scalar(r_ab[:], r_zz[:], 1e-19, None, ALU.max), r_dt)
            dve.wait_ge(r_ez, 2)
            chain(dve.tensor_scalar(r_zz[:], r_zz[:], rowc[:, 2:3], -1.0, ALU.mult, ALU.mult))
            for d in range(2):
                for c0, c1 in ((0, LAT), (LAT, T)):
                    src, dst = r_zz[:, c0:c1], Grow[:, d, c0:c1]
                    if d:
                        src, dst = src[:, ::-1], dst[:, ::-1]
                    one = ones[0:32, 0:1].broadcast_to([32, c1 - c0])
                    chain(dve.tensor_tensor_scan(dst, one, src, 0.0, ALU.mult, ALU.add))
            dve.wait_ge(r_lnd, 1)
            for d in range(2):
                chain(dve.tensor_tensor(r_nb[:, d], r_ln[:], Grow[:, d], ALU.subtract), r_nbd)
            residual("out0", 0, 2, T)

            def exponents(h):
                D = Dm[:, h % 2]
                if h >= 2:
                    dve.wait_ge(m_done, h - 1)
                for d in range(2):
                    dve.wait_ge(rows_mm, 2 * h + d + 1)
                    r = 16 * d + h
                    parts = ((DL, 0, 4, LAT + P), (DC, 4, 6, CTX + P)) if d == 0 else ((DB, 0, 6, P),)
                    for off, c0, c1, step in parts:
                        ins = dve.tensor_tensor(diagonals(D, off, c1 - c0, step), slot(d)[:, c0 * P:c1 * P].rearrange("p (c t) -> p c t", t=P),
                                                nb[:, d, c0:c1, r:r + 1].broadcast_to([P, c1 - c0, P]), ALU.add)
                    ins.then_inc(e_done, 1)

            def head_weights(h):
                D = Dm[:, h % 2]
                dve.wait_ge(exp_done, 3 * h + 3)
                dve.wait_ge(cb_put, 6 * (h // 8) + 6)
                f, b = diagonals(D, DL, 4, LAT + P), diagonals(D, DB, 4, P)
                chain(dve.tensor_tensor(f, f, b, ALU.add))
                f, b = diagonals(D, DC, 2, CTX + P), diagonals(D, DB + 4 * P, 2, P)
                chain(dve.tensor_tensor(f, f, b, ALU.add))
                if h >= 2:
                    dve.wait_ge(y_mm, h - 1)
                dve.tensor_tensor(Mm[:, h % 2], D[:, 0:DB], cb[:], ALU.mult).then_inc(m_done, 1)
                c = Cb[h % 2][:]
                dve.tensor_tensor(c, c, bct[:, 1, 0:LAT].unsqueeze(1).broadcast_to([P, 2, LAT]), ALU.mult).then_inc(cbeta_done, 1)

            def weighted_x(p):
                dve.wait_ge(xt_put, p + 1)
                if p >= 2:
                    dve.wait_ge(s_mm, p - 1)
                for d in range(2):
                    w = al[:, d, :, 16 * d + 2 * p:16 * d + 2 * p + 2].unsqueeze(3).broadcast_to([P, 2, 2, 64])
                    dve.tensor_tensor(xal[:, p % 2, :, d].rearrange("p c (h f) -> p c h f", h=2),
                                      xtok[:, p % 2, 4:6].rearrange("p c (h f) -> p c h f", h=2), w, ALU.mult).then_inc(xal_done, 1)

            def state_copy(p):
                dve.wait_ge(s_mm, p + 1)
                if p >= 2:
                    dve.wait_ge(y_mm, 2 * p - 2)
                dve.tensor_copy(ssS[:, p % 2].rearrange("p d f -> p (d f)"), bank(6, 2 * P)).then_inc(ss_put, 1)

            def output(p):
                dve.wait_ge(y_mm, 2 * p + 2)
                chain(dve.scalar_tensor_tensor(yT[:, p], xt[:, p % 2], dcol[:, p:p + 1], slot(2), ALU.mult, ALU.add), y_put)
                chain(dve.tensor_tensor(yT[:, p], yT[:, p], sz[:, p % 2], ALU.mult), y_done)

            def add_square(p):
                dve.wait_ge(ysq_done, p + 1)
                if p % 4:
                    chain(dve.tensor_tensor(snacc[p // 4][:], snacc[p // 4][:], ssq[:, p % 2], ALU.add), ysum)

            dve.wait_ge(ct_put, 2)
            exponents(0)
            exponents(1)
            for h in range(SSD_HEADS):
                head_weights(h)
                if h % 2 == 0:
                    weighted_x(h // 2)
                    if h:
                        output(h // 2 - 1)
                if h + 2 < SSD_HEADS:
                    exponents(h + 2)
                if h % 2 == 0:
                    state_copy(h // 2)
            output(7)
            for p in range(PAIRS):
                add_square(p)
            for g in range(2):
                dve.drain().then_inc(sum_done, 1)
            for g in range(2):
                rstd_diagonal(T, g, (rdiag, rdiag2)[g])
            for g in range(2):
                dve.wait_ge(rstd_done, rstds[0] - 1 + g)
                for t in range(4 * g, 4 * g + 5):
                    if t < 4 * g + 4:
                        chain(dve.scalar_tensor_tensor(yT[:, t], yT[:, t], par("ssd_norm", t), slot(2 + g), ALU.mult, ALU.mult), yn_done)
                    if t > 4 * g:
                        dve.wait_ge(nhi_done, READY["ssd"] + t)
                        dve.tensor_tensor(act_lo[:, t - 1], yT[:, t - 1], act_hi[:, t - 1].bitcast(F32),
                                          ALU.subtract).then_inc(act_ready, 1)
            residual("out1", 0, 2, T, then="ffn0")
            def ffn(layer, n):
                for g in range(3):
                    n0, count = segs[f"up{layer}{g}"][:2]
                    before = FF_BEFORE[f"{layer}{g}"]

                    def body(r, s):
                        if s % 2 == 0:
                            return
                        i, t = s // 2, r * 2 + (s // 2 - n0 // 2)
                        dve.wait_ge(fsg_done, t + (before + 1))
                        dve.wait_ge(mm_done, r * RING + (s + 1))
                        dve.tensor_tensor(fhp[:, i, 0:n], fsg[:, i, 0:n], slot(s)[:, 0:n], ALU.mult).then_inc(evac, 2)
                        dve.wait_ge(fhh_done, t + (before + 1))
                        hi, lo = (x[:, bass.ds(t, 1), 0:n].rearrange("p a t -> p (a t)") for x in (hid_hi, hid_lo))
                        dve.tensor_tensor(lo, fhp[:, i, 0:n], hi.bitcast(F32), ALU.subtract).then_inc(hid_ready, 1)
                        dve.wait_ge(hid_ready, t + (before + 1))

                    each_ring(dve, n0, count, body)
                    residual(f"down{layer}{g}", layer, 5, n, then=None if g < 2 else ("mix1", "final")[layer])

            norm("ffn0", T)
            ffn(0, T)
            norm("mix1", T)

            dve.wait_ge(m4_done, 1)
            dve.wait_ge(wb_in, 7 * 16)
            dve.wait_ge(wg0, 1)

            def blocks(t):
                if t >= 2:
                    dve.wait_ge(bdt_mm, t - 1)
                dve.tensor_tensor(bd[:, t % 2].rearrange("p m (b e) -> p m b e", e=4),
                                  mask4[:].rearrange("p (b e) -> p b e", e=4).unsqueeze(1).broadcast_to([P, 3, 32, 4]),
                                  w4[:, :, t].unsqueeze(2).broadcast_to([P, 3, 32, 4]), ALU.mult).then_inc(bd_done, 1)

            blocks(0)
            blocks(1)
            def xm_unit(first):
                def body(r, s):
                    j = r * RING + (s - segs["xm"][0])
                    dve.wait_ge(evac, r * RING + (s + 1))
                    if not first:
                        dve.wait_ge(xc_out[s], XC_OUT0 + (r - segs["xm"][0] // RING) * 16)
                    convolve(xms[:, s], xcr[:, s], [par_at("m_conv_w", j + 16 * t) for t in range(3)], par_at("m_conv_b", j), j * 5 + 60)
                return body

            n0 = segs["xm"][0]
            each_ring(dve, n0, RING, xm_unit(True))
            each_ring(dve, n0 + RING, 16 - RING, xm_unit(False))
            for t in range(16):
                if t + 2 < 16:
                    blocks(t + 2)
                dve.wait_ge(wa_mm, t + 1)
                src = bank(1 + 2 * (t % 2))
                dve.tensor_copy(wA[:, t], src[:, 0:P]).then_inc(wa_put, 1)
                gates = src[:, P:P + 32].rearrange("p (x d g) -> p x d g", x=2, d=2)
                for k in range(2):
                    dve.tensor_copy(wG[:, :, t, 32 * k:32 * k + 8].rearrange("p x (d g) -> p x d g", d=2),
                                    gates[:, :, :, 4 * k:4 * k + 4]).then_inc(wa_put, 1)

            dve.wait_ge(gr_put, 4)
            chain(dve.tensor_scalar(mr_i[:], mr_i[:], bif[:, 0:1], None, ALU.add))
            dve.wait_ge(gab_done, 1)
            chain(dve.tensor_scalar(mr_f[:], mr_f[:], bif[:, 1:2], 0.0, ALU.add, ALU.min))
            dve.wait_ge(gln_done, 1)
            chain(dve.tensor_tensor(mr_f[:], mr_f[:], mr_ab[:], ALU.subtract))

            def both_parts(dst, src, start, op):
                for d in range(2):
                    for c0, c1, init in ((LAT, T, start), (0, LAT, dst[:, d, T - 1:T] if d == 0 else dst[:, d, LAT:LAT + 1])):
                        x, y = src(d)[:, c0:c1], dst[:, d, c0:c1]
                        if d:
                            x, y = x[:, ::-1], y[:, ::-1]
                        chain(dve.tensor_tensor_scan(y, ones[0:8, 0:1].broadcast_to([8, c1 - c0]), x, init, ALU.mult, op))

            both_parts(mr_b, lambda d: mr_f[:], 0.0, ALU.add)
            for d in range(2):
                chain(dve.tensor_tensor(mr_u[:, d], mr_i[:], mr_b[:, d], ALU.subtract))
            both_parts(mr_M, lambda d: mr_u[:, d], -1e30, ALU.max)
            for d in range(2):
                chain(dve.tensor_scalar(negM[:, d], mr_M[:, d, 0:LAT], -1.0, None, ALU.mult))
                chain(dve.tensor_tensor(mr_m[:, d], mr_b[:, d, 0:LAT], mr_M[:, d, 0:LAT], ALU.add))
            dve.drain().then_inc(gm_done, 1)

            def value_blocks(h):
                if h:
                    dve.wait_ge(qv_mm, QV_MM0 + 12 * h)
                for t in range(4):
                    dve.tensor_tensor(bdv[:, t].rearrange("p (b e) -> p b e", e=4), mask4[:].rearrange("p (b e) -> p b e", e=4),
                                      w4[:, 2, 4 * h + t].unsqueeze(1).broadcast_to([P, 32, 4]), ALU.mult).then_inc(bdv_done, 1)

            def weight_exponents(h):
                for d in range(2):
                    dve.wait_ge(mrows_mm, MROWS_MM0 + 2 * h + d + 1)
                    r = 4 * d + h
                    blocks = diagonals((Wf, Wb)[d][:].rearrange("p c t -> p (c t)"), 0, 4, LAT + P)
                    dve.tensor_tensor(blocks, bank(d).rearrange("p (c t) -> p c t", t=P), ucol[:, d, 0:4, r:r + 1].broadcast_to([P, 4, P]),
                                      ALU.add).then_inc(de_done, 1)

            def weighted_scores(h, i):
                c = KEYS[i]
                if i == 0:
                    dve.wait_ge(we_done, WE_DONE0 + 2 * h + 2)
                dve.wait_ge(s6_mm, S6_MM0 + 6 * h + i + 1)
                for d, W in enumerate((Wf, Wb)):
                    i0, i1 = (0, LAT) if c >= 4 else (c * P, LAT) if d == 0 else (0, c * P + P)
                    ins = dve.tensor_tensor(W[:, c, i0:i1], W[:, c, i0:i1], bank(SCORE_BANKS[i])[:, i0:i1], ALU.mult)
                    chain(ins, dve_own if d == 0 else s6_put)

            def key_sums(i):
                for d, W in enumerate((Wf, Wb)):
                    acc, c = mtmp[:, 1 + d], KEYS[i]
                    i0, i1 = (c * P, LAT) if d == 0 else (0, c * P + P)
                    if i == 2:
                        chain(dve.tensor_tensor(acc, W[:, 4], W[:, 5], ALU.add))
                    chain(dve.tensor_tensor(acc[:, i0:i1], acc[:, i0:i1], W[:, c, i0:i1], ALU.add))

            value_blocks(0)
            dve.wait_ge(gc_put, 2)
            dve.wait_ge(ge_done, 2)
            weight_exponents(0)
            for h in range(ML_HEADS):
                if h == 0:
                    weighted_scores(h, 0)
                    weighted_scores(h, 1)
                for i in range(2, 6):
                    weighted_scores(h, i)
                    key_sums(i)
                dve.drain().then_inc(den_rdy, 1)
                dve.wait_ge(den_mm, h + 1)
                den = bank(0)[:, 0:8].rearrange("p (d c) -> p d c", d=2)
                chain(dve.tensor_scalar(dcl[:], den, -1.0, None, ALU.mult))
                chain(dve.tensor_tensor(dcl[:], dcl[:], den, ALU.max))
                for d in range(2):
                    chain(dve.tensor_tensor(dcl[:, d], dcl[:, d], ecol[:, d, :, 4 * d + h], ALU.max))
                chain(dve.reciprocal(dcl[:], dcl[:]))
                for d in range(2):
                    dst = rdiag[:, 0:LAT] if d == 0 else mtmp[:, 0]
                    chain(dve.tensor_tensor(dst.rearrange("p (q t) -> p q t", t=P), ident[:].unsqueeze(1).broadcast_to([P, 4, P]),
                                            dcl[:, d].unsqueeze(2).broadcast_to([P, 4, P]), ALU.mult))
                dve.drain().then_inc(rd_rdy, 1)
                if h == 2:
                    residual("mout0", 1, 2, LAT, permuted=True)
                dve.wait_ge(rfb_mm, RFB_MM0 + h + 1)
                rf, rb = bank(0), bank(1)
                for c in KEYS:
                    i0, i1 = (0, LAT) if c >= 4 else (c * P, c * P + P)
                    dve.tensor_tensor(Wf[:, c, i0:LAT], Wf[:, c, i0:LAT], rf[:, i0:LAT], ALU.mult).then_inc(dve_own, 1)
                    dve.tensor_tensor(Wb[:, c, i0:i1], Wb[:, c, i0:i1], rb[:, i0:i1], ALU.mult).then_inc(dve_own, 1)
                    if i0:
                        dve.tensor_tensor(Wf[:, c, 0:i0], Wb[:, c, 0:i0], rb[:, 0:i0], ALU.mult).then_inc(dve_own, 1)
                    chain.n[dve_own] += 3 if i0 else 2
                    dve.wait_ge(dve_own, chain.n[dve_own])
                    chain(dve.tensor_tensor(Wf[:, c, i0:i1], Wf[:, c, i0:i1], Wb[:, c, i0:i1], ALU.add), pn_done)
                if h + 1 < ML_HEADS:
                    value_blocks(h + 1)
                    weight_exponents(h + 1)
                acc = mtmp[:, 1]
                dve.wait_ge(h_put, H_PUT0 + 4 * h + 2)
                chain(dve.tensor_tensor(acc, hh[:, 0], hh[:, 1], ALU.add))
                for t in (2, 3):
                    dve.wait_ge(h_put, H_PUT0 + 4 * h + t + 1)
                    chain(dve.tensor_tensor(acc, acc, hh[:, t], ALU.add))
                dve.drain().then_inc(hs_rdy, 1)
                dve.wait_ge(mean_mm, h + 1)
                for t in range(4):
                    chain(dve.scalar_tensor_tensor(hh[:, t], bank(7), -1.0 / ML_DH, hh[:, t], ALU.mult, ALU.add), hc_done)
                for t in range(1, 4):
                    dve.wait_ge(hsq_done, HSQ_DONE0 + 4 * h + t + 1)
                    chain(dve.tensor_tensor(acc, acc, mtmp[:, (1, 0, 2, 0)[t]], ALU.add), hsum)
                dve.drain().then_inc(sum_done, 1)
                if h + 1 < ML_HEADS:
                    weighted_scores(h + 1, 0)
                rstd_diagonal(LAT)
                if h + 1 < ML_HEADS:
                    weighted_scores(h + 1, 1)
                dve.wait_ge(rstd_done, rstds[0])
                def low_part(t):
                    k = 4 * (h % 2) + t
                    dve.wait_ge(nhi_done, READY["ml0"] + 4 * h + t + 1)
                    dve.tensor_tensor(act1_lo[:, k], hh[:, t], act1_hi[:, k].bitcast(F32), ALU.subtract).then_inc(act_ready, 1)

                for t in range(4):
                    g = 4 * h + t
                    chain(dve.scalar_tensor_tensor(hh[:, t], hh[:, t], par("mh_norm", g), bank(6), ALU.mult, ALU.mult))
                    dve.wait_ge(xs_in[t], XS_IN0 + 16 * (h + 1))
                    chain(dve.scalar_tensor_tensor(halves(hh[:, t]), xs(t), par("skip", g), halves(hh[:, t]), ALU.mult, ALU.add))
                    dve.wait_ge(z_in[t % 2], Z_IN0 + 16 * (2 * h + t // 2 + 1))
                    chain(dve.tensor_tensor(hh[:, t], hh[:, t], zs[:, t % 2], ALU.mult), fin_done)
                    if t:
                        low_part(t - 1)
                low_part(3)
                dve.wait_ge(act_ready, READY["ml0"] + 4 * h + 4)
            residual("mout1", 1, 2, LAT, permuted=True, then="ffn1")
            norm("ffn1", LAT)
            ffn(1, LAT)
            norm_sums("final", LAT)
            for k in range(KD):
                dve.scalar_tensor_tensor(fin[:, k], xT[:, k, 0:LAT], par("final_norm", k), slot(3)[:, 0:LAT], ALU.mult, ALU.mult).then_inc(fin_ready, 1)


_INS = ["x", "c", "ctx", "c_ctx", "w_mod", "b_mod", "norm_mix", "norm_ffn", "ffn_w1", "ffn_w3", "ffn_w2", "a_w_in",
        "a_gla_w_gate", "a_gla_b_gate", "a_gla_norm", "a_ssd_conv_w", "a_ssd_conv_b", "a_ssd_A_log", "a_ssd_dt_bias",
        "a_ssd_D", "a_ssd_norm", "a_w_out", "b_w_up", "b_conv_w", "b_conv_b", "b_wq", "b_wk", "b_wv", "b_w_if", "b_b_if",
        "b_mh_norm", "b_skip", "b_w_down", "final_norm"]


def kernel(**inputs):
    import numpy as _np
    import concourse.bacc as _bacc
    from concourse import mybir as _mybir
    from concourse.bass_utils import run_bass_kernel_spmd as _run

    nc = _bacc.Bacc("TRN2", target_bir_lowering=False, num_devices=1)
    arrays, args = {}, {}
    for name in _INS:
        x = _np.ascontiguousarray(inputs[name])
        arrays[f"in_{name}"] = x
        args[name] = nc.dram_tensor(f"in_{name}", x.shape, _mybir.dt.from_np(x.dtype), kind="ExternalInput").ap()
    out = nc.dram_tensor("out_y", (1, LAT, D), _mybir.dt.float32, kind="ExternalOutput").ap()
    trunk(nc, args, out)
    r = _run(nc, [arrays], core_ids=[0])
    return r.results[0]["out_y"]
```
